# Optimizing a Trainium2 kernel written in Bass

```python
import math
import jax, jax.numpy as jnp
from jax import lax
import numpy as np

D_MODEL = 1024
BATCH = 1
SEQ = 256
DEPTH = 1

N_FOX_HEADS = 8
FOX_HEAD_DIM = 64
FOX_WIDTH = N_FOX_HEADS * FOX_HEAD_DIM
N_DIFF_HEADS = 4
DIFF_QK_DIM = 64
DIFF_V_DIM = 2 * DIFF_QK_DIM
DIFF_QK_WIDTH = N_DIFF_HEADS * 2 * DIFF_QK_DIM
DIFF_WIDTH = N_DIFF_HEADS * DIFF_V_DIM
MIX_WIDTH = FOX_WIDTH + DIFF_WIDTH
IN_SIZES = (FOX_WIDTH, FOX_WIDTH, FOX_WIDTH, N_FOX_HEADS,
            DIFF_QK_WIDTH, DIFF_QK_WIDTH, DIFF_WIDTH)
IN_WIDTH = sum(IN_SIZES)
IN_SPLITS = tuple(int(v) for v in np.cumsum(IN_SIZES)[:-1])
ROPE_THETA = 500000.0
ROPE_DIM = DIFF_QK_DIM // 4
D_FF = 2816
FFN_RESIDUAL_WEIGHT = 0.5
Q_BLOCK = 128
RMS_EPS = 1e-6


def rms_norm(x, g):
    xf = x.astype(jnp.float32)
    y = xf * lax.rsqrt(jnp.mean(xf * xf, axis=-1, keepdims=True) + RMS_EPS)
    return (y * g.astype(jnp.float32)).astype(x.dtype)

def swiglu(x, w_gate, w_up, w_down):
    return (jax.nn.silu(x @ w_gate) * (x @ w_up)) @ w_down

def to_heads(t, n_heads):
    b, s, _ = t.shape
    return t.reshape(b, s, n_heads, -1).transpose(0, 2, 1, 3)

def from_heads(t):
    b, h, s, d = t.shape
    return t.transpose(0, 2, 1, 3).reshape(b, s, h * d)

def partial_rope(t, pos):
    half = ROPE_DIM // 2
    inv_freq = ROPE_THETA ** (-jnp.arange(0, ROPE_DIM, 2, dtype=jnp.float32) / ROPE_DIM)
    ang = pos.astype(jnp.float32)[:, None] * inv_freq[None, :]
    cos, sin = jnp.cos(ang), jnp.sin(ang)
    tf = t.astype(jnp.float32)
    x1, x2, rest = tf[..., :half], tf[..., half:ROPE_DIM], tf[..., ROPE_DIM:]
    out = jnp.concatenate([x1 * cos - x2 * sin, x2 * cos + x1 * sin, rest], axis=-1)
    return out.astype(t.dtype)

def causal_block_attention(q, k, v, log_decay_cum=None):
    seq = q.shape[2]
    scale = q.shape[-1] ** -0.5
    outs = []
    for i in range(seq // Q_BLOCK):
        q0, q1 = i * Q_BLOCK, (i + 1) * Q_BLOCK
        s = jnp.einsum('bhqd,bhkd->bhqk', q[:, :, q0:q1], k[:, :, :q1]).astype(jnp.float32) * scale
        if log_decay_cum is not None:
            s = s + log_decay_cum[:, :, q0:q1, None] - log_decay_cum[:, :, None, :q1]
        mask = jnp.arange(q1)[None, :] <= jnp.arange(q0, q1)[:, None]
        s = jnp.where(mask, s, jnp.finfo(jnp.float32).min)
        p = jax.nn.softmax(s, axis=-1).astype(v.dtype)
        outs.append(jnp.einsum('bhqk,bhkd->bhqd', p, v[:, :, :q1]))
    return jnp.concatenate(outs, axis=2)

def token_mixer(h, w_in, fox_forget_b, lam_q1, lam_k1, lam_q2, lam_k2, subln_g, w_out, layer):
    b, s, _ = h.shape
    pos = jnp.arange(s)
    proj = h @ w_in
    fq, fk, fv, fgate, dq, dk, dv = jnp.split(proj, IN_SPLITS, axis=-1)

    log_f = jax.nn.log_sigmoid(fgate.astype(jnp.float32) + fox_forget_b.astype(jnp.float32))
    c = jnp.cumsum(log_f, axis=1).transpose(0, 2, 1)
    fox_o = causal_block_attention(to_heads(fq, N_FOX_HEADS), to_heads(fk, N_FOX_HEADS),
                                   to_heads(fv, N_FOX_HEADS), c)
    fox_o = from_heads(fox_o)

    dq = dq.reshape(b, s, N_DIFF_HEADS, 2, DIFF_QK_DIM)
    dk = dk.reshape(b, s, N_DIFF_HEADS, 2, DIFF_QK_DIM)
    hd = lambda t: partial_rope(t.transpose(0, 2, 1, 3), pos)
    q1, q2 = hd(dq[..., 0, :]), hd(dq[..., 1, :])
    k1, k2 = hd(dk[..., 0, :]), hd(dk[..., 1, :])
    v = to_heads(dv, N_DIFF_HEADS)
    lam_init = 0.8 - 0.6 * math.exp(-0.3 * layer)
    lam = (jnp.exp(jnp.sum(lam_q1.astype(jnp.float32) * lam_k1.astype(jnp.float32)))
           - jnp.exp(jnp.sum(lam_q2.astype(jnp.float32) * lam_k2.astype(jnp.float32)))
           + lam_init)
    a1 = causal_block_attention(q1, k1, v)
    a2 = causal_block_attention(q2, k2, v)
    diff_o = a1 - lam.astype(a1.dtype) * a2
    diff_o = rms_norm(diff_o, subln_g) * (1.0 - lam_init)
    diff_o = from_heads(diff_o)

    return jnp.concatenate([fox_o, diff_o], axis=-1) @ w_out

def first_inputs(seed: int = 0) -> dict:
    key = jax.random.key(seed)
    ks = jax.random.split(key, 24)
    L = DEPTH
    nrm = lambda k, shape, scale: jax.random.normal(k, shape, jnp.float32) * scale
    gain = lambda k, n: 1.0 + 0.02 * jax.random.normal(k, (L, n), jnp.float32)
    return {
        "x": jax.random.normal(ks[0], (BATCH, SEQ, D_MODEL), jnp.float32),
        "ffn1_pre_g": gain(ks[1], D_MODEL),
        "ffn1_post_g": gain(ks[2], D_MODEL),
        "ffn1_w_gate": nrm(ks[3], (L, D_MODEL, D_FF), D_MODEL ** -0.5),
        "ffn1_w_up": nrm(ks[4], (L, D_MODEL, D_FF), D_MODEL ** -0.5),
        "ffn1_w_down": nrm(ks[5], (L, D_FF, D_MODEL), D_FF ** -0.5),
        "mix_pre_g": gain(ks[6], D_MODEL),
        "mix_post_g": gain(ks[7], D_MODEL),
        "w_in": nrm(ks[8], (L, D_MODEL, IN_WIDTH), D_MODEL ** -0.5),
        "fox_forget_b": nrm(ks[9], (L, N_FOX_HEADS), 0.02),
        "diff_lambda_q1": nrm(ks[10], (L, DIFF_QK_DIM), 0.1),
        "diff_lambda_k1": nrm(ks[11], (L, DIFF_QK_DIM), 0.1),
        "diff_lambda_q2": nrm(ks[12], (L, DIFF_QK_DIM), 0.1),
        "diff_lambda_k2": nrm(ks[13], (L, DIFF_QK_DIM), 0.1),
        "diff_subln_g": gain(ks[14], DIFF_V_DIM),
        "w_out": nrm(ks[15], (L, MIX_WIDTH, D_MODEL), MIX_WIDTH ** -0.5),
        "ffn2_pre_g": gain(ks[16], D_MODEL),
        "ffn2_post_g": gain(ks[17], D_MODEL),
        "ffn2_w_gate": nrm(ks[18], (L, D_MODEL, D_FF), D_MODEL ** -0.5),
        "ffn2_w_up": nrm(ks[19], (L, D_MODEL, D_FF), D_MODEL ** -0.5),
        "ffn2_w_down": nrm(ks[20], (L, D_FF, D_MODEL), D_FF ** -0.5),
    }

def first_block(x, ffn1_pre_g, ffn1_post_g, ffn1_w_gate, ffn1_w_up, ffn1_w_down,
              mix_pre_g, mix_post_g, w_in, fox_forget_b,
              diff_lambda_q1, diff_lambda_k1, diff_lambda_q2, diff_lambda_k2, diff_subln_g,
              w_out, ffn2_pre_g, ffn2_post_g, ffn2_w_gate, ffn2_w_up, ffn2_w_down):
    for l in range(DEPTH):
        f1 = swiglu(rms_norm(x, ffn1_pre_g[l]), ffn1_w_gate[l], ffn1_w_up[l], ffn1_w_down[l])
        x = x + FFN_RESIDUAL_WEIGHT * rms_norm(f1, ffn1_post_g[l])
        m = token_mixer(rms_norm(x, mix_pre_g[l]), w_in[l], fox_forget_b[l],
                        diff_lambda_q1[l], diff_lambda_k1[l], diff_lambda_q2[l], diff_lambda_k2[l],
                        diff_subln_g[l], w_out[l], l)
        x = x + rms_norm(m, mix_post_g[l])
        f2 = swiglu(rms_norm(x, ffn2_pre_g[l]), ffn2_w_gate[l], ffn2_w_up[l], ffn2_w_down[l])
        x = x + FFN_RESIDUAL_WEIGHT * rms_norm(f2, ffn2_post_g[l])
    return x


HG_HEADS = 8
HG_DK = 128
HG_DV = 128
HG_WIDTH = HG_HEADS * HG_DK
HG_CHUNK = 64
AT_HEADS = 8
AT_DH = 128
AT_WIDTH = AT_HEADS * AT_DH
MOBA_BLOCK = 256
MOBA_TOPK = 3
Q_CHUNK = 16
REL_BUCKETS = 32
REL_MAX_DIST = 128
D_FF_2 = -(-8 * D_MODEL // (3 * 256)) * 256
N_BRANCH = 2
NORM_EPS = 1e-6
IN_SIZES_2 = [HG_WIDTH, HG_WIDTH, HG_HEADS * HG_DV, HG_HEADS * HG_DV,
            AT_WIDTH, AT_WIDTH, AT_WIDTH, N_BRANCH * D_MODEL]
IN_COLS = sum(IN_SIZES_2)
IN_SPLITS_2 = [int(s) for s in np.cumsum(IN_SIZES_2)[:-1]]


def rmsnorm(x, g):
    xf = x.astype(jnp.float32)
    y = xf * lax.rsqrt(jnp.mean(xf * xf, axis=-1, keepdims=True) + NORM_EPS)
    return (y * g.astype(jnp.float32)).astype(x.dtype)

def t5_bucket(dist):
    n = jnp.maximum(dist, 0)
    max_exact = REL_BUCKETS // 2
    nf = jnp.maximum(n, 1).astype(jnp.float32)
    large = max_exact + (jnp.log(nf / max_exact) / math.log(REL_MAX_DIST / max_exact)
                         * (REL_BUCKETS - max_exact)).astype(jnp.int32)
    large = jnp.minimum(large, REL_BUCKETS - 1)
    return jnp.where(n < max_exact, n, large)

def hgrn2_mix(q, f_logit, i, g, lb, out_gain):
    B, S, _ = q.shape
    f32 = jnp.float32
    C = HG_CHUNK
    N = S // C
    z = f_logit.astype(f32)
    f = lb + (1.0 - lb) * jax.nn.sigmoid(z)
    log_f = jnp.log(f)
    k = (1.0 - lb) * jax.nn.sigmoid(-z)
    qs = q.astype(f32) * HG_DK ** -0.5

    def to_chunks(t, d):
        return t.reshape(B, N, C, HG_HEADS, d).transpose(1, 0, 3, 2, 4)

    qc = to_chunks(qs, HG_DK)
    kc = to_chunks(k, HG_DK)
    lfc = to_chunks(log_f, HG_DK)
    vc = to_chunks(i.astype(f32), HG_DV)
    causal = jnp.tril(jnp.ones((C, C), dtype=bool))

    def step(state, inp):
        q_, k_, v_, lf_ = inp
        b = jnp.cumsum(lf_, axis=2)
        o_inter = jnp.einsum('bhtk,bhkv->bhtv', q_ * jnp.exp(b), state)
        diff = b[:, :, :, None, :] - b[:, :, None, :, :]
        decay = jnp.exp(jnp.where(causal[:, :, None], diff, -jnp.inf))
        attn = jnp.einsum('bhtk,bhsk,bhtsk->bhts', q_, k_, decay)
        o = o_inter + jnp.einsum('bhts,bhsv->bhtv', attn, v_)
        b_last = b[:, :, -1:, :]
        k_dec = k_ * jnp.exp(b_last - b)
        new_state = (jnp.exp(b_last[:, :, 0, :])[..., None] * state
                     + jnp.einsum('bhsk,bhsv->bhkv', k_dec, v_))
        return new_state, o

    s0 = jnp.zeros((B, HG_HEADS, HG_DK, HG_DV), f32)
    _, o = lax.scan(step, s0, (qc, kc, vc, lfc))
    o = o.transpose(1, 0, 3, 2, 4).reshape(B, S, HG_HEADS, HG_DV)
    o = rmsnorm(o, out_gain) * jax.nn.silu(g.astype(f32).reshape(B, S, HG_HEADS, HG_DV))
    return o.reshape(B, S, HG_HEADS * HG_DV).astype(q.dtype)

def moba_attention(q, k, v, rel_table):
    B, H, S, Dh = q.shape
    f32 = jnp.float32
    BLK = MOBA_BLOCK
    NB = -(-S // BLK)
    pad = NB * BLK - S
    kp = jnp.pad(k, ((0, 0), (0, 0), (0, pad), (0, 0)))
    vp = jnp.pad(v, ((0, 0), (0, 0), (0, pad), (0, 0)))
    kb = kp.reshape(B, H, NB, BLK, Dh)
    vb = vp.reshape(B, H, NB, BLK, Dh)
    kmean = jnp.mean(kb.astype(f32), axis=3)
    topk = min(MOBA_TOPK, NB)
    scale = Dh ** -0.5
    table_h = rel_table.astype(f32).T
    b_idx = jnp.arange(B)[:, None, None, None]
    h_idx = jnp.arange(H)[None, :, None, None]
    h_idx5 = jnp.arange(H)[None, :, None, None, None]
    n_chunks = S // Q_CHUNK

    def one_chunk(c):
        t0 = c * Q_CHUNK
        qc = lax.dynamic_slice_in_dim(q, t0, Q_CHUNK, axis=2)
        tpos = t0 + jnp.arange(Q_CHUNK)
        cur = t0 // BLK
        gate = jnp.einsum('bhqd,bhnd->bhqn', qc.astype(f32), kmean)
        gate = jnp.where(jnp.arange(NB) < cur, gate, -jnp.inf)
        _, sel = lax.top_k(gate, topk)
        sel_valid = sel < cur
        ks = kb[b_idx, h_idx, sel]
        vs = vb[b_idx, h_idx, sel]
        lp = jnp.einsum('bhqd,bhqjsd->bhqjs', qc, ks).astype(f32) * scale
        kpos = sel[..., None] * BLK + jnp.arange(BLK)
        bias_p = table_h[h_idx5, t5_bucket(tpos[:, None, None] - kpos)]
        lp = jnp.where(sel_valid[..., None], lp + bias_p, -jnp.inf)
        ko = lax.dynamic_slice_in_dim(kp, cur * BLK, BLK, axis=2)
        vo = lax.dynamic_slice_in_dim(vp, cur * BLK, BLK, axis=2)
        lo = jnp.einsum('bhqd,bhsd->bhqs', qc, ko).astype(f32) * scale
        dist_o = tpos[:, None] - (cur * BLK + jnp.arange(BLK))[None, :]
        lo = jnp.where(dist_o >= 0, lo + table_h[:, t5_bucket(dist_o)], -jnp.inf)
        logits = jnp.concatenate([lo, lp.reshape(B, H, Q_CHUNK, topk * BLK)], axis=-1)
        p = jax.nn.softmax(logits, axis=-1)
        p_own = p[..., :BLK].astype(v.dtype)
        p_past = p[..., BLK:].reshape(B, H, Q_CHUNK, topk, BLK).astype(v.dtype)
        return (jnp.einsum('bhqs,bhsd->bhqd', p_own, vo)
                + jnp.einsum('bhqjs,bhqjsd->bhqd', p_past, vs))

    out = lax.map(one_chunk, jnp.arange(n_chunks))
    return out.transpose(1, 2, 0, 3, 4).reshape(B, H, S, Dh)

def second_inputs(seed: int = 0) -> dict:
    key = jax.random.key(seed)
    ks = jax.random.split(key, 16)
    f32 = jnp.float32
    nrm = lambda k, shape, s: jax.random.normal(k, shape, f32) * s
    return {
        "x": jax.random.normal(ks[0], (BATCH, SEQ, D_MODEL), f32),
        "attn_norm_g": 1.0 + nrm(ks[1], (DEPTH, D_MODEL), 0.02),
        "w_in": nrm(ks[2], (DEPTH, D_MODEL, IN_COLS), D_MODEL ** -0.5),
        "hg_lb_gamma": nrm(ks[3], (DEPTH + 1, HG_WIDTH), 0.5),
        "hg_out_norm_g": 1.0 + nrm(ks[4], (DEPTH, HG_DV), 0.02),
        "q_norm_g": 1.0 + nrm(ks[5], (DEPTH, AT_DH), 0.02),
        "k_norm_g": 1.0 + nrm(ks[6], (DEPTH, AT_DH), 0.02),
        "rel_bias_table": nrm(ks[7], (REL_BUCKETS, AT_HEADS), 0.2),
        "w_branch_hg": nrm(ks[8], (DEPTH, HG_HEADS * HG_DV, D_MODEL), (HG_HEADS * HG_DV) ** -0.5),
        "w_branch_attn": nrm(ks[9], (DEPTH, AT_WIDTH, D_MODEL), AT_WIDTH ** -0.5),
        "w_out": nrm(ks[10], (DEPTH, D_MODEL, D_MODEL), D_MODEL ** -0.5),
        "ffn_norm_g": 1.0 + nrm(ks[11], (DEPTH, D_MODEL), 0.02),
        "w_ffn_gate": nrm(ks[12], (DEPTH, D_MODEL, D_FF_2), D_MODEL ** -0.5),
        "w_ffn_up": nrm(ks[13], (DEPTH, D_MODEL, D_FF_2), D_MODEL ** -0.5),
        "w_ffn_down": nrm(ks[14], (DEPTH, D_FF_2, D_MODEL), D_FF_2 ** -0.5),
    }

def second_block(x, attn_norm_g, w_in, hg_lb_gamma, hg_out_norm_g, q_norm_g, k_norm_g,
              rel_bias_table, w_branch_hg, w_branch_attn, w_out, ffn_norm_g,
              w_ffn_gate, w_ffn_up, w_ffn_down):
    B, S, D = x.shape
    lb_all = jnp.cumsum(jax.nn.softmax(hg_lb_gamma.astype(jnp.float32), axis=0), axis=0)[:DEPTH]
    for l in range(DEPTH):
        h = rmsnorm(x, attn_norm_g[l])
        proj = h @ w_in[l]
        hq, hf, hi, hg, aq, ak, av, gl = jnp.split(proj, IN_SPLITS_2, axis=-1)
        y_hg = hgrn2_mix(hq, hf, hi, hg, lb_all[l], hg_out_norm_g[l]) @ w_branch_hg[l]
        qh = rmsnorm(aq.reshape(B, S, AT_HEADS, AT_DH), q_norm_g[l]).transpose(0, 2, 1, 3)
        kh = rmsnorm(ak.reshape(B, S, AT_HEADS, AT_DH), k_norm_g[l]).transpose(0, 2, 1, 3)
        vh = av.reshape(B, S, AT_HEADS, AT_DH).transpose(0, 2, 1, 3)
        att = moba_attention(qh, kh, vh, rel_bias_table)
        y_at = att.transpose(0, 2, 1, 3).reshape(B, S, AT_WIDTH) @ w_branch_attn[l]
        gates = jax.nn.sigmoid(gl.reshape(B, S, N_BRANCH, D))
        merged = gates[:, :, 0, :] * y_hg + gates[:, :, 1, :] * y_at
        x = x + merged @ w_out[l]
        h2 = rmsnorm(x, ffn_norm_g[l])
        x = x + (jax.nn.silu(h2 @ w_ffn_gate[l]) * (h2 @ w_ffn_up[l])) @ w_ffn_down[l]
    return x


def setup_inputs(seed=0):
    out = dict(first_inputs(seed))
    for name, value in second_inputs(seed + 1).items():
        if name != "x":
            out[name + "_2"] = value
    return out


def reference(
    x, ffn1_pre_g, ffn1_post_g, ffn1_w_gate, ffn1_w_up, ffn1_w_down, mix_pre_g, mix_post_g,
    w_in, fox_forget_b, diff_lambda_q1, diff_lambda_k1, diff_lambda_q2, diff_lambda_k2,
    diff_subln_g, w_out, ffn2_pre_g, ffn2_post_g, ffn2_w_gate, ffn2_w_up, ffn2_w_down,
    attn_norm_g_2, w_in_2, hg_lb_gamma_2, hg_out_norm_g_2, q_norm_g_2, k_norm_g_2,
    rel_bias_table_2, w_branch_hg_2, w_branch_attn_2, w_out_2, ffn_norm_g_2, w_ffn_gate_2,
    w_ffn_up_2, w_ffn_down_2,
):
    x = first_block(
        x, ffn1_pre_g, ffn1_post_g, ffn1_w_gate, ffn1_w_up, ffn1_w_down, mix_pre_g, mix_post_g,
        w_in, fox_forget_b, diff_lambda_q1, diff_lambda_k1, diff_lambda_q2, diff_lambda_k2,
        diff_subln_g, w_out, ffn2_pre_g, ffn2_post_g, ffn2_w_gate, ffn2_w_up, ffn2_w_down,
    )
    return second_block(
        x, attn_norm_g_2, w_in_2, hg_lb_gamma_2, hg_out_norm_g_2, q_norm_g_2, k_norm_g_2,
        rel_bias_table_2, w_branch_hg_2, w_branch_attn_2, w_out_2, ffn_norm_g_2, w_ffn_gate_2,
        w_ffn_up_2, w_ffn_down_2,
    )


_drawn_inputs = setup_inputs


def setup_inputs(seed=0):
    import zlib

    import numpy as np

    out = dict(_drawn_inputs(seed))
    spreads = {}
    factors = {'ffn1_post_g': 3.858,
     'mix_post_g': 3.547,
     'fox_forget_b': 8.0,
     'diff_lambda_q1': 8.0,
     'diff_subln_g': 4.626,
     'ffn2_pre_g': 5.476,
     'ffn2_post_g': 7.928,
     'attn_norm_g_2': 5.625,
     'hg_out_norm_g_2': 8.0,
     'q_norm_g_2': 8.0,
     'k_norm_g_2': 8.0,
     'rel_bias_table_2': 5.003,
     'ffn_norm_g_2': 5.363}
    for name, (base, spread) in spreads.items():
        noise = np.random.default_rng([zlib.crc32(name.encode()), seed]).standard_normal(out[name].shape)
        drawn = base * np.exp(spread * noise) if base else spread * noise
        out[name] = __import__('jax').numpy.asarray(drawn.astype(out[name].dtype))
    for name, factor in factors.items():
        out[name] = (out[name] * factor).astype(out[name].dtype)
    return out
```

```python
from contextlib import ExitStack

import numpy as np

import concourse.bass as bass
from concourse import mybir

F32 = mybir.dt.float32
F32R = mybir.dt.float32r
BF16 = mybir.dt.bfloat16
U8 = mybir.dt.uint8
ALU = mybir.AluOpType
ACT = mybir.ActivationFunctionType
AX = mybir.AxisListType.X

P = 128
S = 256
TT = S // P
D = 1024
KT = D // P
D_FF = 2816
FC = 256
NC = D_FF // FC
BLK = 512
RING = 3
PIECE = 2048
EPS = 1e-6
LAM_INIT = 0.2
ROPE_HALF = 8
ROPE_THETA = 500000.0
REL_BUCKETS, REL_MAX_DIST = 32, 128
MASKED = -1e30
HG_SCALE = float(128) ** -0.5
FOX_SCALE = 0.125
MOBA_SCALE = float(128) ** -0.5
FOX_HEADS = 8
FOX_GATE = 1536
TOEP = 384

FQ, FK, FV, DQ, DK, DV, MIX = 0, 512, 1024, 1536, 2048, 2560, 3072
HQ, HF, HI, HG, AQ, AK, AV, G0, G1 = (1024 * n for n in range(9))
PROJ = 9 * 1024

FFN_PIECES = 3 * NC
N_FFN1 = 0
N_WIN = N_FFN1 + FFN_PIECES
N_WOUT = N_WIN + 12
N_FFN2 = N_WOUT + 4
N_WIN2 = N_FFN2 + FFN_PIECES
N_WHG = N_WIN2 + 36
N_WAT = N_WHG + 4
N_WOUT2 = N_WAT + 4
N_FFN3 = N_WOUT2 + 4
N_END = N_FFN3 + FFN_PIECES

T_FFN1, T_WIN, T_WOUT, T_FFN2, T_WIN2, T_WHG, T_WAT, T_WOUT2, T_FFN3 = range(9)
TURN_AFTER = [0, N_WIN, N_WOUT, N_FFN2, N_WIN2, N_WHG, N_WAT, N_WOUT2, N_FFN3]

C_ID, C_TRI, C_AFTER, C_MASK, C_COS, C_SIN = 0, 128, 256, 512, 640, 656
C_END = 672
LEVELS = [1, 2, 4, 8, 16, 32, 64]
R_LAM, R_FB, R_END = 0, 256, 264
G_TURN, G_QG, G_KG, G_GAM, G_END = 0, 72, 73, 74, 90


def constants():
    c = np.zeros((P, C_END), np.float32)
    row, col = np.arange(P)[:, None], np.arange(P)[None, :]
    c[:, C_ID:C_ID + P] = row == col
    c[:, C_TRI:C_TRI + P] = row <= col
    c[:, C_AFTER:C_AFTER + P] = 1.0
    c[:, C_AFTER + P:C_AFTER + 2 * P] = row > col
    c[:, C_MASK:C_MASK + P] = np.where(col > row, MASKED, 0.0)
    inv = np.float32(ROPE_THETA) ** (-np.arange(0, 16, 2, dtype=np.float32) / np.float32(16))
    ang = np.arange(S, dtype=np.float32)[:, None] * inv[None, :].astype(np.float32)
    for t in range(TT):
        c[:, C_COS + 8 * t:C_COS + 8 * t + 8] = np.cos(ang[t * P:(t + 1) * P])
        c[:, C_SIN + 8 * t:C_SIN + 8 * t + 8] = np.sin(ang[t * P:(t + 1) * P])
    lv = np.zeros((P, len(LEVELS), P), np.float32)
    for n, m in enumerate(LEVELS):
        lv[:, n, :] = (row // (2 * m) == col // (2 * m)) & (row // m % 2 == 0) & (col // m % 2 == 1)
    dist = 255 - np.arange(S)
    exact = REL_BUCKETS // 2
    nf = np.maximum(dist, 1).astype(np.float32)
    large = exact + (np.log(nf / exact) / np.log(REL_MAX_DIST / exact) * (REL_BUCKETS - exact)).astype(np.int32)
    bucket = np.where(dist < exact, dist, np.minimum(large, REL_BUCKETS - 1))
    hot = (np.arange(REL_BUCKETS)[:, None] == bucket[None, :]).astype(np.float32)
    return c, lv, hot


def per(ap, m):
    n = ap.shape[1]
    return ap.rearrange("p (k o) -> p k o", o=1).to_broadcast([ap.shape[0], n, m])


def build(nc, x_d, wg_d, wu_d, wd_d, win_d, wout_d, win2_d, whg_d, wat_d, wout2_d,
          cols_d, rows_d, post_d, rel_d, const_d, level_d, hot_d, out_d, skew_d):
    with ExitStack() as ctx:
        def sb(name, shape, dt=F32):
            return ctx.enter_context(nc.sbuf_tensor(name, shape, dt))

        def sem(name):
            return ctx.enter_context(nc.semaphore(name))

        x = sb("x", [P, TT, D])
        raw = sb("raw", [P, RING, PIECE])
        whi = sb("whi", [P, RING, PIECE], F32R)
        wlo = sb("wlo", [P, RING, PIECE], F32R)
        act_hi = sb("act_hi", [P, KT, S], F32R)
        act_lo = sb("act_lo", [P, KT, S], F32R)
        rows = sb("rows", [P, R_END])
        cols = sb("cols", [P, G_END])
        cst = sb("cst", [P, C_END])
        level = sb("level", [P, len(LEVELS), P], U8)
        hot = sb("hot", [REL_BUCKETS, S])
        rel = sb("rel", [REL_BUCKETS, 8])
        id16 = sb("id16", [P, P], BF16)
        mask16 = sb("mask16", [P, P], BF16)
        xs = sb("xs", [P, TT, D])
        tmp = sb("tmp", [P, 2, BLK])
        junk = sb("junk", [P, D], BF16)
        post = sb("post", [P, D])
        proj = sb("proj", [P, TT, PROJ])
        fgw = sb("fgw", [P, KT, 8])
        fgw_hi = sb("fgw_hi", [P, KT, 8], F32R)
        fgw_lo = sb("fgw_lo", [P, KT, 8], F32R)
        lf = sb("lf", [P, 5, TT, 8])
        lb = sb("lb", [P, 8, 8])
        lam = sb("lam", [P, 8])
        sums = sb("sums", [P, 58])
        ms = sb("ms", [P, 32])
        rstd = sb("rstd", [P, 58])
        mhalf = sb("mhalf", [P, 32])
        mx = sb("mx", [P, 4])
        nmx = sb("nmx", [P, 4])
        den = sb("den", [P, 4])
        rden = sb("rden", [P, 6])
        with ExitStack() as ffn_part:
            sil, hid = (ffn_part.enter_context(nc.sbuf_tensor(n, [P, TT, FC], F32)) for n in ("sil", "hid"))
            hT_hi, hT_lo = (ffn_part.enter_context(nc.sbuf_tensor(n, [P, 2, S], F32R)) for n in ("hT_hi", "hT_lo"))
        with nc.sbuf_tensor("hg_attn", [P, 8, 3, P], F32) as attnT:
            pass
        q_sb = sb("att_q", [P, 2, S])
        k_sb = sb("att_k", [P, 2, S])
        e_sb = sb("att_e", [P, 2, 3 * P])
        pT_sb = sb("att_pT", [P, 2, 3 * P])
        dec_sb = sb("att_dec", [P, 2, 3 * P])

        acc = ctx.enter_context(nc.psum_tensor("acc", [P, TT, 2, BLK], F32))
        gu = ctx.enter_context(nc.psum_tensor("gu", [P, TT, BLK], F32))
        tp = ctx.enter_context(nc.psum_tensor("tp", [P, 2, BLK], F32))

        def pair(b):
            return [gu[:, :, :], acc[:, :, 0, :], acc[:, :, 1, :]][b % 3]

        def heads(ap, n):
            return ap.rearrange("p (h n) -> p h n", h=n)

        idn = cst[:, C_ID:C_ID + P]
        tri = cst[:, C_TRI:C_TRI + P]
        ones = cst[:, C_AFTER:C_AFTER + P]
        after = cst[:, C_AFTER + P:C_AFTER + 2 * P]

        x_in, head_in, tail_in = sem("x_in"), sem("head_in"), sem("tail_in")
        raw_in = [sem(f"raw_in{s}") for s in range(RING)]
        hi_ready, lo_ready, piece_used = sem("hi_ready"), sem("lo_ready"), sem("piece_used")
        row_product, row_copied, row_padded = sem("row_product"), sem("row_copied"), sem("row_padded")
        row_out, bias_in, post_in = sem("row_out"), sem("bias_in"), sem("post_in")
        dve_setup, act_setup = sem("dve_setup"), sem("act_setup")
        src_ready, turn_full, turn_scaled = sem("src_ready"), sem("turn_full"), sem("turn_scaled")
        act_hi_ready, act_lo_ready = sem("act_hi_ready"), sem("act_lo_ready")
        row_sums, head_squares, head_sums = sem("row_sums"), sem("head_squares"), sem("head_sums")
        rstd_ready, pool_step, dve_step = sem("rstd_ready"), sem("pool_step"), sem("dve_step")
        sil_ready, h_ready, hT_full = sem("sil_ready"), sem("h_ready"), sem("hT_full")
        hT_hi_ready, hT_lo_ready = sem("hT_hi_ready"), sem("hT_lo_ready")
        acc_first, x_ready = sem("acc_first"), sem("x_ready")
        evac_a, evac_d = sem("evac_a"), sem("evac_d")
        gate_product, gate_abs, gate_log, decay_ready = (
            sem("gate_product"), sem("gate_abs"), sem("gate_log"), sem("decay_ready"))
        lb_in, lb_exp, lam_in, lam_exp = sem("lb_in"), sem("lb_exp"), sem("lam_in"), sem("lam_exp")
        roped, moba_normed = sem("roped"), sem("moba_normed")
        staged, qkT_full, qT_ready, kT_ready = sem("staged"), sem("qkT_full"), sem("qT_ready"), sem("kT_ready")
        dec_ready, scores_done, logits_ready = sem("dec_ready"), sem("scores_done"), sem("logits_ready")
        max_found, nmax_ready, exp_done = sem("max_found"), sem("nmax_ready"), sem("exp_done")
        rden_ready, lam_scaled, other_scaled = sem("rden_ready"), sem("lam_scaled"), sem("other_scaled")
        pT_full, pT_a, pT_d, pv_done, o_out = sem("pT_full"), sem("pT_a"), sem("pT_d"), sem("pv_done"), sem("o_out")
        hg_sig, hg_turned, hg_f, hg_q0 = sem("hg_sig"), sem("hg_turned"), sem("hg_f"), sem("hg_q0")
        hg_q, hg_k, hg_tot, hg_prod, hg_copied = (
            sem("hg_q"), sem("hg_k"), sem("hg_tot"), sem("hg_prod"), sem("hg_copied"))
        hg_cross, hg_o, hg_gate = sem("hg_cross"), sem("hg_o"), sem("hg_gate")
        merge_gates, merged = sem("merge_gates"), sem("merged")
        out_in = sem("out_in")

        block = ctx.enter_context(nc.Block())

        def landed(k, r):
            return 32 * (k // RING + 1) + 32 * r

        def former(engine, done, p):
            if not (isinstance(p, int) and p == 0):
                engine.wait_ge(done, p)

        def turn_n(u):
            return 4 * u

        def src_n(u, t):
            return TT * u + t + 1

        norms = []
        for name in ("pre0", "post0", "pre1", "diff", "post1", "pre2", "post2", "pre3", "hg", "moba", "pre4"):
            if name == "diff":
                norms.append((name, 0, 2, 8, 1 / 128))
            elif name == "moba":
                norms.append((name, 0, 26, 32, 1 / 128))
            else:
                norms += [(name, t, 10 + 8 * t, 8, 1 / 128) if name == "hg" else (name, t, t, 1, 1 / D)
                          for t in range(TT)]

        def norm_n(name, t=0):
            return [(m, a) for m, a, *_ in norms].index((name, t)) + 1

        def row_n(name, t):
            return [(m, a) for m, a, *_ in norms if m[:2] == "pr" or m[:2] == "po"].index((name, t)) + 1

        def head_n(name, t=0):
            return [(m, a) for m, a, *_ in norms if m[:2] != "pr" and m[:2] != "po"].index((name, t)) + 1

        ACC_AFTER = [N_WIN, N_FFN2, N_WIN2, N_FFN3, N_END]

        def tot_of(n, t):
            if n == 0:
                return xs[:, t, :]
            if n == 1:
                return tmp[:, t, :]
            at = 512 - (1024 >> (n - 1))
            return post[:, t * 512 + at:t * 512 + at + (1024 >> n)]

        @block.sync
        def _(sp):
            sp.dma_start(x[:, 0, :], x_d[0:P, :]).then_inc(x_in, 16)
            sp.dma_start(x[:, 1, :], x_d[P:S, :]).then_inc(x_in, 16)

            def load(k, r, parts):
                if k >= RING:
                    sp.wait_ge(lo_ready, k - RING + 1 + 3 * r)
                for dst, src in parts:
                    sp.dma_start(dst, src).then_inc(raw_in[k % RING], 16)

            def gate_up(f, k, r, c, j):
                dst = raw[:, k % RING, :].rearrange("p (k n) -> p k n", k=4)
                load(k, r, [(dst[:, :, w * FC:(w + 1) * FC],
                             m.rearrange("(k p) n -> p k n", p=P)[:, 4 * j:4 * j + 4, bass.ds(c * FC, FC)])
                            for w, m in enumerate((wg_d[f], wu_d[f]))])

            def down(f, k, r, c):
                dst = raw[:, k % RING, :].rearrange("p (k n) -> p k n", k=2)
                load(k, r, [(dst[:, w, :], wd_d[f][bass.ds(c * FC + w * P, P), :]) for w in range(2)])

            def ffn(f, n0):
                gate_up(f, n0, 0, 0, 0)
                gate_up(f, n0 + 1, 0, 0, 1)

                def step(k, c, r):
                    gate_up(f, k, r, c, 0)
                    gate_up(f, k + 1, r, c, 1)
                    down(f, k + 2, r, c - 1)

                step(n0 + 2, 1, 0)
                with sp.Fori(2, NC) as c:
                    step(n0 - 1 + 6, c, c - 2)
                down(f, n0 + 3 * NC - 1, 0, NC - 1)

            def wide(w, k, r, col, j):
                dst = raw[:, k % RING, :].rearrange("p (k n) -> p k n", k=4)
                src = w.rearrange("(k p) n -> p k n", p=P)
                load(k, r, [(dst[:, 2 * a:2 * a + 2, :], src[:, 4 * j + 2 * a:4 * j + 2 * a + 2, bass.ds(col, BLK)])
                            for a in range(2)])

            def two_blocks(w, n0):
                for b in range(2):
                    for j in range(2):
                        wide(w, n0 + 2 * b + j, 0, b * BLK, j)

            def three_blocks(w, n0, i, group):
                for b in range(3):
                    for j in range(2):
                        wide(w, n0 + 2 * b + j, 2 * i, i * group + b * BLK, j)

            def post_gain(m):
                if m:
                    sp.wait_ge(x_ready, TT * m)
                else:
                    sp.wait_ge(dve_setup, 1)
                sp.dma_start(post[:, :], post_d[m:m + 1, :].to_broadcast([P, D])).then_inc(post_in, 16)

            ffn(0, N_FFN1)
            post_gain(0)
            with sp.Fori(0, 2) as i:
                three_blocks(win_d, N_WIN, i, 3 * BLK + 8)
            post_gain(1)
            two_blocks(wout_d, N_WOUT)
            ffn(1, N_FFN2)
            post_gain(2)
            with sp.Fori(0, 6) as i:
                three_blocks(win2_d, N_WIN2, i, 3 * BLK)
            two_blocks(whg_d, N_WHG)
            sp.wait_ge(hg_o, TT)
            sp.wait_ge(row_out, 16)
            for t in range(TT):
                sp.dma_start(heads(proj[:, t, HI:HI + D], 8),
                             bass.AP(tensor=skew_d.tensor, offset=P - 1 + t * P,
                                     ap=[[8 * TOEP - 1, P], [TOEP, 8], [1, P]])).then_inc(bias_in, 16)
            two_blocks(wat_d, N_WAT)
            two_blocks(wout2_d, N_WOUT2)
            ffn(2, N_FFN3)
            for t in range(TT):
                sp.wait_ge(x_ready, 4 * TT + t + 1)
                sp.dma_start(out_d[t * P:(t + 1) * P, :], x[:, t, :]).then_inc(out_in, 16)
            sp.wait_ge(out_in, 16 * TT)

        @block.tensor
        def _(pe):
            def three(out, hi, lo, w_hi, w_lo, start, stop):
                pe.matmul(out, hi, w_hi, start=start, stop=False)
                pe.matmul(out, hi, w_lo, start=False, stop=False)
                return pe.matmul(out, lo, w_hi, start=False, stop=stop)

            def wide(k, r, banks, j, first_tile=None):
                pe.wait_ge(lo_ready, k + 1 + 3 * r)
                w_hi = whi[:, k % RING, :].rearrange("p (k n) -> p k n", k=4)
                w_lo = wlo[:, k % RING, :].rearrange("p (k n) -> p k n", k=4)
                for t in range(TT):
                    for a in range(4):
                        f = 4 * j + a
                        mm = three(banks[:, t, :], act_hi[:, f, t * P:(t + 1) * P],
                                   act_lo[:, f, t * P:(t + 1) * P], w_hi[:, a, :], w_lo[:, a, :],
                                   start=(f == 0), stop=(f == KT - 1))
                    if first_tile is not None and t == 0:
                        mm.then_inc(first_tile, 1)
                mm.then_inc(piece_used, 1)

            def turn(u, src):
                for t in range(TT):
                    pe.wait_ge(src_ready, src_n(u, t))
                    for h in range(2):
                        f = turn_n(u) + 2 * t + h
                        if f >= 2:
                            pe.wait_ge(turn_scaled, f - 1)
                        for a in range(4):
                            mm = pe.transpose(tp[:, f % 2, a * P:(a + 1) * P], src(t, 4 * h + a), idn)
                        mm.then_inc(turn_full, 1)

            def from_xs(t, k):
                return xs[:, t, k * P:(k + 1) * P]

            def from_proj(col):
                return lambda t, k: proj[:, t, col + k * P:col + (k + 1) * P]

            def activations(u):
                pe.wait_ge(act_lo_ready, turn_n(u + 1))

            def ffn(f, n0):
                activations((T_FFN1, T_FFN2, T_FFN3)[f])
                h0 = f * NC

                def turn_hidden(c):
                    pe.wait_ge(h_ready, h0 + 1 + c)
                    for a in range(2):
                        for t in range(TT):
                            mm = pe.transpose(tp[:, 0, a * S + t * P:a * S + (t + 1) * P],
                                              hid[:, t, a * P:(a + 1) * P], idn)
                    mm.then_inc(hT_full, 1)

                def down(k, r, c, first, last):
                    pe.wait_ge(hT_lo_ready, h0 + 1 + c)
                    pe.wait_ge(lo_ready, k + 1 + 3 * r)
                    w_hi = whi[:, k % RING, :].rearrange("p (k n) -> p k n", k=2)
                    w_lo = wlo[:, k % RING, :].rearrange("p (k n) -> p k n", k=2)
                    for t in range(TT):
                        for a in range(2):
                            for b in range(2):
                                mm = three(acc[:, t, b, :], hT_hi[:, a, t * P:(t + 1) * P],
                                           hT_lo[:, a, t * P:(t + 1) * P], w_hi[:, a, b * BLK:(b + 1) * BLK],
                                           w_lo[:, a, b * BLK:(b + 1) * BLK], start=first and a == 0,
                                           stop=last and a == 1)
                        if last and t == 0:
                            mm.then_inc(acc_first, 1)
                    mm.then_inc(piece_used, 1)

                def step(k, r, c, first):
                    pe.wait_ge(h_ready, h0 + c)
                    wide(k, r, gu, 0)
                    turn_hidden(c - 1)
                    wide(k + 1, r, gu, 1)
                    down(k + 2, r, c - 1, first, False)

                wide(n0, 0, gu, 0)
                wide(n0 + 1, 0, gu, 1)
                step(n0 + 2, 0, 1, True)
                with pe.Fori(2, NC) as c:
                    step(n0 - 1 + 6, c - 2, c, False)
                turn_hidden(NC - 1)
                down(n0 + 3 * NC - 1, 0, NC - 1, False, True)

            def three_blocks(n0, g, i=0, reused=True):
                for b in range(3):
                    if reused:
                        pe.wait_ge(evac_a, g + b - 2 + 3 * i)
                        pe.wait_ge(evac_d, g + b - 2 + 3 * i)
                    for j in range(2):
                        wide(n0 + 2 * b + j, 2 * i, pair(b), j)

            def two_blocks(u, n0, first_tile=None):
                activations(u)
                for b in range(2):
                    for j in range(2):
                        wide(n0 + 2 * b + j, 0, acc[:, :, b, :], j, first_tile if b == j == 1 else None)

            def attention(kind, i):
                p = 4 * kind + i
                pe.wait_ge(staged, p + 1)
                former(pe, qT_ready, p)
                former(pe, kT_ready, p)
                if kind < 2:
                    for n in range(2):
                        for t in range(TT):
                            mm = pe.transpose(acc[:, 1, n, t * P:(t + 1) * P],
                                              xs[:, n, t * P:(t + 1) * P], idn)
                else:
                    for n in range(2):
                        for h in range(2):
                            for t in range(TT):
                                mm = pe.transpose(acc[:, 1, n, h * S + t * P:h * S + (t + 1) * P],
                                                  xs[:, n, t * S + h * P:t * S + (h + 1) * P], idn)
                mm.then_inc(qkT_full, 1)
                pe.wait_ge(qT_ready, p + 1)
                pe.wait_ge(kT_ready, p + 1)
                if kind == 0:
                    pe.wait_ge(dec_ready, 1 + i)
                former(pe, exp_done, p)
                for h in range(2):
                    q, k = q_sb[:, h, :], k_sb[:, h if kind == 2 else 0, :]
                    late, early = gu[:, 0, h * S:(h + 1) * S], gu[:, 1, h * P:(h + 1) * P]
                    mm = pe.matmul(late, q[:, P:S], k, start=True, stop=kind == 2)
                    if kind == 0:
                        pe.matmul(late[:, 0:P], ones, dec_sb[:, h, 0:P], start=False, stop=False)
                        pe.matmul(late, tri, dec_sb[:, h, P:3 * P], start=False, stop=False)
                    if kind < 2:
                        mm = pe.matmul(late[:, P:S], id16[:, :], mask16[:, :], start=False, stop=True)
                    mm = pe.matmul(early, q[:, 0:P], k[:, 0:P], start=True, stop=kind == 2)
                    if kind == 0:
                        pe.matmul(early, tri, dec_sb[:, h, 0:P], start=False, stop=False)
                    if kind < 2:
                        mm = pe.matmul(early, id16[:, :], mask16[:, :], start=False, stop=True)
                mm.then_inc(scores_done, 1)
                pe.wait_ge(exp_done, p + 1)
                former(pe, pT_a, p)
                former(pe, pT_d, p)
                for h in range(2):
                    for n in range(3):
                        mm = pe.transpose(acc[:, 0, h, n * P:(n + 1) * P], e_sb[:, h, n * P:(n + 1) * P], idn)
                mm.then_inc(pT_full, 1)
                pe.wait_ge(pT_a, p + 1)
                pe.wait_ge(pT_d, p + 1)
                former(pe, o_out, p)
                for h in range(2):
                    wid = 64 if kind == 0 else P
                    col = (FV + i * P + 64 * h) if kind == 0 else (DV + i * P) if kind == 1 else (AV + i * S + h * P)
                    v = [proj[:, t, bass.ds(col, wid)] for t in range(TT)]
                    o = [tp[:, 1, (2 * h + t) * P:(2 * h + t) * P + wid] for t in range(TT)]
                    pe.matmul(o[1], pT_sb[:, h, 0:P], v[0], start=True, stop=False)
                    pe.matmul(o[1], pT_sb[:, h, P:2 * P], v[1], start=False, stop=True)
                    mm = pe.matmul(o[0], pT_sb[:, h, 2 * P:3 * P], v[0], start=True, stop=True)
                mm.then_inc(pv_done, 1)

            def q_at(t, h):
                return proj[:, t, HQ + h * P:HQ + (h + 1) * P]

            def k_at(t, h):
                return proj[:, t, HF + h * P:HF + (h + 1) * P]

            def hgrn():
                where = [acc[:, 0, :, :], acc[:, 1, :, :], gu[:, :, :]]
                for t in range(TT):
                    pe.wait_ge(hg_sig, t + 1)
                    if t:
                        pe.wait_ge(hg_f, t)
                        pe.wait_ge(hg_k, t)
                        pe.wait_ge(hg_q0, t)
                    for n, src in enumerate((xs[:, t, :], proj[:, t, HF:HF + D], proj[:, t, HQ:HQ + D])):
                        for h in range(8):
                            mm = pe.transpose(where[n][:, h // 4, h % 4 * P:(h % 4 + 1) * P],
                                              src[:, h * P:(h + 1) * P], idn)
                    mm.then_inc(hg_turned, 1)
                for n in range(len(LEVELS) + 1):
                    for t in range(TT):
                        if n == 0:
                            if t == 0:
                                pe.wait_ge(hg_q0, TT)
                                pe.wait_ge(hg_f, TT)
                                pe.wait_ge(hg_k, TT)
                        else:
                            pe.wait_ge(hg_q, TT * (n - 1) + t + 1)
                            if n > 1:
                                pe.wait_ge(hg_k, TT * (n - 1) + t + 1)
                            pe.wait_ge(hg_copied, TT * (n - 1) + t + 1)
                        for h in range(8):
                            mm = pe.matmul(acc[:, t, h // 4, h % 4 * P:(h % 4 + 1) * P], k_at(t, h), q_at(t, h),
                                           start=True, stop=True)
                        mm.then_inc(hg_prod, 1)
                n = len(LEVELS)
                pe.wait_ge(hg_q, TT * n + 1)
                pe.wait_ge(hg_k, TT * n + 1)
                for h in range(8):
                    mm = pe.matmul(gu[:, h // 4, h % 4 * P:(h % 4 + 1) * P], k_at(0, h), q_at(1, h),
                                   start=True, stop=True)
                mm.then_inc(hg_prod, 1)
                for t in range(TT):
                    pe.wait_ge(hg_copied, TT * n + t + 1)
                    if t:
                        pe.wait_ge(hg_cross, 1)
                    for h in range(8):
                        v = [proj[:, a, HI + h * P:HI + (h + 1) * P] for a in range(TT)]
                        o = acc[:, t, h // 4, h % 4 * P:(h % 4 + 1) * P]
                        if t:
                            pe.matmul(o, attnT[:, h, 1, :], v[0], start=True, stop=False)
                        mm = pe.matmul(o, attnT[:, h, 2 if t else 0, :], v[t], start=not t, stop=True)
                    mm.then_inc(hg_o, 1)

            pe.wait_ge(head_in, 16 * 4)
            for h in range(8):
                if h >= 2:
                    pe.wait_ge(row_copied, h - 1)
                pe.matmul(tp[:, h % 2, 0:S], rel[:, h:h + 1].to_broadcast([REL_BUCKETS, P]), hot[:, :],
                          start=True, stop=True).then_inc(row_product, 1)
            pe.wait_ge(row_copied, 8)

            turn(T_FFN1, from_xs)
            ffn(0, N_FFN1)
            turn(T_WIN, from_xs)
            activations(T_WIN)
            pe.wait_ge(dve_setup, 1)
            for t in range(TT):
                for f in range(KT):
                    mm = three(tp[:, 0, t * 8:t * 8 + 8], act_hi[:, f, t * P:(t + 1) * P],
                               act_lo[:, f, t * P:(t + 1) * P], fgw_hi[:, f, :], fgw_lo[:, f, :],
                               start=f == 0, stop=f == KT - 1)
            mm.then_inc(gate_product, 1)
            three_blocks(N_WIN, 0, reused=False)
            three_blocks(N_WIN + 6, 3)
            pe.wait_ge(evac_a, 6)
            pe.wait_ge(evac_d, 6)
            pe.wait_ge(decay_ready, 1)
            attention(0, 0)
            with pe.Fori(1, 4) as i:
                attention(0, i)
            with pe.Fori(0, 4) as i:
                attention(1, i)
            turn(T_WOUT, from_proj(MIX))
            two_blocks(T_WOUT, N_WOUT, acc_first)
            turn(T_FFN2, from_xs)
            ffn(1, N_FFN2)
            turn(T_WIN2, from_xs)
            activations(T_WIN2)
            three_blocks(N_WIN2, 6, reused=False)
            with pe.Fori(0, 5) as i:
                three_blocks(N_WIN2 + 6, 9, i)
            pe.wait_ge(evac_a, 24)
            pe.wait_ge(evac_d, 24)
            hgrn()
            turn(T_WHG, from_proj(HQ))
            two_blocks(T_WHG, N_WHG)
            pe.wait_ge(merged, 2)
            with pe.Fori(0, 4) as i:
                attention(2, i)
            turn(T_WAT, from_proj(AQ))
            two_blocks(T_WAT, N_WAT)
            turn(T_WOUT2, from_proj(HG))
            two_blocks(T_WOUT2, N_WOUT2, acc_first)
            turn(T_FFN3, from_xs)
            ffn(2, N_FFN3)

        @block.scalar
        def _(act):
            def hi(k, r=0):
                act.wait_ge(raw_in[k % RING], landed(k, r))
                if k >= RING:
                    act.wait_ge(piece_used, k - RING + 1 + 3 * r)
                act.activation(whi[:, k % RING, :], raw[:, k % RING, :], ACT.Copy).then_inc(hi_ready, 1)

            def turn(u):
                if TURN_AFTER[u]:
                    act.wait_ge(piece_used, TURN_AFTER[u])
                for a in range(4):
                    f = turn_n(u) + a
                    act.wait_ge(turn_scaled, f + 1)
                    act.activation(act_hi[:, 4 * (a % 2):4 * (a % 2) + 4, a // 2 * P:(a // 2 + 1) * P],
                                   tmp[:, f % 2, :].rearrange("p (k n) -> p k n", k=4), ACT.Copy)\
                       .then_inc(act_hi_ready, 1)

            def x_sums(m):
                for t in range(TT):
                    if m:
                        act.wait_ge(x_ready, TT * (m - 1) + t + 1)
                    if m or t:
                        act.wait_ge(row_sums, row_n(f"pre{m}", t) - 1)
                    act.activation(junk[:, :], x[:, t, :], ACT.Square, accum_out=sums[:, t:t + 1]).then_inc(row_sums, 1)

            def acc_ready(j, t):
                if t == 0:
                    act.wait_ge(acc_first, j + 1)
                else:
                    act.wait_ge(piece_used, ACC_AFTER[j])

            def acc_sums(m):
                for t in range(TT):
                    acc_ready(m, t)
                    act.wait_ge(row_sums, row_n(f"post{m}", t) - 1)
                    act.activation(junk[:, :], acc[:, t, :, :].rearrange("p b n -> p (b n)"), ACT.Square,
                                   accum_out=sums[:, t:t + 1]).then_inc(row_sums, 1)

            def ffn(f, n0):
                h0 = f * NC

                def silu(k, r, c):
                    act.wait_ge(piece_used, k + 1 + 3 * r)
                    if not isinstance(c, int) or c or f:
                        act.wait_ge(h_ready, h0 + c)
                    act.activation(sil[:, :, :], gu[:, :, 0:FC], ACT.Silu).then_inc(sil_ready, 1)

                def hidden(k, r, c):
                    act.wait_ge(hT_full, h0 + 1 + c)
                    if k:
                        act.wait_ge(piece_used, k + 1 + 3 * r)
                    act.activation(hT_hi[:, :, :], tp[:, 0, :].rearrange("p (a n) -> p a n", a=2), ACT.Copy)\
                       .then_inc(hT_hi_ready, 1)

                hi(n0 + 1)
                hi(n0 + 2)
                hi(n0 + 3)
                silu(n0 + 1, 0, 0)
                hi(n0 + 4)
                hidden(0, 0, 0)
                hi(n0 + 5)
                silu(n0 + 3, 0, 1)
                hi(n0 + 6)
                hi(n0 + 7)
                with act.Fori(2, NC - 1) as c:
                    hidden(n0 + 4, c - 2, c - 1)
                    hi(n0 + 8, c - 2)
                    silu(n0 + 6, c - 2, c)
                    hi(n0 + 9, c - 2)
                    hi(n0 + 10, c - 2)
                hidden(n0 + 3 * NC - 5, 0, NC - 2)
                hi(n0 + 3 * NC - 1)
                silu(n0 + 3 * NC - 3, 0, NC - 1)
                hidden(n0 + 3 * NC - 2, 0, NC - 1)

            def evac(k, r, b, dst):
                act.wait_ge(piece_used, k + 1 + 3 * r)
                act.activation(dst, pair(b)[:, 0, :], ACT.Copy).then_inc(evac_a, 1)

            def attention(kind, i):
                p = 4 * kind + i
                n = 2 * P if kind < 2 else 4 * P
                former(act, qkT_full, p)
                for w, col in enumerate([(FQ, FK), (DQ, DK), (AQ, AK)][kind]):
                    last = act.activation(xs[:, w, 0:n].rearrange("p (t n) -> p t n", t=TT),
                                          proj[:, :, bass.ds(col + i * (n // 2), n // 2)], ACT.Copy,
                                          scale=FOX_SCALE if kind < 2 and w == 0 else 1.0)
                last.then_inc(staged, 1)
                act.wait_ge(qkT_full, p + 1)
                former(act, scores_done, p)
                if kind < 2:
                    act.activation(q_sb[0:64, 0, :], acc[0:64, 1, 0, 0:S], ACT.Copy)
                    act.activation(q_sb[64:P, 1, :], acc[64:P, 1, 0, 0:S], ACT.Copy).then_inc(qT_ready, 1)
                else:
                    act.activation(q_sb[:, :, :], heads(acc[:, 1, 0, :], 2), ACT.Copy,
                                   scale=cols[:, G_QG:G_QG + 1]).then_inc(qT_ready, 1)
                act.wait_ge(nmax_ready, p + 1)
                former(act, pT_full, p)
                former(act, rden_ready, p)
                for h in range(2):
                    late = gu[:, 0, h * S:(h + 1) * S] if kind < 2 else dec_sb[:, h, 0:S]
                    early = gu[:, 1, h * P:(h + 1) * P] if kind < 2 else dec_sb[:, h, S:3 * P]
                    act.activation(e_sb[:, h, 0:S], late, ACT.Exp, bias=nmx[:, h:h + 1], accum_out=den[:, h:h + 1])
                    last = act.activation(e_sb[:, h, S:3 * P], early, ACT.Exp, bias=nmx[:, 2 + h:3 + h],
                                          accum_out=den[:, 2 + h:3 + h])
                last.then_inc(exp_done, 1)
                act.wait_ge(pT_full, p + 1)
                former(act, pv_done, p)
                act.activation(pT_sb[:, 0, :], acc[:, 0, 0, 0:3 * P], ACT.Copy).then_inc(pT_a, 1)

            def two_blocks(n0):
                for k in range(1, 4):
                    hi(n0 + k)

            for dst, src in ((cst[:, :], const_d), (cols[:, :], cols_d), (hot[:, :], hot_d), (rel[:, :], rel_d)):
                act.dma_start(dst, src).then_inc(head_in, 16)
            act.dma_start(rows[:, :], rows_d.to_broadcast([P, R_END])).then_inc(tail_in, 16)
            act.dma_start(post[:, 0:len(LEVELS) * P], level_d).then_inc(tail_in, 16)
            with nc.allow_non_contiguous_dma(reason="eight columns"):
                act.dma_start(fgw[:, :, :], win_d.rearrange("(k p) n -> p k n", p=P)[:, :, FOX_GATE:FOX_GATE + 8])\
                   .then_inc(tail_in, 16)
            act.wait_ge(x_in, 16 * TT)
            x_sums(0)
            for h in range(8):
                act.wait_ge(row_product, h + 1)
                act.activation(proj[:, 0, h * TOEP:h * TOEP + S], tp[:, h % 2, 0:S], ACT.Copy).then_inc(row_copied, 1)
            hi(0)
            turn(T_FFN1)
            act.wait_ge(row_copied, 8)
            act.wait_ge(row_padded, 1)
            act.dma_start(skew_d.rearrange("(p n) -> p n", p=P), proj[:, 0, 0:8 * TOEP]).then_inc(row_out, 16)
            act.wait_ge(tail_in, 16 * 3)
            act.activation(fgw_hi[:, :, :], fgw[:, :, :], ACT.Copy).then_inc(act_setup, 1)
            ffn(0, N_FFN1)
            acc_sums(0)
            x_sums(1)
            hi(N_WIN)
            turn(T_WIN)
            hi(N_WIN + 1)
            hi(N_WIN + 2)
            act.wait_ge(gate_abs, 1)
            act.activation(lf[:, 2, :, :], lf[:, 1, :, :], ACT.Exp, scale=-1.0).then_inc(gate_log, 1)
            act.wait_ge(gate_log, 1)
            act.activation(lf[:, 3, :, :], lf[:, 2, :, :], ACT.Ln, bias=1.0).then_inc(gate_log, 1)
            act.wait_ge(lb_in, 1)
            act.activation(lb[:, 3:5, :], lb[:, 1:3, :], ACT.Exp).then_inc(lb_exp, 1)
            act.wait_ge(lam_in, 1)
            act.activation(lam[:, 2:4], lam[:, 0:2], ACT.Exp).then_inc(lam_exp, 1)
            hi(N_WIN + 3)
            act.wait_ge(row_out, 16)
            for b in range(6):
                evac(N_WIN + 2 * b + 1, 0, b, proj[:, 0, b * BLK:(b + 1) * BLK])
                for k in (2 * b + 4, 2 * b + 5):
                    if k < 12:
                        hi(N_WIN + k)
            act.wait_ge(evac_a, 6)
            act.wait_ge(evac_d, 6)
            attention(0, 0)
            with act.Fori(1, 4) as i:
                attention(0, i)
            act.wait_ge(roped, 1)
            with act.Fori(0, 4) as i:
                attention(1, i)
            act.wait_ge(o_out, 8)
            act.activation(xs[:, :, 0:BLK], proj[:, :, MIX + BLK:MIX + 2 * BLK], ACT.Square).then_inc(head_squares, 1)
            hi(N_WOUT)
            turn(T_WOUT)
            two_blocks(N_WOUT)
            acc_sums(1)
            x_sums(2)
            hi(N_FFN2)
            turn(T_FFN2)
            ffn(1, N_FFN2)
            acc_sums(2)
            x_sums(3)
            hi(N_WIN2)
            turn(T_WIN2)
            for k in range(1, 4):
                hi(N_WIN2 + k)
            evac(N_WIN2 + 1, 0, 0, proj[:, 0, 0:BLK])
            hi(N_WIN2 + 4)
            hi(N_WIN2 + 5)
            with act.Fori(0, 5) as i:
                for b in range(3):
                    evac(N_WIN2 + 3 + 2 * b, 2 * i, b + 1, proj[:, 0, bass.ds((1 + b) * BLK + i * (3 * BLK), BLK)])
                    hi(N_WIN2 + 6 + 2 * b, 2 * i)
                    hi(N_WIN2 + 7 + 2 * b, 2 * i)
            for b in (16, 17):
                evac(N_WIN2 + 2 * b + 1, 0, b, proj[:, 0, b * BLK:(b + 1) * BLK])
            act.wait_ge(evac_a, 24)
            act.wait_ge(evac_d, 24)
            for t in range(TT):
                act.activation(xs[:, t, :], proj[:, t, HF:HF + D], ACT.Sigmoid)
                act.activation(proj[:, t, HF:HF + D], proj[:, t, HF:HF + D], ACT.Sigmoid, scale=-1.0)
                act.activation(proj[:, t, HQ:HQ + D], proj[:, t, HQ:HQ + D], ACT.Copy, scale=HG_SCALE).then_inc(hg_sig, 1)
            for t in range(TT):
                act.wait_ge(hg_turned, t + 1)
                act.activation(proj[:, t, HQ:HQ + D], gu[:, :, :].rearrange("p b n -> p (b n)"), ACT.Copy)\
                   .then_inc(hg_q0, 1)
            hi(N_WHG)
            for t in range(TT):
                act.activation(proj[:, t, G0:G0 + 2 * D], proj[:, t, G0:G0 + 2 * D], ACT.Sigmoid).then_inc(merge_gates, 1)
            n = TT * (len(LEVELS) + 1)
            act.wait_ge(hg_prod, n + 1)
            act.activation(attnT[:, :, 1, :], heads(gu[:, :, :].rearrange("p b n -> p (b n)"), 8), ACT.Copy)\
               .then_inc(hg_cross, 1)
            for t in range(TT):
                act.activation(proj[:, t, HF:HF + D], proj[:, t, HG:HG + D], ACT.Sigmoid).then_inc(hg_gate, 1)
            for t in range(TT):
                act.wait_ge(hg_o, t + 1)
                act.activation(xs[:, t, :], acc[:, t, :, :].rearrange("p b n -> p (b n)"), ACT.Square)\
                   .then_inc(head_squares, 1)
            turn(T_WHG)
            two_blocks(N_WHG)
            for n, col in enumerate((AQ, AK)):
                for t in range(TT):
                    act.wait_ge(head_sums, head_n("hg", 1) + (2 * n + t - 1 if 2 * n + t > 1 else 0))
                    act.activation(xs[:, t, :], proj[:, t, col:col + D], ACT.Square).then_inc(head_squares, 1)
            hi(N_WAT)
            act.wait_ge(moba_normed, 1)
            with act.Fori(0, 4) as i:
                attention(2, i)
            turn(T_WAT)
            two_blocks(N_WAT)
            hi(N_WOUT2)
            turn(T_WOUT2)
            two_blocks(N_WOUT2)
            x_sums(4)
            hi(N_FFN3)
            turn(T_FFN3)
            ffn(2, N_FFN3)

        @block.gpsimd
        def _(pool):
            steps = [0]

            def link(ins):
                steps[0] += 1
                ins.then_inc(pool_step, 1)
                pool.wait_ge(pool_step, steps[0])

            def norm(name):
                for m, t, col, n, inv in norms:
                    if m != name:
                        continue
                    if name[:2] in ("pr", "po"):
                        pool.wait_ge(row_sums, row_n(name, t))
                    elif name == "moba":
                        pool.wait_ge(head_sums, head_n("hg", 1) + 4)
                    else:
                        pool.wait_ge(head_sums, head_n(name, t))
                    link(pool.tensor_scalar(ms[:, 0:n], sums[:, col:col + n], inv, EPS, ALU.mult, ALU.add))
                    pool.tensor_tensor(rstd[:, col:col + n], ms[:, 0:n], mhalf[:, 0:n], ALU.pow).then_inc(rstd_ready, 1)
                    pool.wait_ge(rstd_ready, norm_n(name, t))

            link(pool.memset(mhalf[:, :], -0.5))
            for name in ("pre0", "post0", "pre1", "diff", "post1", "pre2", "post2", "pre3"):
                norm(name)
            for n in range(2, len(LEVELS) + 2):
                m = 2 ** (n - 2)
                for t in range(TT if n <= len(LEVELS) else 1):
                    pool.wait_ge(hg_tot, TT * (n - 2) + t + 1)
                    pool.wait_ge(hg_prod, TT * (n - 1) + t + 1)
                    k = proj[:, t, HF:HF + D].rearrange("p (b two m) -> p b two m", two=2, m=m)[:, :, 0, :]
                    tot = tot_of(n - 2, t).rearrange("p (b two) -> p b two", two=2)[:, :, 1:2]
                    pool.tensor_tensor(k, k, tot.to_broadcast([P, D // (2 * m), m]), ALU.mult).then_inc(hg_k, 1)
            norm("hg")
            norm("moba")
            norm("pre4")

        @block.vector
        def _(dve):
            steps = [0]

            def link(ins):
                steps[0] += 1
                ins.then_inc(dve_step, 1)
                dve.wait_ge(dve_step, steps[0])

            def lo(k, r=0):
                dve.wait_ge(hi_ready, k + 1 + 3 * r)
                dve.tensor_tensor(wlo[:, k % RING, :], raw[:, k % RING, :], whi[:, k % RING, :].bitcast(F32),
                                  ALU.subtract).then_inc(lo_ready, 1)

            def turn(u):
                def scale(a):
                    f = turn_n(u) + a
                    dve.wait_ge(turn_full, f + 1)
                    if f >= 2:
                        dve.wait_ge(act_lo_ready, f - 1)
                    g = cols[:, G_TURN + 8 * u + 4 * (a % 2):G_TURN + 8 * u + 4 * (a % 2) + 4]
                    dve.tensor_tensor(heads(tmp[:, f % 2, :], 4), heads(tp[:, f % 2, :], 4), per(g, P), ALU.mult)\
                       .then_inc(turn_scaled, 1)

                def rest(a):
                    f = turn_n(u) + a
                    dve.wait_ge(act_hi_ready, f + 1)
                    s = (slice(None), slice(4 * (a % 2), 4 * (a % 2) + 4), slice(a // 2 * P, (a // 2 + 1) * P))
                    dve.tensor_tensor(act_lo[s], heads(tmp[:, f % 2, :], 4), act_hi[s].bitcast(F32), ALU.subtract)\
                       .then_inc(act_lo_ready, 1)

                scale(0)
                for a in range(1, 4):
                    scale(a)
                    rest(a - 1)
                rest(3)

            def prenorm(m, u):
                for t in range(TT):
                    dve.wait_ge(rstd_ready, norm_n(f"pre{m}", t))
                    dve.tensor_scalar(xs[:, t, :], x[:, t, :], rstd[:, t:t + 1], None, ALU.mult).then_inc(src_ready, 1)

            def postnorm(m):
                for t in range(TT):
                    dve.wait_ge(rstd_ready, norm_n(f"post{m}", t))
                    if t:
                        dve.wait_ge(piece_used, ACC_AFTER[m])
                    else:
                        dve.wait_ge(post_in, 16 * (m + 1))
                    if m != 1:
                        link(dve.tensor_scalar(rstd[:, t:t + 1], rstd[:, t:t + 1], 0.5, None, ALU.mult))
                    link(dve.scalar_tensor_tensor(out=xs[:, t, :], in0=acc[:, t, :, :].rearrange("p b n -> p (b n)"),
                                                  scalar=rstd[:, t:t + 1],
                                                  in1=post[:, :],
                                                  op0=ALU.mult, op1=ALU.mult))
                    dve.tensor_tensor(x[:, t, :], x[:, t, :], xs[:, t, :], ALU.add).then_inc(x_ready, 1)
                dve.wait_ge(x_ready, TT * (m + 1))

            def residual(j):
                for t in range(TT):
                    if t == 0:
                        dve.wait_ge(acc_first, j + 1)
                    else:
                        dve.wait_ge(piece_used, ACC_AFTER[j])
                    dve.tensor_tensor(x[:, t, :], x[:, t, :], acc[:, t, :, :].rearrange("p b n -> p (b n)"), ALU.add)\
                       .then_inc(x_ready, 1)
                dve.wait_ge(x_ready, TT * (j + 1))

            def ffn(f, n0):
                h0 = f * NC

                def product(c):
                    dve.wait_ge(sil_ready, h0 + 1 + c)
                    if f or not isinstance(c, int) or c:
                        dve.wait_ge(hT_full, h0 + c)
                    dve.tensor_tensor(hid[:, :, :], sil[:, :, :], gu[:, :, FC:2 * FC], ALU.mult).then_inc(h_ready, 1)

                def hidden(c):
                    dve.wait_ge(hT_hi_ready, h0 + 1 + c)
                    dve.tensor_tensor(hT_lo[:, :, :], tp[:, 0, :].rearrange("p (a n) -> p a n", a=2),
                                      hT_hi[:, :, :].bitcast(F32), ALU.subtract).then_inc(hT_lo_ready, 1)

                lo(n0 + 1)
                lo(n0 + 2)
                lo(n0 + 3)
                product(0)
                lo(n0 + 4)
                with dve.Fori(1, NC - 1) as c:
                    hidden(c - 1)
                    lo(n0 + 5, c - 1)
                    product(c)
                    lo(n0 + 6, c - 1)
                    lo(n0 + 7, c - 1)
                hidden(NC - 2)
                lo(n0 + 3 * NC - 1)
                product(NC - 1)
                hidden(NC - 1)

            def evac(k, r, b, dst):
                dve.wait_ge(piece_used, k + 1 + 3 * r)
                dve.tensor_copy(dst, pair(b)[:, 1, :]).then_inc(evac_d, 1)

            def attention(kind, i):
                p = 4 * kind + i
                if kind == 0:
                    former(dve, scores_done, p)
                    for h in range(2):
                        f0, f1 = (lf[:, 4, t, bass.ds(2 * i + h, 1)] for t in range(TT))
                        dve.tensor_scalar(dec_sb[:, h, 0:P], after, f0, None, ALU.mult)
                        last = dve.tensor_scalar(dec_sb[:, h, P:3 * P], cst[:, C_AFTER:C_AFTER + 2 * P], f1, None, ALU.mult)
                    last.then_inc(dec_ready, 1)
                dve.wait_ge(qkT_full, p + 1)
                former(dve, scores_done, p)
                if kind < 2:
                    dve.tensor_copy(k_sb[:, 0, :], acc[:, 1, 1, 0:S]).then_inc(kT_ready, 1)
                else:
                    dve.tensor_scalar(k_sb[:, :, :], heads(acc[:, 1, 1, :], 2), cols[:, G_KG:G_KG + 1], None, ALU.mult)\
                       .then_inc(kT_ready, 1)
                dve.wait_ge(scores_done, p + 1)
                former(dve, exp_done, p)
                late, early = heads(gu[:, 0, :], 2), heads(gu[:, 1, 0:S], 2)
                if kind == 2:
                    b = [heads(proj[:, t, bass.ds(HI + i * S, S)], 2) for t in range(TT)]
                    for t in range(TT):
                        dve.scalar_tensor_tensor(out=dec_sb[:, :, t * P:(t + 1) * P], in0=late[:, :, t * P:(t + 1) * P],
                                                 scalar=MOBA_SCALE, in1=b[t], op0=ALU.mult, op1=ALU.add)
                    dve.scalar_tensor_tensor(out=dec_sb[:, :, S:3 * P], in0=early, scalar=MOBA_SCALE, in1=b[1],
                                             op0=ALU.mult, op1=ALU.add).then_inc(logits_ready, 1)
                    dve.wait_ge(logits_ready, i + 1)
                    late, early = dec_sb[:, :, 0:S], dec_sb[:, :, S:3 * P]
                dve.tensor_reduce(mx[:, 0:2], late, AX, ALU.max)
                dve.tensor_reduce(mx[:, 2:4], early, AX, ALU.max).then_inc(max_found, 1)
                dve.wait_ge(max_found, p + 1)
                dve.tensor_scalar(nmx[:, :], mx[:, :], -1.0, None, ALU.mult).then_inc(nmax_ready, 1)
                dve.wait_ge(exp_done, p + 1)
                dve.reciprocal(rden[:, 0:4], den[:, :]).then_inc(rden_ready, 1)
                dve.wait_ge(rden_ready, p + 1)
                if kind == 1:
                    dve.tensor_scalar(rden[:, 4:6], rden[:, 1:4:2], lam[:, 5:6], None, ALU.mult).then_inc(lam_scaled, 1)
                dve.wait_ge(pT_full, p + 1)
                former(dve, pv_done, p)
                dve.tensor_copy(pT_sb[:, 1, :], acc[:, 0, 1, 0:3 * P]).then_inc(pT_d, 1)
                dve.wait_ge(pv_done, p + 1)
                for t in range(TT):
                    r = 0 if t else 2
                    if kind == 1:
                        o1, o2 = (tp[:, 1, (2 * h + t) * P:(2 * h + t + 1) * P] for h in range(2))
                        if t == 0:
                            dve.wait_ge(lam_scaled, i + 1)
                        dve.tensor_scalar(tmp[:, 0, t * P:(t + 1) * P], o2, rden[:, 4 + r // 2:5 + r // 2], None, ALU.mult)\
                           .then_inc(other_scaled, 1)
                        dve.wait_ge(other_scaled, 2 * i + t + 1)
                        last = dve.scalar_tensor_tensor(
                            out=proj[:, t, bass.ds(MIX + BLK + i * P, P)], in0=o1, scalar=rden[:, r:r + 1],
                            in1=tmp[:, 0, t * P:(t + 1) * P], op0=ALU.mult, op1=ALU.subtract)
                        continue
                    for h in range(2):
                        wid = 64 if kind == 0 else P
                        col = (MIX + i * P + 64 * h) if kind == 0 else (AQ + i * S + h * P)
                        last = dve.tensor_scalar(proj[:, t, bass.ds(col, wid)],
                                                 tp[:, 1, (2 * h + t) * P:(2 * h + t) * P + wid],
                                                 rden[:, r + h:r + h + 1], None, ALU.mult)
                last.then_inc(o_out, 1)

            def two_blocks(n0):
                for k in range(1, 4):
                    lo(n0 + k)

            def bank_pair(b):
                return acc[:, :, b, :]

            for h in range(8):
                last = dve.memset(proj[:, 0, h * TOEP + S:(h + 1) * TOEP], MASKED)
            last.then_inc(row_padded, 1)
            dve.wait_ge(head_in, 16 * 4)
            dve.wait_ge(x_in, 16 * TT)
            prenorm(0, T_FFN1)
            dve.tensor_copy(id16[:, :], idn)
            dve.tensor_copy(mask16[:, :], cst[:, C_MASK:C_MASK + P])
            lo(0)
            turn(T_FFN1)
            dve.wait_ge(tail_in, 16 * 3)
            dve.tensor_copy(level[:, :, :].rearrange("p l n -> p (l n)"), post[:, 0:len(LEVELS) * P])
            dve.wait_ge(act_setup, 1)
            dve.tensor_tensor(fgw_lo[:, :, :], fgw[:, :, :], fgw_hi[:, :, :].bitcast(F32), ALU.subtract).then_inc(dve_setup, 1)
            g = cols[:, G_TURN + 8 * T_WOUT + 4:G_TURN + 8 * T_WOUT + 8]
            link(dve.tensor_scalar(g, g, 1.0 - LAM_INIT, None, ALU.mult))
            ffn(0, N_FFN1)
            postnorm(0)
            prenorm(1, T_WIN)
            lo(N_WIN)
            turn(T_WIN)
            lo(N_WIN + 1)
            lo(N_WIN + 2)
            dve.wait_ge(gate_product, 1)
            for t in range(TT):
                ins = dve.tensor_tensor(lf[:, 0, t, :], tp[:, 0, 8 * t:8 * t + 8], rows[:, R_FB:R_FB + 8], ALU.add)
            link(ins)
            dve.scalar_tensor_tensor(out=lf[:, 1, :, :], in0=lf[:, 0, :, :], scalar=-1.0, in1=lf[:, 0, :, :],
                                     op0=ALU.mult, op1=ALU.max).then_inc(gate_abs, 1)
            g0, g1 = cols[:, G_GAM:G_GAM + 8], cols[:, G_GAM + 8:G_GAM + 16]
            link(dve.tensor_tensor(lb[:, 0, :], g0, g1, ALU.max))
            dve.tensor_tensor(lb[:, 1, :], g0, lb[:, 0, :], ALU.subtract)
            dve.tensor_tensor(lb[:, 2, :], g1, lb[:, 0, :], ALU.subtract).then_inc(lb_in, 1)
            for n in range(2):
                q1, k1 = (rows[:, R_LAM + (2 * n + a) * 64:R_LAM + (2 * n + a + 1) * 64] for a in range(2))
                ins = dve.tensor_tensor_reduce(tmp[:, 0, n * 64:(n + 1) * 64], q1, k1, 1.0, 0.0, ALU.mult, ALU.add,
                                               lam[:, n:n + 1])
            ins.then_inc(lam_in, 1)
            dve.wait_ge(lb_exp, 1)
            link(dve.tensor_tensor(lb[:, 5, :], lb[:, 3, :], lb[:, 4, :], ALU.add))
            link(dve.reciprocal(lb[:, 0, :], lb[:, 5, :]))
            link(dve.tensor_tensor(lb[:, 6, :], lb[:, 3, :], lb[:, 0, :], ALU.mult))
            dve.tensor_scalar(lb[:, 7, :], lb[:, 6, :], -1.0, 1.0, ALU.mult, ALU.add)
            dve.wait_ge(lam_exp, 1)
            link(dve.tensor_tensor(lam[:, 4:5], lam[:, 2:3], lam[:, 3:4], ALU.subtract))
            dve.tensor_scalar(lam[:, 5:6], lam[:, 4:5], LAM_INIT, None, ALU.add)
            dve.wait_ge(gate_log, 2)
            link(dve.scalar_tensor_tensor(out=lf[:, 4, :, :], in0=lf[:, 0, :, :], scalar=0.0, in1=lf[:, 3, :, :],
                                          op0=ALU.min, op1=ALU.subtract))
            dve.memset(q_sb[:, :, :], 0.0).then_inc(decay_ready, 1)
            lo(N_WIN + 3)
            dve.wait_ge(row_out, 16)
            for b in range(6):
                evac(N_WIN + 2 * b + 1, 0, b, proj[:, 1, b * BLK:(b + 1) * BLK])
                for k in (2 * b + 4, 2 * b + 5):
                    if k < 12:
                        lo(N_WIN + k)
            dve.wait_ge(evac_a, 6)
            dve.wait_ge(evac_d, 6)
            for t in range(TT):
                qk = proj[:, t, DQ:DQ + D].rearrange("p (g n) -> p g n", g=16)
                x1, x2 = qk[:, :, 0:8], qk[:, :, 8:16]
                c, s = (cst[:, C + 8 * t:C + 8 * t + 8].rearrange("p (o n) -> p o n", o=1).to_broadcast([P, 16, 8])
                        for C in (C_COS, C_SIN))
                part = [tmp[:, 1, n * P:(n + 1) * P].rearrange("p (g n) -> p g n", g=16) for n in range(4)]
                dve.tensor_tensor(part[0], x1, c, ALU.mult)
                dve.tensor_tensor(part[1], x2, s, ALU.mult)
                dve.tensor_tensor(part[2], x2, c, ALU.mult)
                link(dve.tensor_tensor(part[3], x1, s, ALU.mult))
                dve.tensor_tensor(x1, part[0], part[1], ALU.subtract)
                link(dve.tensor_tensor(x2, part[2], part[3], ALU.add))
            dve.nop().then_inc(roped, 1)
            attention(0, 0)
            with dve.Fori(1, 4) as i:
                attention(0, i)
            with dve.Fori(0, 4) as i:
                attention(1, i)
            dve.wait_ge(head_squares, 1)
            dve.tensor_reduce(sums[:, 2:10], xs[:, :, 0:BLK].rearrange("p t (h n) -> p t h n", h=4), AX, ALU.add)\
               .then_inc(head_sums, 1)
            lo(N_WOUT)
            dve.wait_ge(rstd_ready, norm_n("diff"))
            for t in range(TT):
                d = heads(proj[:, t, MIX + BLK:MIX + 2 * BLK], 4)
                dve.tensor_tensor(d, d, per(rstd[:, 2 + 4 * t:6 + 4 * t], P), ALU.mult).then_inc(src_ready, 1)
            turn(T_WOUT)
            two_blocks(N_WOUT)
            postnorm(1)
            prenorm(2, T_FFN2)
            lo(N_FFN2)
            turn(T_FFN2)
            ffn(1, N_FFN2)
            postnorm(2)
            prenorm(3, T_WIN2)
            lo(N_WIN2)
            turn(T_WIN2)
            for k in range(1, 4):
                lo(N_WIN2 + k)
            evac(N_WIN2 + 1, 0, 0, proj[:, 1, 0:BLK])
            lo(N_WIN2 + 4)
            lo(N_WIN2 + 5)
            with dve.Fori(0, 5) as i:
                for b in range(3):
                    evac(N_WIN2 + 3 + 2 * b, 2 * i, b + 1, proj[:, 1, bass.ds((1 + b) * BLK + i * (3 * BLK), BLK)])
                    lo(N_WIN2 + 6 + 2 * b, 2 * i)
                    lo(N_WIN2 + 7 + 2 * b, 2 * i)
            for b in (16, 17):
                evac(N_WIN2 + 2 * b + 1, 0, b, proj[:, 1, b * BLK:(b + 1) * BLK])
            for t in range(TT):
                dve.wait_ge(hg_turned, t + 1)
                f = heads(xs[:, t, :], 8)
                link(dve.tensor_tensor(f, heads(acc[:, 0, :, :].rearrange("p b n -> p (b n)"), 8), per(lb[:, 7, :], P),
                                       ALU.mult))
                dve.tensor_tensor(f, f, per(lb[:, 6, :], P), ALU.add).then_inc(hg_f, 1)
                dve.tensor_tensor(heads(proj[:, t, HF:HF + D], 8), heads(acc[:, 1, :, :].rearrange("p b n -> p (b n)"), 8),
                                  per(lb[:, 7, :], P), ALU.mult).then_inc(hg_k, 1)
                dve.wait_ge(hg_f, t + 1)
                dve.nop().then_inc(hg_tot, 1)
            lo(N_WHG)

            def diag(t, n):
                dve.wait_ge(hg_prod, TT * n + t + 1)
                src = heads(acc[:, t, :, :].rearrange("p b n -> p (b n)"), 8)
                dst = attnT[:, :, 2 * t, :]
                if n == 0:
                    ins = dve.tensor_tensor(dst, src, idn.rearrange("p (o n) -> p o n", o=1).to_broadcast([P, 8, P]), ALU.mult)
                else:
                    ins = dve.copy_predicated(dst, level[:, n - 1:n, :].to_broadcast([P, 8, P]), src)
                ins.then_inc(hg_copied, 1)

            for n in range(1, len(LEVELS) + 2):
                for t in range(TT):
                    dve.wait_ge(hg_prod, TT * (n - 1) + t + 1)
                    q = proj[:, t, HQ:HQ + D]
                    done = TT * (n - 1) + t + 1
                    if n > len(LEVELS):
                        if t == 0:
                            diag(t, n - 1)
                            continue
                        done -= 1
                    if n == 1:
                        dve.wait_ge(hg_q0, TT)
                        dve.tensor_tensor(q, q, xs[:, t, :], ALU.mult).then_inc(hg_q, 1)
                    else:
                        m = 2 ** (n - 2)
                        right = q.rearrange("p (b two m) -> p b two m", two=2, m=m)[:, :, 1, :]
                        tot = tot_of(n - 2, t).rearrange("p (b two) -> p b two", two=2)
                        dve.tensor_tensor(right, right, tot[:, :, 0:1].to_broadcast([P, D // (2 * m), m]), ALU.mult)\
                           .then_inc(hg_q, 1)
                        if n <= len(LEVELS):
                            nxt = tot_of(n - 1, t).rearrange("p (b o) -> p b o", o=1)
                            dve.tensor_tensor(nxt, tot[:, :, 0:1], tot[:, :, 1:2], ALU.mult).then_inc(hg_tot, 1)
                            dve.wait_ge(hg_tot, TT * (n - 1) + t + 1)
                    dve.wait_ge(hg_q, done)
                    diag(t, n - 1)
            for t in range(TT):
                dve.wait_ge(hg_gate, t + 1)
                link(dve.tensor_tensor(proj[:, t, HG:HG + D], proj[:, t, HG:HG + D], proj[:, t, HF:HF + D], ALU.mult))
            for t in range(TT):
                dve.wait_ge(head_squares, 2 + t)
                dve.tensor_reduce(sums[:, 10 + 8 * t:18 + 8 * t], heads(xs[:, t, :], 8), AX, ALU.add).then_inc(head_sums, 1)
            for t in range(TT):
                dve.wait_ge(rstd_ready, norm_n("hg", t))
                o = heads(proj[:, t, HQ:HQ + D], 8)
                link(dve.tensor_tensor(o, heads(acc[:, t, :, :].rearrange("p b n -> p (b n)"), 8),
                                       per(rstd[:, 10 + 8 * t:18 + 8 * t], P), ALU.mult))
                dve.tensor_tensor(proj[:, t, HQ:HQ + D], proj[:, t, HQ:HQ + D], proj[:, t, HG:HG + D], ALU.mult)\
                   .then_inc(src_ready, 1)
            turn(T_WHG)
            two_blocks(N_WHG)
            for n, col in enumerate((AQ, AK)):
                for t in range(TT):
                    dve.wait_ge(head_squares, 4 + 2 * n + t)
                    at = 26 + 8 * (2 * n + t)
                    dve.tensor_reduce(sums[:, at:at + 8], heads(xs[:, t, :], 8), AX, ALU.add).then_inc(head_sums, 1)
            dve.wait_ge(merge_gates, TT)
            for b in range(2):
                dve.wait_ge(piece_used, N_WHG + 4)
                s = slice(b * BLK, (b + 1) * BLK)
                dve.tensor_tensor(proj[:, :, HG:HG + D][:, :, s], bank_pair(b), proj[:, :, G0:G0 + D][:, :, s], ALU.mult)\
                   .then_inc(merged, 1)
            lo(N_WAT)
            dve.wait_ge(rstd_ready, norm_n("moba"))
            for n, col in enumerate((AQ, AK)):
                for t in range(TT):
                    at = 26 + 8 * (2 * n + t)
                    v = heads(proj[:, t, col:col + D], 8)
                    ins = dve.tensor_tensor(v, v, per(rstd[:, at:at + 8], P), ALU.mult)
            ins.then_inc(moba_normed, 1)
            dve.wait_ge(bias_in, 16 * TT)
            with dve.Fori(0, 4) as i:
                attention(2, i)
            dve.wait_ge(o_out, 12)
            dve.nop().then_inc(src_ready, TT)
            turn(T_WAT)
            two_blocks(N_WAT)
            for b in range(2):
                dve.wait_ge(piece_used, N_WAT + 4)
                s = slice(b * BLK, (b + 1) * BLK)
                link(dve.tensor_tensor(proj[:, :, G1:G1 + D][:, :, s], bank_pair(b), proj[:, :, G1:G1 + D][:, :, s], ALU.mult))
            for t in range(TT):
                dve.tensor_tensor(proj[:, t, HG:HG + D], proj[:, t, HG:HG + D], proj[:, t, G1:G1 + D], ALU.add)\
                   .then_inc(src_ready, 1)
            lo(N_WOUT2)
            turn(T_WOUT2)
            two_blocks(N_WOUT2)
            residual(3)
            prenorm(4, T_FFN3)
            lo(N_FFN3)
            turn(T_FFN3)
            ffn(2, N_FFN3)
            residual(4)


def kernel(**inputs):
    import concourse.bacc as bacc
    from concourse.bass_utils import run_bass_kernel_spmd

    def of(name, *shape):
        return np.ascontiguousarray(np.asarray(inputs[name]).reshape(shape))

    const, lv, hot_np = constants()
    one = np.ones((P, 8), np.float32)

    def by_feature(name):
        return of(name, KT, P).T

    def of_head(name, times):
        return np.repeat(of(name, P, 1), times, axis=1)

    packed_cols = np.concatenate([
        by_feature("ffn1_pre_g"), by_feature("mix_pre_g"),
        one[:, 0:4], of_head("diff_subln_g", 4),
        by_feature("ffn2_pre_g"), by_feature("attn_norm_g_2"), of_head("hg_out_norm_g_2", 8), one, one,
        by_feature("ffn_norm_g_2"), of("q_norm_g_2", P, 1), of("k_norm_g_2", P, 1),
        of("hg_lb_gamma_2", 2, KT, P).transpose(2, 0, 1).reshape(P, 16)], axis=1)
    packed_rows = np.concatenate([
        of(n, 1, 64) for n in ("diff_lambda_q1", "diff_lambda_k1", "diff_lambda_q2", "diff_lambda_k2")
    ] + [of("fox_forget_b", 1, 8)], axis=1)

    arrays = {"x": of("x", S, D)}
    for f, names in enumerate((("ffn1_w_gate", "ffn1_w_up", "ffn1_w_down"),
                               ("ffn2_w_gate", "ffn2_w_up", "ffn2_w_down"),
                               ("w_ffn_gate_2", "w_ffn_up_2", "w_ffn_down_2"))):
        for what, name in zip(("gate", "up"), names):
            arrays[f"{what}{f}"] = of(name, D, D_FF)
        arrays[f"down{f}"] = of(names[2], D_FF, D)
    arrays["w_in"] = of("w_in", D, 3080)
    arrays["w_out"] = of("w_out", D, D)
    arrays["w_in_2"] = of("w_in_2", D, PROJ)
    for name in ("w_branch_hg_2", "w_branch_attn_2", "w_out_2"):
        arrays[name] = of(name, D, D)
    arrays["packed_cols"] = np.ascontiguousarray(packed_cols)
    arrays["packed_rows"] = np.ascontiguousarray(packed_rows)
    arrays["post_gains"] = np.concatenate([of(n, 1, D) for n in ("ffn1_post_g", "mix_post_g", "ffn2_post_g")], axis=0)
    arrays["rel_table"] = of("rel_bias_table_2", REL_BUCKETS, 8)
    arrays["const"] = const
    arrays["level_masks"] = lv.reshape(P, -1)
    arrays["one_hot"] = hot_np

    nc = bacc.Bacc("TRN2", target_bir_lowering=False, num_devices=1)
    d = {n: nc.dram_tensor("in_" + n, a.shape, mybir.dt.from_np(a.dtype), kind="ExternalInput").ap() for n, a in arrays.items()}
    out = nc.dram_tensor("out", (S, D), F32, kind="ExternalOutput").ap()
    skew = nc.dram_tensor("skew", (P * 8 * TOEP,), F32, kind="Internal").ap()
    build(nc, d["x"], [d[f"gate{f}"] for f in range(3)], [d[f"up{f}"] for f in range(3)],
          [d[f"down{f}"] for f in range(3)], d["w_in"], d["w_out"], d["w_in_2"], d["w_branch_hg_2"],
          d["w_branch_attn_2"], d["w_out_2"], d["packed_cols"], d["packed_rows"], d["post_gains"], d["rel_table"], d["const"],
          d["level_masks"], d["one_hot"], out, skew)
    r = run_bass_kernel_spmd(nc, [{"in_" + n: a for n, a in arrays.items()}], core_ids=[0])
    return r.results[0]["out"].reshape(1, S, D)
```

```python
from contextlib import ExitStack

import numpy as np

import concourse.bass as bass
from concourse import mybir

F32 = mybir.dt.float32
F32R = mybir.dt.float32r
BF16 = mybir.dt.bfloat16
U8 = mybir.dt.uint8
ALU = mybir.AluOpType
ACT = mybir.ActivationFunctionType
AX = mybir.AxisListType.X

P = 128
S = 256
TT = S // P
D = 1024
KT = D // P
D_FF = 2816
FC = 256
NC = D_FF // FC
BLK = 512
RING = 3
PIECE = 2048
EPS = 1e-6
LAM_INIT = 0.2
ROPE_HALF = 8
ROPE_THETA = 500000.0
REL_BUCKETS, REL_MAX_DIST = 32, 128
MASKED = -1e30
HG_SCALE = float(128) ** -0.5
FOX_SCALE = 0.125
MOBA_SCALE = float(128) ** -0.5
FOX_HEADS = 8
FOX_GATE = 1536
TOEP = 384

AUG = 64 + 2
FQ, FK, FV, DQ, DK, DV, MIX = 0, 8 * AUG, 16 * AUG, 16 * AUG + 512, 16 * AUG + 1024, 16 * AUG + 1536, 16 * AUG + 2048
HQ, HF, HI, HG, AQ, AK, AV, G0, G1 = (1024 * n for n in range(9))
PROJ = 9 * 1024

FFN_PIECES = 3 * NC
N_FFN1 = 0
N_WIN = N_FFN1 + FFN_PIECES
N_WOUT = N_WIN + 12
N_FFN2 = N_WOUT + 4
N_WIN2 = N_FFN2 + FFN_PIECES
N_WHG = N_WIN2 + 36
N_WAT = N_WHG + 4
N_WOUT2 = N_WAT + 4
N_FFN3 = N_WOUT2 + 4
N_END = N_FFN3 + FFN_PIECES

T_FFN1, T_WIN, T_WOUT, T_FFN2, T_WIN2, T_WHG, T_WAT, T_WOUT2, T_FFN3 = range(9)
TURN_AFTER = [0, N_WIN, N_WOUT, N_FFN2, N_WIN2, N_WHG, N_WAT, N_WOUT2, N_FFN3]

C_ID, C_TRI, C_ONES, C_MASK, C_COS, C_SIN = 0, 128, 256, 384, 512, 528
C_END = 544
HG_FIRST, HG_LEAD, MOBA_FIRST = 24, 4, 60
LEVELS = [1, 2, 4, 8, 16, 32, 64]
R_LAM, R_FB, R_END = 0, 256, 264
G_TURN, G_QG, G_KG, G_GAM, G_END = 0, 72, 73, 74, 90


def constants():
    c = np.zeros((P, C_END), np.float32)
    row, col = np.arange(P)[:, None], np.arange(P)[None, :]
    c[:, C_ID:C_ID + P] = row == col
    c[:, C_TRI:C_TRI + P] = row <= col
    c[:, C_ONES:C_ONES + P] = 1.0
    c[:, C_MASK:C_MASK + P] = np.where(col > row, MASKED, 0.0)
    inv = np.float32(ROPE_THETA) ** (-np.arange(0, 16, 2, dtype=np.float32) / np.float32(16))
    ang = np.arange(S, dtype=np.float32)[:, None] * inv[None, :].astype(np.float32)
    for t in range(TT):
        c[:, C_COS + 8 * t:C_COS + 8 * t + 8] = np.cos(ang[t * P:(t + 1) * P])
        c[:, C_SIN + 8 * t:C_SIN + 8 * t + 8] = np.sin(ang[t * P:(t + 1) * P])
    lv = np.zeros((P, len(LEVELS), P), np.float32)
    for n, m in enumerate(LEVELS):
        lv[:, n, :] = (row // (2 * m) == col // (2 * m)) & (row // m % 2 == 0) & (col // m % 2 == 1)
    dist = 255 - np.arange(S)
    exact = REL_BUCKETS // 2
    nf = np.maximum(dist, 1).astype(np.float32)
    large = exact + (np.log(nf / exact) / np.log(REL_MAX_DIST / exact) * (REL_BUCKETS - exact)).astype(np.int32)
    bucket = np.where(dist < exact, dist, np.minimum(large, REL_BUCKETS - 1))
    hot = (np.arange(REL_BUCKETS)[:, None] == bucket[None, :]).astype(np.float32)
    return c, lv, hot


def per(ap, m):
    n = ap.shape[1]
    return ap.rearrange("p (k o) -> p k o", o=1).to_broadcast([ap.shape[0], n, m])


def build(nc, x_d, wg_d, wu_d, wd_d, win_d, wout_d, win2_d, whg_d, wat_d, wout2_d,
          cols_d, rows_d, post_d, rel_d, const_d, level_d, hot_d, out_d, skew_d):
    with ExitStack() as ctx:
        def sb(name, shape, dt=F32):
            return ctx.enter_context(nc.sbuf_tensor(name, shape, dt))

        def sem(name):
            return ctx.enter_context(nc.semaphore(name))

        x = sb("x", [P, TT, D])
        raw = sb("raw", [P, RING, PIECE])
        whi = sb("whi", [P, RING, PIECE], F32R)
        wlo = sb("wlo", [P, RING, PIECE], F32R)
        act_hi = sb("act_hi", [P, KT, S], F32R)
        act_lo = sb("act_lo", [P, KT, S], F32R)
        rows = sb("rows", [P, R_END])
        cols = sb("cols", [P, G_END])
        cst = sb("cst", [P, C_END])
        level = sb("level", [P, len(LEVELS), P], U8)
        hot = sb("hot", [REL_BUCKETS, S])
        rel = sb("rel", [REL_BUCKETS, 8])
        id16 = sb("id16", [P, P], BF16)
        mask16 = sb("mask16", [P, P], BF16)
        xs = sb("xs", [P, TT, D])
        tmp = sb("tmp", [P, 2, BLK])
        junk = sb("junk", [P, D], BF16)
        post = sb("post", [P, D])
        proj = sb("proj", [P, TT, PROJ])
        fgw = sb("fgw", [P, KT, 8])
        fgw_hi = sb("fgw_hi", [P, KT, 8], F32R)
        fgw_lo = sb("fgw_lo", [P, KT, 8], F32R)
        lf = sb("lf", [P, 5, TT, 8])
        lb = sb("lb", [P, 8, 8])
        lam = sb("lam", [P, 8])
        sums = sb("sums", [P, 58])
        ms = sb("ms", [P, 32])
        rstd = sb("rstd", [P, 58])
        mhalf = sb("mhalf", [P, 32])
        mx = sb("mx", [P, 8])
        nmx = sb("nmx", [P, 8])
        den = sb("den", [P, 4])
        rden = sb("rden", [P, 12])
        with ExitStack() as ffn_part:
            sil, hid = (ffn_part.enter_context(nc.sbuf_tensor(n, [P, TT, FC], F32)) for n in ("sil", "hid"))
            hT_hi, hT_lo = (ffn_part.enter_context(nc.sbuf_tensor(n, [P, 2, S], F32R)) for n in ("hT_hi", "hT_lo"))
        with nc.sbuf_tensor("hg_attn", [P, 8, 3, P], F32) as attnT:
            pass
        q_sb = sb("att_q", [P, 2, S])
        k_sb = sb("att_k", [P, 2, S])
        e_sb = sb("att_e", [P, 2, 3 * P])
        pT_sb = sb("att_pT", [P, 2, 3 * P])
        dec_sb = sb("att_dec", [P, 2, 3 * P])
        qd_sb = dec_sb[:, :, :].rearrange("p a n -> p (a n)")[:, 0:2 * S].rearrange("p (a n) -> p a n", a=2)

        acc = ctx.enter_context(nc.psum_tensor("acc", [P, TT, 2, BLK], F32))
        gu = ctx.enter_context(nc.psum_tensor("gu", [P, TT, BLK], F32))
        tp = ctx.enter_context(nc.psum_tensor("tp", [P, 2, BLK], F32))

        def block_banks(g):
            b = g - 6
            if b < 6:
                return [gu, acc[:, 0, :, :], acc[:, 1, :, :], tp, acc[:, 0, :, :], tp][g] if b < 0 else \
                    [gu, acc[:, 0, :, :], acc[:, 1, :, :]][b % 3]
            return [gu, tp][b % 2] if b < 14 else [acc[:, 0, :, :], tp][b % 2]

        FORMER = {4: 1, 5: 3, 12: 9, 14: 12, 15: 13, 16: 14, 17: 15, 18: 16, 19: 17, 21: 19, 22: 20, 23: 21}

        def heads(ap, n):
            return ap.rearrange("p (h n) -> p h n", h=n)

        idn = cst[:, C_ID:C_ID + P]
        tri = cst[:, C_TRI:C_TRI + P]
        ones = cst[:, C_ONES:C_ONES + P]

        x_in, head_in, tail_in = sem("x_in"), sem("head_in"), sem("tail_in")
        raw_in = [sem(f"raw_in{s}") for s in range(RING)]
        hi_ready, lo_ready, piece_used = sem("hi_ready"), sem("lo_ready"), sem("piece_used")
        row_product, row_copied, row_padded = sem("row_product"), sem("row_copied"), sem("row_padded")
        row_out, bias_in, post_in = sem("row_out"), sem("bias_in"), sem("post_in")
        dve_setup, act_setup = sem("dve_setup"), sem("act_setup")
        src_ready, turn_full, turn_scaled = sem("src_ready"), sem("turn_full"), sem("turn_scaled")
        act_hi_ready, act_lo_ready = sem("act_hi_ready"), sem("act_lo_ready")
        row_sums, head_squares, head_sums = sem("row_sums"), sem("head_squares"), sem("head_sums")
        rstd_ready, pool_step, dve_step = sem("rstd_ready"), sem("pool_step"), sem("dve_step")
        sil_ready, h_ready, hT_full = sem("sil_ready"), sem("h_ready"), sem("hT_full")
        hT_hi_ready, hT_lo_ready = sem("hT_hi_ready"), sem("hT_lo_ready")
        acc_first, x_ready = sem("acc_first"), sem("x_ready")
        evac_a, evac_d = sem("evac_a"), sem("evac_d")
        gate_product, gate_abs, gate_log = sem("gate_product"), sem("gate_abs"), sem("gate_log")
        log_f_ready, decay_sum, aug_ready, padded = (
            sem("log_f_ready"), sem("decay_sum"), sem("aug_ready"), sem("padded"))
        lb_in, lb_exp, lam_in, lam_exp = sem("lb_in"), sem("lb_exp"), sem("lam_in"), sem("lam_exp")
        roped, moba_normed = sem("roped"), sem("moba_normed")
        qkT_full, qT_ready, kT_ready = sem("qkT_full"), sem("qT_ready"), sem("kT_ready")
        scores_done, logits_ready = sem("scores_done"), sem("logits_ready")
        max_found, nmax_ready, exp_done = sem("max_found"), sem("nmax_ready"), sem("exp_done")
        rden_ready, lam_scaled, other_scaled = sem("rden_ready"), sem("lam_scaled"), sem("other_scaled")
        pT_full, pT_a, pT_d, pv_done, o_out = sem("pT_full"), sem("pT_a"), sem("pT_d"), sem("pv_done"), sem("o_out")
        hg_sig, hg_turned, hg_q_turned, hg_f, hg_q0 = (
            sem("hg_sig"), sem("hg_turned"), sem("hg_q_turned"), sem("hg_f"), sem("hg_q0"))
        hg_q, hg_k, hg_tot, hg_prod, hg_copied = (
            sem("hg_q"), sem("hg_k"), sem("hg_tot"), sem("hg_prod"), sem("hg_copied"))
        hg_cross, hg_o, hg_gate, hg_out = sem("hg_cross"), sem("hg_o"), sem("hg_gate"), sem("hg_out")
        merge_gates, merged = sem("merge_gates"), sem("merged")
        out_in = sem("out_in")

        block = ctx.enter_context(nc.Block())

        def landed(k, r):
            return 32 * (k // RING + 1) + 32 * r

        turned = acc[:, 1, :, :]

        def late(p):
            return (tp if p in (5, 7) else gu)[:, 0, :]

        def early(p):
            return (tp if p in (5, 7) else gu)[:, 1, 0:S]

        def o_bank(p):
            return acc[:, 0, p % 2, :] if 4 <= p < 8 else gu[:, 0, :]

        def logits(p):
            return dec_sb[:, :, :] if p % 2 else tmp[:, :, 0:3 * P]

        def win_place(b, t):
            if b < 2:
                return heads(proj[:, t, b * 8 * AUG:(b + 1) * 8 * AUG], 8)[:, :, 0:64]
            return proj[:, t, FV + (b - 2) * BLK:FV + (b - 1) * BLK]

        def turn_n(u):
            return 4 * u

        def src_n(u, t):
            return TT * u + t + 1

        norms = []
        for name in ("pre0", "post0", "pre1", "diff", "post1", "pre2", "post2", "pre3", "hg", "moba", "pre4"):
            if name == "diff":
                norms.append((name, 0, 2, 8, 1 / 128))
            elif name == "moba":
                norms.append((name, 0, 26, 32, 1 / 128))
            else:
                norms += [(name, t, 10 + 8 * t, 8, 1 / 128) if name == "hg" else (name, t, t, 1, 1 / D)
                          for t in range(TT)]

        def norm_n(name, t=0):
            return [(m, a) for m, a, *_ in norms].index((name, t)) + 1

        def row_n(name, t):
            return [(m, a) for m, a, *_ in norms if m[:2] == "pr" or m[:2] == "po"].index((name, t)) + 1

        def head_n(name, t=0):
            return [(m, a) for m, a, *_ in norms if m[:2] != "pr" and m[:2] != "po"].index((name, t)) + 1

        ACC_AFTER = [N_WIN, N_FFN2, N_WIN2, N_FFN3, N_END]

        def tot_of(n, t):
            if n == 0:
                return xs[:, t, :]
            if n == 1:
                return tmp[:, t, :]
            at = 512 - (1024 >> (n - 1))
            return post[:, t * 512 + at:t * 512 + at + (1024 >> n)]

        @block.sync
        def _(sp):
            sp.dma_start(x[:, 0, :], x_d[0:P, :]).then_inc(x_in, 16)
            sp.dma_start(x[:, 1, :], x_d[P:S, :]).then_inc(x_in, 16)

            def load(k, r, parts):
                if k >= RING:
                    sp.wait_ge(lo_ready, k - RING + 1 + 3 * r)
                for dst, src in parts:
                    sp.dma_start(dst, src).then_inc(raw_in[k % RING], 16)

            def gate_up(f, k, r, c, j):
                dst = raw[:, k % RING, :].rearrange("p (k n) -> p k n", k=4)
                load(k, r, [(dst[:, :, w * FC:(w + 1) * FC],
                             m.rearrange("(k p) n -> p k n", p=P)[:, 4 * j:4 * j + 4, bass.ds(c * FC, FC)])
                            for w, m in enumerate((wg_d[f], wu_d[f]))])

            def down(f, k, r, c):
                dst = raw[:, k % RING, :].rearrange("p (k n) -> p k n", k=2)
                load(k, r, [(dst[:, w, :], wd_d[f][bass.ds(c * FC + w * P, P), :]) for w in range(2)])

            def ffn(f, n0):
                gate_up(f, n0, 0, 0, 0)
                gate_up(f, n0 + 1, 0, 0, 1)

                def step(k, c, r):
                    gate_up(f, k, r, c, 0)
                    gate_up(f, k + 1, r, c, 1)
                    down(f, k + 2, r, c - 1)

                step(n0 + 2, 1, 0)
                with sp.Fori(2, NC) as c:
                    step(n0 - 1 + 6, c, c - 2)
                down(f, n0 + 3 * NC - 1, 0, NC - 1)

            def wide(w, k, r, col, j):
                dst = raw[:, k % RING, :].rearrange("p (k n) -> p k n", k=4)
                src = w.rearrange("(k p) n -> p k n", p=P)
                load(k, r, [(dst[:, 2 * a:2 * a + 2, :], src[:, 4 * j + 2 * a:4 * j + 2 * a + 2, bass.ds(col, BLK)])
                            for a in range(2)])

            def two_blocks(w, n0):
                for b in range(2):
                    for j in range(2):
                        wide(w, n0 + 2 * b + j, 0, b * BLK, j)

            def three_blocks(w, n0, i, group):
                for b in range(3):
                    for j in range(2):
                        wide(w, n0 + 2 * b + j, 2 * i, i * group + b * BLK, j)

            def post_gain(m):
                if m:
                    sp.wait_ge(x_ready, TT * m)
                else:
                    sp.wait_ge(dve_setup, 1)
                sp.dma_start(post[:, :], post_d[m:m + 1, :].to_broadcast([P, D])).then_inc(post_in, 16)

            ffn(0, N_FFN1)
            post_gain(0)
            with sp.Fori(0, 2) as i:
                three_blocks(win_d, N_WIN, i, 3 * BLK + 8)
            post_gain(1)
            two_blocks(wout_d, N_WOUT)
            ffn(1, N_FFN2)
            post_gain(2)
            with sp.Fori(0, 6) as i:
                three_blocks(win2_d, N_WIN2, i, 3 * BLK)
            two_blocks(whg_d, N_WHG)
            two_blocks(wat_d, N_WAT)
            two_blocks(wout2_d, N_WOUT2)
            ffn(2, N_FFN3)
            for t in range(TT):
                sp.wait_ge(x_ready, 4 * TT + t + 1)
                sp.dma_start(out_d[t * P:(t + 1) * P, :], x[:, t, :]).then_inc(out_in, 16)
            sp.wait_ge(out_in, 16 * TT)

        @block.tensor
        def _(pe):
            def three(out, hi, lo, w_hi, w_lo, start, stop):
                pe.matmul(out, hi, w_hi, start=start, stop=False)
                pe.matmul(out, hi, w_lo, start=False, stop=False)
                return pe.matmul(out, lo, w_hi, start=False, stop=stop)

            def half(k, r, banks, j, t):
                if t == 0:
                    pe.wait_ge(lo_ready, k + 1 + 3 * r)
                w_hi = whi[:, k % RING, :].rearrange("p (k n) -> p k n", k=4)
                w_lo = wlo[:, k % RING, :].rearrange("p (k n) -> p k n", k=4)
                for a in range(4):
                    f = 4 * j + a
                    mm = three(banks[:, t, :], act_hi[:, f, t * P:(t + 1) * P], act_lo[:, f, t * P:(t + 1) * P],
                               w_hi[:, a, :], w_lo[:, a, :], start=(f == 0), stop=(f == KT - 1))
                if t:
                    mm.then_inc(piece_used, 1)
                return mm

            def wide(k, r, banks, j, first_tile=None):
                mm = half(k, r, banks, j, 0)
                if first_tile is not None:
                    mm.then_inc(first_tile, 1)
                half(k, r, banks, j, 1)

            def block_half(n0, g0, h):
                g = g0 + h // 4
                if h % 4 == 0 and g in FORMER:
                    pe.wait_ge(evac_a, FORMER[g] + 1)
                    pe.wait_ge(evac_d, FORMER[g] + 1)
                half(n0 + h // 2, 0, block_banks(g), h // 2 % 2, h % 2)

            def turn(u, src):
                for t in range(TT):
                    pe.wait_ge(src_ready, src_n(u, t))
                    for h in range(2):
                        f = turn_n(u) + 2 * t + h
                        if f >= 2:
                            pe.wait_ge(turn_scaled, f - 1)
                        for a in range(4):
                            mm = pe.transpose(tp[:, f % 2, a * P:(a + 1) * P], src(t, 4 * h + a), idn)
                        mm.then_inc(turn_full, 1)

            def from_xs(t, k):
                return xs[:, t, k * P:(k + 1) * P]

            def from_proj(col):
                return lambda t, k: proj[:, t, col + k * P:col + (k + 1) * P]

            def activations(u):
                pe.wait_ge(act_lo_ready, turn_n(u + 1))

            def ffn(f, n0):
                activations((T_FFN1, T_FFN2, T_FFN3)[f])
                h0 = f * NC

                def turn_hidden(c):
                    pe.wait_ge(h_ready, h0 + 1 + c)
                    for a in range(2):
                        for t in range(TT):
                            mm = pe.transpose(tp[:, 0, a * S + t * P:a * S + (t + 1) * P],
                                              hid[:, t, a * P:(a + 1) * P], idn)
                    mm.then_inc(hT_full, 1)

                def down(k, r, c, first, last):
                    pe.wait_ge(hT_lo_ready, h0 + 1 + c)
                    pe.wait_ge(lo_ready, k + 1 + 3 * r)
                    w_hi = whi[:, k % RING, :].rearrange("p (k n) -> p k n", k=2)
                    w_lo = wlo[:, k % RING, :].rearrange("p (k n) -> p k n", k=2)
                    for t in range(TT):
                        for a in range(2):
                            for b in range(2):
                                mm = three(acc[:, t, b, :], hT_hi[:, a, t * P:(t + 1) * P],
                                           hT_lo[:, a, t * P:(t + 1) * P], w_hi[:, a, b * BLK:(b + 1) * BLK],
                                           w_lo[:, a, b * BLK:(b + 1) * BLK], start=first and a == 0,
                                           stop=last and a == 1)
                        if last and t == 0:
                            mm.then_inc(acc_first, 1)
                    mm.then_inc(piece_used, 1)

                def step(k, r, c, first):
                    pe.wait_ge(h_ready, h0 + c)
                    wide(k, r, gu, 0)
                    turn_hidden(c - 1)
                    wide(k + 1, r, gu, 1)
                    down(k + 2, r, c - 1, first, False)

                wide(n0, 0, gu, 0)
                wide(n0 + 1, 0, gu, 1)
                step(n0 + 2, 0, 1, True)
                with pe.Fori(2, NC) as c:
                    step(n0 - 1 + 6, c - 2, c, False)
                turn_hidden(NC - 1)
                down(n0 + 3 * NC - 1, 0, NC - 1, False, True)

            def two_blocks(u, n0, first_tile=None):
                activations(u)
                for b in range(2):
                    for j in range(2):
                        wide(n0 + 2 * b + j, 0, acc[:, :, b, :], j, first_tile if b == j == 1 else None)

            def turn_qk(p):
                kind, i = divmod(p, 4)
                for n in range(2):
                    for h in range(1 if kind == 1 else 2):
                        for t in range(TT):
                            if kind == 0:
                                src = proj[:, t, ((FQ, FK)[n] + (2 * i + h) * AUG):((FQ, FK)[n] + (2 * i + h + 1) * AUG)]
                            else:
                                col = (DQ, DK)[n] + i * P if kind == 1 else (AQ, AK)[n] + i * S + h * P
                                src = proj[:, t, col:col + P]
                            mm = pe.transpose(turned[0:src.shape[1], n, h * S + t * P:h * S + (t + 1) * P], src, idn)
                mm.then_inc(qkT_full, 1)

            def scores(p):
                kind = p // 4
                pe.wait_ge(qT_ready, p + 1)
                pe.wait_ge(kT_ready, p + 1)
                if p in (1, 2, 3, 4, 9, 10, 11):
                    pe.wait_ge(o_out, p)
                rows_used = AUG if kind == 0 else P
                for h in range(2):
                    q = (qd_sb if kind == 1 else q_sb)[0:rows_used, h, :]
                    k = k_sb[0:rows_used, 0 if kind == 1 else h, :]
                    lt, el = late(p)[:, h * S:(h + 1) * S], early(p)[:, h * P:(h + 1) * P]
                    mm = pe.matmul(lt, q[:, P:S], k, start=True, stop=kind == 2)
                    if kind < 2:
                        mm = pe.matmul(lt[:, P:S], id16[:, :], mask16[:, :], start=False, stop=True)
                    mm = pe.matmul(el, q[:, 0:P], k[:, 0:P], start=True, stop=kind == 2)
                    if kind < 2:
                        mm = pe.matmul(el, id16[:, :], mask16[:, :], start=False, stop=True)
                mm.then_inc(scores_done, 1)

            def turn_weights(p):
                pe.wait_ge(exp_done, p + 1)
                for h in range(2):
                    for n in range(3):
                        mm = pe.transpose(turned[:, h, n * P:(n + 1) * P], e_sb[:, h, n * P:(n + 1) * P], idn)
                mm.then_inc(pT_full, 1)

            def values(p):
                kind, i = divmod(p, 4)
                pe.wait_ge(pT_a, p + 1)
                pe.wait_ge(pT_d, p + 1)
                if p >= 2:
                    pe.wait_ge(o_out, p - 1)
                for h in range(2):
                    wid = 64 if kind == 0 else P
                    col = (FV + i * P + 64 * h, DV + i * P, AV + i * S + h * P)[kind]
                    v = [proj[:, t, col:col + wid] for t in range(TT)]
                    o = [o_bank(p)[:, (2 * h + t) * P:(2 * h + t) * P + wid] for t in range(TT)]
                    pe.matmul(o[1], pT_sb[:, h, 0:P], v[0], start=True, stop=False)
                    pe.matmul(o[1], pT_sb[:, h, P:2 * P], v[1], start=False, stop=True)
                    mm = pe.matmul(o[0], pT_sb[:, h, 2 * P:3 * P], v[0], start=True, stop=True)
                mm.then_inc(pv_done, 1)

            def attention(p0, p1):
                turn_qk(p0)
                scores(p0)
                turn_qk(p0 + 1)
                for p in range(p0, p1):
                    if p + 1 < p1:
                        scores(p + 1)
                    turn_weights(p)
                    values(p)
                    if p + 2 < p1:
                        turn_qk(p + 2)

            def q_at(t, h):
                return proj[:, t, HQ + h * P:HQ + (h + 1) * P]

            def k_at(t, h):
                return proj[:, t, HF + h * P:HF + (h + 1) * P]

            def hg_turn_sig(t):
                pe.wait_ge(hg_sig, t + 1)
                if t:
                    pe.wait_ge(hg_q0, t)
                    pe.wait_ge(hg_k, t)
                for n, src in enumerate((xs[:, t, :], proj[:, t, HF:HF + D])):
                    for h in range(8):
                        mm = pe.transpose(acc[:, n, h // 4, h % 4 * P:(h % 4 + 1) * P], src[:, h * P:(h + 1) * P], idn)
                mm.then_inc(hg_turned, 1)

            def hg_turn_q(t):
                pe.wait_ge(hg_f, t + 1)
                for h in range(8):
                    mm = pe.transpose(acc[:, 0, h // 4, h % 4 * P:(h % 4 + 1) * P], q_at(t, h), idn)
                mm.then_inc(hg_q_turned, 1)

            def hg_level(n, t):
                if n == 0:
                    pe.wait_ge(hg_q0, TT)
                    pe.wait_ge(hg_k, TT)
                else:
                    pe.wait_ge(hg_q, TT * (n - 1) + t + 1)
                    if n > 1:
                        pe.wait_ge(hg_k, TT * (n - 1) + t + 1)
                    pe.wait_ge(hg_copied, TT * (n - 1) + t + 1)
                for h in range(8):
                    mm = pe.matmul(acc[:, t, h // 4, h % 4 * P:(h % 4 + 1) * P], k_at(t, h), q_at(t, h),
                                   start=True, stop=True)
                mm.then_inc(hg_prod, 1)

            def hg_across():
                n = len(LEVELS)
                pe.wait_ge(hg_q, TT * n + 1)
                pe.wait_ge(hg_k, TT * n + 1)
                pe.wait_ge(hg_copied, TT * n + 1)
                for h in range(8):
                    mm = pe.matmul(acc[:, 0, h // 4, h % 4 * P:(h % 4 + 1) * P], k_at(0, h), q_at(1, h),
                                   start=True, stop=True)
                mm.then_inc(hg_prod, 1)

            def hg_values(t):
                pe.wait_ge(hg_copied, TT * len(LEVELS) + t + 1)
                pe.wait_ge(hg_cross, 1)
                for h in range(8):
                    v = [proj[:, a, HI + h * P:HI + (h + 1) * P] for a in range(TT)]
                    o = acc[:, t, h // 4, h % 4 * P:(h % 4 + 1) * P]
                    if t:
                        pe.matmul(o, attnT[:, h, 1, :], v[0], start=True, stop=False)
                    mm = pe.matmul(o, attnT[:, h, 2 if t else 0, :], v[t], start=not t, stop=True)
                mm.then_inc(hg_o, 1)

            def attention_between(p0, n0, g0, h0):
                turn_qk(p0)
                for p in range(p0, p0 + 4):
                    h = h0 + 3 * (p - p0)
                    if p == p0:
                        block_half(n0, g0, h0)
                    scores(p)
                    block_half(n0, g0, h + 1)
                    turn_weights(p)
                    block_half(n0, g0, h + 2)
                    values(p)
                    if p < p0 + 3:
                        turn_qk(p + 1)
                        block_half(n0, g0, h + 3)

            pe.wait_ge(head_in, 16 * 4)
            for h in range(8):
                if h >= 2:
                    pe.wait_ge(row_copied, h - 1)
                pe.matmul(tp[:, h % 2, 0:S], rel[:, h:h + 1].to_broadcast([REL_BUCKETS, P]), hot[:, :],
                          start=True, stop=True).then_inc(row_product, 1)
            pe.wait_ge(row_copied, 8)

            turn(T_FFN1, from_xs)
            ffn(0, N_FFN1)
            turn(T_WIN, from_xs)
            activations(T_WIN)
            pe.wait_ge(dve_setup, 1)
            for t in range(TT):
                for f in range(KT):
                    mm = three(tp[:, 0, t * 8:t * 8 + 8], act_hi[:, f, t * P:(t + 1) * P],
                               act_lo[:, f, t * P:(t + 1) * P], fgw_hi[:, f, :], fgw_lo[:, f, :],
                               start=f == 0, stop=f == KT - 1)
            mm.then_inc(gate_product, 1)
            for b in range(2):
                for a in range(4):
                    block_half(N_WIN, 0, 4 * b + a)
            pe.wait_ge(log_f_ready, 1)
            f = [lf[:, 4, t, :] for t in range(TT)]
            pe.matmul(tp[:, 1, 0:8], tri, f[0], start=True, stop=True)
            pe.matmul(tp[:, 1, 8:16], ones, f[0], start=True, stop=False)
            pe.matmul(tp[:, 1, 8:16], tri, f[1], start=False, stop=True).then_inc(decay_sum, 1)
            for a in range(4):
                block_half(N_WIN, 0, 8 + a)
            pe.wait_ge(aug_ready, 1)
            pe.wait_ge(evac_a, 3)
            pe.wait_ge(evac_d, 3)
            attention_between(0, N_WIN, 0, 12)
            pe.wait_ge(evac_a, 6)
            pe.wait_ge(evac_d, 6)
            pe.wait_ge(roped, 1)
            attention(4, 8)
            turn(T_WOUT, from_proj(MIX))
            two_blocks(T_WOUT, N_WOUT, acc_first)
            turn(T_FFN2, from_xs)
            ffn(1, N_FFN2)
            turn(T_WIN2, from_xs)
            activations(T_WIN2)
            with pe.Fori(0, 2) as i:
                for b in range(3):
                    pe.wait_ge(evac_a, 4 + b + 3 * i)
                    pe.wait_ge(evac_d, 4 + b + 3 * i)
                    for j in range(2):
                        wide(N_WIN2 + 2 * b + j, 2 * i, block_banks(6 + b), j)
            h = HG_FIRST
            for _ in range(HG_LEAD):
                block_half(N_WIN2, 6, h)
                h += 1
            pe.wait_ge(evac_a, 12)
            pe.wait_ge(evac_d, 12)
            for t in range(TT):
                hg_turn_sig(t)
                block_half(N_WIN2, 6, h)
                hg_turn_q(t)
                block_half(N_WIN2, 6, h + 1)
                h += 2
            for n in range(len(LEVELS) + 1):
                for t in range(TT):
                    hg_level(n, t)
                    block_half(N_WIN2, 6, h)
                    h += 1
            hg_across()
            block_half(N_WIN2, 6, h)
            hg_values(0)
            block_half(N_WIN2, 6, h + 1)
            hg_values(1)
            for h in range(h + 2, MOBA_FIRST):
                block_half(N_WIN2, 6, h)
            pe.wait_ge(hg_out, TT)
            pe.wait_ge(moba_normed, 2)
            attention_between(8, N_WIN2, 6, MOBA_FIRST)
            for h in range(MOBA_FIRST + 12, 72):
                block_half(N_WIN2, 6, h)
            pe.wait_ge(evac_a, 24)
            pe.wait_ge(evac_d, 24)
            turn(T_WHG, from_proj(HQ))
            two_blocks(T_WHG, N_WHG)
            turn(T_WAT, from_proj(AQ))
            pe.wait_ge(merged, 2)
            two_blocks(T_WAT, N_WAT)
            turn(T_WOUT2, from_proj(HG))
            two_blocks(T_WOUT2, N_WOUT2, acc_first)
            turn(T_FFN3, from_xs)
            ffn(2, N_FFN3)

        @block.scalar
        def _(act):
            def hi(k, r=0):
                act.wait_ge(raw_in[k % RING], landed(k, r))
                if k >= RING:
                    act.wait_ge(piece_used, k - RING + 1 + 3 * r)
                act.activation(whi[:, k % RING, :], raw[:, k % RING, :], ACT.Copy).then_inc(hi_ready, 1)

            def turn(u):
                if TURN_AFTER[u]:
                    act.wait_ge(piece_used, TURN_AFTER[u])
                for a in range(4):
                    f = turn_n(u) + a
                    act.wait_ge(turn_scaled, f + 1)
                    act.activation(act_hi[:, 4 * (a % 2):4 * (a % 2) + 4, a // 2 * P:(a // 2 + 1) * P],
                                   tmp[:, f % 2, :].rearrange("p (k n) -> p k n", k=4), ACT.Copy)\
                       .then_inc(act_hi_ready, 1)

            def x_sums(m):
                for t in range(TT):
                    if m:
                        act.wait_ge(x_ready, TT * (m - 1) + t + 1)
                    if m or t:
                        act.wait_ge(row_sums, row_n(f"pre{m}", t) - 1)
                    act.activation(junk[:, :], x[:, t, :], ACT.Square, accum_out=sums[:, t:t + 1]).then_inc(row_sums, 1)

            def acc_ready(j, t):
                if t == 0:
                    act.wait_ge(acc_first, j + 1)
                else:
                    act.wait_ge(piece_used, ACC_AFTER[j])

            def acc_sums(m):
                for t in range(TT):
                    acc_ready(m, t)
                    act.wait_ge(row_sums, row_n(f"post{m}", t) - 1)
                    act.activation(junk[:, :], acc[:, t, :, :].rearrange("p b n -> p (b n)"), ACT.Square,
                                   accum_out=sums[:, t:t + 1]).then_inc(row_sums, 1)

            def ffn(f, n0):
                h0 = f * NC

                def silu(k, r, c):
                    act.wait_ge(piece_used, k + 1 + 3 * r)
                    if not isinstance(c, int) or c or f:
                        act.wait_ge(h_ready, h0 + c)
                    act.activation(sil[:, :, :], gu[:, :, 0:FC], ACT.Silu).then_inc(sil_ready, 1)

                def hidden(k, r, c):
                    act.wait_ge(hT_full, h0 + 1 + c)
                    if k:
                        act.wait_ge(piece_used, k + 1 + 3 * r)
                    act.activation(hT_hi[:, :, :], tp[:, 0, :].rearrange("p (a n) -> p a n", a=2), ACT.Copy)\
                       .then_inc(hT_hi_ready, 1)

                hi(n0 + 1)
                hi(n0 + 2)
                hi(n0 + 3)
                silu(n0 + 1, 0, 0)
                hi(n0 + 4)
                hidden(0, 0, 0)
                hi(n0 + 5)
                silu(n0 + 3, 0, 1)
                hi(n0 + 6)
                hi(n0 + 7)
                with act.Fori(2, NC - 1) as c:
                    hidden(n0 + 4, c - 2, c - 1)
                    hi(n0 + 8, c - 2)
                    silu(n0 + 6, c - 2, c)
                    hi(n0 + 9, c - 2)
                    hi(n0 + 10, c - 2)
                hidden(n0 + 3 * NC - 5, 0, NC - 2)
                hi(n0 + 3 * NC - 1)
                silu(n0 + 3 * NC - 3, 0, NC - 1)
                hidden(n0 + 3 * NC - 2, 0, NC - 1)

            def evac(g, used, dst):
                act.wait_ge(piece_used, used)
                src = block_banks(g)[:, 0, :]
                act.activation(dst, heads(src, 8) if len(dst.shape) == 3 else src, ACT.Copy).then_inc(evac_a, 1)

            def after(n0, g0, h):
                if h % 2:
                    j = h // 2
                    if j % 2:
                        b = j // 2
                        evac(g0 + b, n0 + j + 1, win_place(b, 0) if g0 == 0 else proj[:, 0, b * BLK:(b + 1) * BLK])
                    if j + RING < (12 if g0 == 0 else 36):
                        hi(n0 + j + RING)

            def q_out(p):
                act.wait_ge(qkT_full, p + 1)
                if p // 4 == 1:
                    act.activation(qd_sb[0:64, 0, :], turned[0:64, 0, 0:S], ACT.Copy, scale=FOX_SCALE)
                    act.activation(qd_sb[64:P, 1, :], turned[64:P, 0, 0:S], ACT.Copy, scale=FOX_SCALE).then_inc(qT_ready, 1)
                else:
                    r = AUG if p < 4 else P
                    act.activation(q_sb[0:r, :, :], heads(turned[0:r, 0, :], 2), ACT.Copy,
                                   scale=FOX_SCALE if p < 4 else cols[:, G_QG:G_QG + 1]).then_inc(qT_ready, 1)

            def exps(p):
                act.wait_ge(nmax_ready, p + 1)
                if p:
                    act.wait_ge(pT_full, p)
                    act.wait_ge(rden_ready, p)
                src = logits(p)
                for h in range(2):
                    lt = late(p)[:, h * S:(h + 1) * S] if p < 8 else src[:, h, 0:S]
                    el = early(p)[:, h * P:(h + 1) * P] if p < 8 else src[:, h, S:3 * P]
                    n = 4 * (p % 2)
                    act.activation(e_sb[:, h, 0:S], lt, ACT.Exp, bias=nmx[:, n + h:n + h + 1], accum_out=den[:, h:h + 1])
                    last = act.activation(e_sb[:, h, S:3 * P], el, ACT.Exp, bias=nmx[:, n + 2 + h:n + 3 + h],
                                          accum_out=den[:, 2 + h:3 + h])
                last.then_inc(exp_done, 1)

            def weights_out(p):
                act.wait_ge(pT_full, p + 1)
                if p:
                    act.wait_ge(pv_done, p)
                act.activation(pT_sb[:, 0, :], turned[:, 0, 0:3 * P], ACT.Copy).then_inc(pT_a, 1)

            def attention(p0, p1):
                q_out(p0)
                exps(p0)
                q_out(p0 + 1)
                for p in range(p0, p1):
                    weights_out(p)
                    if p + 1 < p1:
                        exps(p + 1)
                    if p + 2 < p1:
                        q_out(p + 2)

            def attention_between(p0, n0, g0, h0, also=lambda p: None):
                q_out(p0)
                for p in range(p0, p0 + 4):
                    h = h0 + 3 * (p - p0)
                    if p == p0:
                        after(n0, g0, h0)
                    exps(p)
                    after(n0, g0, h + 1)
                    weights_out(p)
                    after(n0, g0, h + 2)
                    if p < p0 + 3:
                        q_out(p + 1)
                        after(n0, g0, h + 3)
                    also(p)

            def two_blocks(n0):
                for k in range(1, 4):
                    hi(n0 + k)

            for dst, src in ((cst[:, :], const_d), (cols[:, :], cols_d), (hot[:, :], hot_d), (rel[:, :], rel_d)):
                act.dma_start(dst, src).then_inc(head_in, 16)
            act.dma_start(rows[:, :], rows_d.to_broadcast([P, R_END])).then_inc(tail_in, 16)
            act.dma_start(post[:, 0:len(LEVELS) * P], level_d).then_inc(tail_in, 16)
            with nc.allow_non_contiguous_dma(reason="eight columns"):
                act.dma_start(fgw[:, :, :], win_d.rearrange("(k p) n -> p k n", p=P)[:, :, FOX_GATE:FOX_GATE + 8])\
                   .then_inc(tail_in, 16)
            act.wait_ge(x_in, 16 * TT)
            x_sums(0)
            for h in range(8):
                act.wait_ge(row_product, h + 1)
                act.activation(proj[:, 0, h * TOEP:h * TOEP + S], tp[:, h % 2, 0:S], ACT.Copy).then_inc(row_copied, 1)
            hi(0)
            turn(T_FFN1)
            act.wait_ge(row_copied, 8)
            act.wait_ge(row_padded, 1)
            act.dma_start(skew_d.rearrange("(p n) -> p n", p=P), proj[:, 0, 0:8 * TOEP]).then_inc(row_out, 16)
            act.wait_ge(tail_in, 16 * 3)
            act.activation(fgw_hi[:, :, :], fgw[:, :, :], ACT.Copy).then_inc(act_setup, 1)
            ffn(0, N_FFN1)
            acc_sums(0)
            x_sums(1)
            hi(N_WIN)
            turn(T_WIN)
            hi(N_WIN + 1)
            hi(N_WIN + 2)
            act.wait_ge(gate_abs, 1)
            act.activation(lf[:, 2, :, :], lf[:, 1, :, :], ACT.Exp, scale=-1.0).then_inc(gate_log, 1)
            act.wait_ge(gate_log, 1)
            act.activation(lf[:, 3, :, :], lf[:, 2, :, :], ACT.Ln, bias=1.0).then_inc(gate_log, 1)
            act.wait_ge(lb_in, 1)
            act.activation(lb[:, 3:5, :], lb[:, 1:3, :], ACT.Exp).then_inc(lb_exp, 1)
            act.wait_ge(lam_in, 1)
            act.activation(lam[:, 2:4], lam[:, 0:2], ACT.Exp).then_inc(lam_exp, 1)
            act.wait_ge(row_out, 16)
            for h in range(12):
                after(N_WIN, 0, h)
            attention_between(0, N_WIN, 0, 12)
            act.wait_ge(padded, 1)
            attention(4, 8)
            act.wait_ge(o_out, 8)
            act.activation(xs[:, :, 0:BLK], proj[:, :, MIX + BLK:MIX + 2 * BLK], ACT.Square).then_inc(head_squares, 1)
            hi(N_WOUT)
            turn(T_WOUT)
            two_blocks(N_WOUT)
            acc_sums(1)
            x_sums(2)
            hi(N_FFN2)
            turn(T_FFN2)
            ffn(1, N_FFN2)
            acc_sums(2)
            x_sums(3)
            hi(N_WIN2)
            turn(T_WIN2)
            hi(N_WIN2 + 1)
            hi(N_WIN2 + 2)
            with act.Fori(0, 2) as i:
                for b in range(3):
                    hi(N_WIN2 + 3 + 2 * b, 2 * i)
                    evac(6 + b, N_WIN2 + 2 + 2 * b + 6 * i, proj[:, 0, bass.ds(b * BLK + i * (3 * BLK), BLK)])
                    hi(N_WIN2 + 4 + 2 * b, 2 * i)
            h = HG_FIRST
            act.wait_ge(evac_d, 12)
            act.wait_ge(evac_a, 12)
            for t in range(TT):
                act.activation(xs[:, t, :], proj[:, t, HF:HF + D], ACT.Sigmoid)
                act.activation(proj[:, t, HF:HF + D], proj[:, t, HF:HF + D], ACT.Sigmoid, scale=-1.0)
                act.activation(proj[:, t, HQ:HQ + D], proj[:, t, HQ:HQ + D], ACT.Copy, scale=HG_SCALE).then_inc(hg_sig, 1)
                for _ in range(HG_LEAD // 2):
                    after(N_WIN2, 6, h)
                    h += 1
            for t in range(TT):
                after(N_WIN2, 6, h)
                act.wait_ge(hg_q_turned, t + 1)
                act.activation(proj[:, t, HQ:HQ + D], acc[:, 0, :, :].rearrange("p b n -> p (b n)"), ACT.Copy)\
                   .then_inc(hg_q0, 1)
                after(N_WIN2, 6, h + 1)
                h += 2
            n = TT * (len(LEVELS) + 1)
            for _ in range(n):
                after(N_WIN2, 6, h)
                h += 1
            act.wait_ge(hg_prod, n + 1)
            act.activation(attnT[:, :, 1, :], heads(acc[:, 0, :, :].rearrange("p b n -> p (b n)"), 8), ACT.Copy)\
               .then_inc(hg_cross, 1)
            after(N_WIN2, 6, h)
            for t in range(TT):
                act.wait_ge(hg_o, t + 1)
                act.activation(xs[:, t, :], acc[:, t, :, :].rearrange("p b n -> p (b n)"), ACT.Square)\
                   .then_inc(head_squares, 1)
                after(N_WIN2, 6, h + 1 + t)
            for h in range(h + 3, MOBA_FIRST):
                after(N_WIN2, 6, h)
            for n, col in enumerate((AQ, AK)):
                for t in range(TT):
                    act.wait_ge(head_sums, head_n("hg", 1) + (2 * n + t - 1 if 2 * n + t > 1 else 0))
                    act.activation(xs[:, t, :], proj[:, t, col:col + D], ACT.Square).then_inc(head_squares, 1)
            for t in range(TT):
                act.activation(proj[:, t, HF:HF + D], proj[:, t, HG:HG + D], ACT.Sigmoid).then_inc(hg_gate, 1)
            attention_between(8, N_WIN2, 6, MOBA_FIRST)
            for h in range(MOBA_FIRST + 12, 72):
                after(N_WIN2, 6, h)
            hi(N_WHG)
            turn(T_WHG)
            two_blocks(N_WHG)
            act.wait_ge(evac_d, 24)
            act.wait_ge(evac_a, 24)
            for t in range(TT):
                act.activation(proj[:, t, G0:G0 + 2 * D], proj[:, t, G0:G0 + 2 * D], ACT.Sigmoid).then_inc(merge_gates, 1)
            hi(N_WAT)
            turn(T_WAT)
            two_blocks(N_WAT)
            hi(N_WOUT2)
            turn(T_WOUT2)
            two_blocks(N_WOUT2)
            x_sums(4)
            hi(N_FFN3)
            turn(T_FFN3)
            ffn(2, N_FFN3)

        @block.gpsimd
        def _(pool):
            steps = [0]

            def link(ins):
                steps[0] += 1
                ins.then_inc(pool_step, 1)
                pool.wait_ge(pool_step, steps[0])

            def norm(name):
                for m, t, col, n, inv in norms:
                    if m != name:
                        continue
                    if name[:2] in ("pr", "po"):
                        pool.wait_ge(row_sums, row_n(name, t))
                    elif name == "moba":
                        pool.wait_ge(head_sums, head_n("hg", 1) + 4)
                    else:
                        pool.wait_ge(head_sums, head_n(name, t))
                    link(pool.tensor_scalar(ms[:, 0:n], sums[:, col:col + n], inv, EPS, ALU.mult, ALU.add))
                    pool.tensor_tensor(rstd[:, col:col + n], ms[:, 0:n], mhalf[:, 0:n], ALU.pow).then_inc(rstd_ready, 1)
                    pool.wait_ge(rstd_ready, norm_n(name, t))

            link(pool.memset(mhalf[:, :], -0.5))
            for name in ("pre0", "post0", "pre1"):
                norm(name)
            pool.wait_ge(evac_a, 5)
            pool.wait_ge(evac_d, 5)
            for t in range(TT):
                qk = proj[:, t, DQ:DQ + D].rearrange("p (g n) -> p g n", g=16)
                x1, x2 = qk[:, :, 0:8], qk[:, :, 8:16]
                c, s = (cst[:, C + 8 * t:C + 8 * t + 8].rearrange("p (o n) -> p o n", o=1).to_broadcast([P, 16, 8])
                        for C in (C_COS, C_SIN))
                part = [tmp[:, 1, n * P:(n + 1) * P].rearrange("p (g n) -> p g n", g=16) for n in range(4)]
                pool.tensor_tensor(part[0], x1, c, ALU.mult)
                pool.tensor_tensor(part[1], x2, s, ALU.mult)
                pool.tensor_tensor(part[2], x2, c, ALU.mult)
                link(pool.tensor_tensor(part[3], x1, s, ALU.mult))
                pool.tensor_tensor(x1, part[0], part[1], ALU.subtract)
                link(pool.tensor_tensor(x2, part[2], part[3], ALU.add))
            pool.nop().then_inc(roped, 1)
            for name in ("diff", "post1", "pre2", "post2", "pre3"):
                norm(name)
            for n in range(2, len(LEVELS) + 2):
                m = 2 ** (n - 2)
                for t in range(TT if n <= len(LEVELS) else 1):
                    pool.wait_ge(hg_tot, TT * (n - 2) + t + 1)
                    pool.wait_ge(hg_prod, TT * (n - 1) + t + 1)
                    k = proj[:, t, HF:HF + D].rearrange("p (b two m) -> p b two m", two=2, m=m)[:, :, 0, :]
                    tot = tot_of(n - 2, t).rearrange("p (b two) -> p b two", two=2)[:, :, 1:2]
                    pool.tensor_tensor(k, k, tot.to_broadcast([P, D // (2 * m), m]), ALU.mult).then_inc(hg_k, 1)
            pool.wait_ge(hg_o, TT)
            pool.wait_ge(row_out, 16)
            for t in range(TT):
                pool.dma_start(heads(proj[:, t, HI:HI + D], 8),
                             bass.AP(tensor=skew_d.tensor, offset=P - 1 + t * P,
                                     ap=[[8 * TOEP - 1, P], [TOEP, 8], [1, P]])).then_inc(bias_in, 16)
            norm("hg")
            norm("moba")
            for t in range(TT):
                v = heads(proj[:, t, AK:AK + D], 8)
                ins = pool.tensor_tensor(v, v, per(rstd[:, 42 + 8 * t:50 + 8 * t], P), ALU.mult)
            ins.then_inc(moba_normed, 1)
            norm("pre4")

        @block.vector
        def _(dve):
            steps = [0]

            def link(ins):
                steps[0] += 1
                ins.then_inc(dve_step, 1)
                dve.wait_ge(dve_step, steps[0])

            def lo(k, r=0):
                dve.wait_ge(hi_ready, k + 1 + 3 * r)
                dve.tensor_tensor(wlo[:, k % RING, :], raw[:, k % RING, :], whi[:, k % RING, :].bitcast(F32),
                                  ALU.subtract).then_inc(lo_ready, 1)

            def turn(u):
                def scale(a):
                    f = turn_n(u) + a
                    dve.wait_ge(turn_full, f + 1)
                    if f >= 2:
                        dve.wait_ge(act_lo_ready, f - 1)
                    g = cols[:, G_TURN + 8 * u + 4 * (a % 2):G_TURN + 8 * u + 4 * (a % 2) + 4]
                    dve.tensor_tensor(heads(tmp[:, f % 2, :], 4), heads(tp[:, f % 2, :], 4), per(g, P), ALU.mult)\
                       .then_inc(turn_scaled, 1)

                def rest(a):
                    f = turn_n(u) + a
                    dve.wait_ge(act_hi_ready, f + 1)
                    s = (slice(None), slice(4 * (a % 2), 4 * (a % 2) + 4), slice(a // 2 * P, (a // 2 + 1) * P))
                    dve.tensor_tensor(act_lo[s], heads(tmp[:, f % 2, :], 4), act_hi[s].bitcast(F32), ALU.subtract)\
                       .then_inc(act_lo_ready, 1)

                scale(0)
                for a in range(1, 4):
                    scale(a)
                    rest(a - 1)
                rest(3)

            def prenorm(m, u):
                for t in range(TT):
                    dve.wait_ge(rstd_ready, norm_n(f"pre{m}", t))
                    dve.tensor_scalar(xs[:, t, :], x[:, t, :], rstd[:, t:t + 1], None, ALU.mult).then_inc(src_ready, 1)

            def postnorm(m):
                for t in range(TT):
                    dve.wait_ge(rstd_ready, norm_n(f"post{m}", t))
                    if t:
                        dve.wait_ge(piece_used, ACC_AFTER[m])
                    else:
                        dve.wait_ge(post_in, 16 * (m + 1))
                    if m != 1:
                        link(dve.tensor_scalar(rstd[:, t:t + 1], rstd[:, t:t + 1], 0.5, None, ALU.mult))
                    link(dve.scalar_tensor_tensor(out=xs[:, t, :], in0=acc[:, t, :, :].rearrange("p b n -> p (b n)"),
                                                  scalar=rstd[:, t:t + 1],
                                                  in1=post[:, :],
                                                  op0=ALU.mult, op1=ALU.mult))
                    dve.tensor_tensor(x[:, t, :], x[:, t, :], xs[:, t, :], ALU.add).then_inc(x_ready, 1)
                dve.wait_ge(x_ready, TT * (m + 1))

            def residual(j):
                for t in range(TT):
                    if t == 0:
                        dve.wait_ge(acc_first, j + 1)
                    else:
                        dve.wait_ge(piece_used, ACC_AFTER[j])
                    dve.tensor_tensor(x[:, t, :], x[:, t, :], acc[:, t, :, :].rearrange("p b n -> p (b n)"), ALU.add)\
                       .then_inc(x_ready, 1)
                dve.wait_ge(x_ready, TT * (j + 1))

            def ffn(f, n0):
                h0 = f * NC

                def product(c):
                    dve.wait_ge(sil_ready, h0 + 1 + c)
                    if f or not isinstance(c, int) or c:
                        dve.wait_ge(hT_full, h0 + c)
                    dve.tensor_tensor(hid[:, :, :], sil[:, :, :], gu[:, :, FC:2 * FC], ALU.mult).then_inc(h_ready, 1)

                def hidden(c):
                    dve.wait_ge(hT_hi_ready, h0 + 1 + c)
                    dve.tensor_tensor(hT_lo[:, :, :], tp[:, 0, :].rearrange("p (a n) -> p a n", a=2),
                                      hT_hi[:, :, :].bitcast(F32), ALU.subtract).then_inc(hT_lo_ready, 1)

                lo(n0 + 1)
                lo(n0 + 2)
                lo(n0 + 3)
                product(0)
                lo(n0 + 4)
                with dve.Fori(1, NC - 1) as c:
                    hidden(c - 1)
                    lo(n0 + 5, c - 1)
                    product(c)
                    lo(n0 + 6, c - 1)
                    lo(n0 + 7, c - 1)
                hidden(NC - 2)
                lo(n0 + 3 * NC - 1)
                product(NC - 1)
                hidden(NC - 1)

            def evac(g, used, dst):
                dve.wait_ge(piece_used, used)
                src = block_banks(g)[:, 1, :]
                dve.tensor_copy(dst, heads(src, 8) if len(dst.shape) == 3 else src).then_inc(evac_d, 1)

            def after(n0, g0, h):
                if h % 2:
                    j = h // 2
                    if j % 2:
                        b = j // 2
                        evac(g0 + b, n0 + j + 1, win_place(b, 1) if g0 == 0 else proj[:, 1, b * BLK:(b + 1) * BLK])
                    if j + RING < (12 if g0 == 0 else 36):
                        lo(n0 + j + RING)

            def k_out(p):
                dve.wait_ge(qkT_full, p + 1)
                if p // 4 == 1:
                    dve.tensor_copy(k_sb[:, 0, :], turned[:, 1, 0:S]).then_inc(kT_ready, 1)
                elif p < 4:
                    dve.tensor_copy(k_sb[0:AUG, :, :], heads(turned[0:AUG, 1, :], 2)).then_inc(kT_ready, 1)
                else:
                    dve.tensor_scalar(k_sb[:, :, :], heads(turned[:, 1, :], 2), cols[:, G_KG:G_KG + 1], None, ALU.mult)\
                       .then_inc(kT_ready, 1)

            def maxima(p):
                dve.wait_ge(scores_done, p + 1)
                lt, el = heads(late(p), 2), heads(early(p), 2)
                if p >= 8:
                    if p >= 10:
                        dve.wait_ge(exp_done, p - 1)
                    i, dst = p - 8, logits(p)
                    b = [heads(proj[:, t, HI + i * S:HI + (i + 1) * S], 2) for t in range(TT)]
                    for t in range(TT):
                        dve.scalar_tensor_tensor(out=dst[:, :, t * P:(t + 1) * P], in0=lt[:, :, t * P:(t + 1) * P],
                                                 scalar=MOBA_SCALE, in1=b[t], op0=ALU.mult, op1=ALU.add)
                    dve.scalar_tensor_tensor(out=dst[:, :, S:3 * P], in0=el, scalar=MOBA_SCALE, in1=b[1],
                                             op0=ALU.mult, op1=ALU.add).then_inc(logits_ready, 1)
                    dve.wait_ge(logits_ready, i + 1)
                    lt, el = dst[:, :, 0:S], dst[:, :, S:3 * P]
                n = 4 * (p % 2)
                dve.tensor_reduce(mx[:, n:n + 2], lt, AX, ALU.max)
                dve.tensor_reduce(mx[:, n + 2:n + 4], el, AX, ALU.max).then_inc(max_found, 1)
                dve.wait_ge(max_found, p + 1)
                if p >= 2:
                    dve.wait_ge(exp_done, p - 1)
                dve.tensor_scalar(nmx[:, n:n + 4], mx[:, n:n + 4], -1.0, None, ALU.mult).then_inc(nmax_ready, 1)

            def weights_out(p):
                dve.wait_ge(exp_done, p + 1)
                n = 6 * (p % 2)
                dve.reciprocal(rden[:, n:n + 4], den[:, :]).then_inc(rden_ready, 1)
                dve.wait_ge(rden_ready, p + 1)
                if p // 4 == 1:
                    dve.tensor_scalar(rden[:, n + 4:n + 6], rden[:, n + 1:n + 4:2], lam[:, 5:6], None, ALU.mult)\
                       .then_inc(lam_scaled, 1)
                dve.wait_ge(pT_full, p + 1)
                if p:
                    dve.wait_ge(pv_done, p)
                dve.tensor_copy(pT_sb[:, 1, :], turned[:, 1, 0:3 * P]).then_inc(pT_d, 1)

            def output(p):
                kind, i = divmod(p, 4)
                dve.wait_ge(pv_done, p + 1)
                o = [[o_bank(p)[:, (2 * h + t) * P:(2 * h + t + 1) * P] for t in range(TT)] for h in range(2)]
                n = 6 * (p % 2)
                if kind == 1:
                    dve.wait_ge(lam_scaled, i + 1)
                    for t in range(TT):
                        r = n + 4 + (0 if t else 1)
                        ins = dve.tensor_scalar(tmp[:, 0, t * P:(t + 1) * P], o[1][t], rden[:, r:r + 1], None, ALU.mult)
                    ins.then_inc(other_scaled, 1)
                    dve.wait_ge(other_scaled, i + 1)
                for t in range(TT):
                    for h in range(1 if kind == 1 else 2):
                        r = rden[:, n + (0 if t else 2) + h:n + (0 if t else 2) + h + 1]
                        col = (MIX + i * P + 64 * h, MIX + BLK + i * P, AQ + i * S + h * P)[kind]
                        if kind == 1:
                            ins = dve.scalar_tensor_tensor(out=proj[:, t, col:col + P], in0=o[0][t], scalar=r,
                                                           in1=tmp[:, 0, t * P:(t + 1) * P], op0=ALU.mult, op1=ALU.subtract)
                        else:
                            wid = 64 if kind == 0 else P
                            ins = dve.tensor_scalar(proj[:, t, col:col + wid], o[h][t][:, 0:wid], r, None, ALU.mult)
                ins.then_inc(o_out, 1)

            def attention(p0, p1):
                k_out(p0)
                maxima(p0)
                k_out(p0 + 1)
                for p in range(p0, p1):
                    if p + 1 < p1:
                        maxima(p + 1)
                    weights_out(p)
                    output(p)
                    if p + 2 < p1:
                        k_out(p + 2)

            def attention_between(p0, n0, g0, h0, also=lambda p: None):
                k_out(p0)
                for p in range(p0, p0 + 4):
                    h = h0 + 3 * (p - p0)
                    if p == p0:
                        after(n0, g0, h0)
                    maxima(p)
                    after(n0, g0, h + 1)
                    weights_out(p)
                    after(n0, g0, h + 2)
                    output(p)
                    if p < p0 + 3:
                        k_out(p + 1)
                        after(n0, g0, h + 3)
                    also(p)

            def two_blocks(n0):
                for k in range(1, 4):
                    lo(n0 + k)

            def bank_pair(b):
                return acc[:, :, b, :]

            for h in range(8):
                last = dve.memset(proj[:, 0, h * TOEP + S:(h + 1) * TOEP], MASKED)
            last.then_inc(row_padded, 1)
            dve.wait_ge(head_in, 16 * 4)
            dve.wait_ge(x_in, 16 * TT)
            prenorm(0, T_FFN1)
            dve.tensor_copy(id16[:, :], idn)
            dve.tensor_copy(mask16[:, :], cst[:, C_MASK:C_MASK + P])
            lo(0)
            turn(T_FFN1)
            dve.wait_ge(tail_in, 16 * 3)
            dve.tensor_copy(level[:, :, :].rearrange("p l n -> p (l n)"), post[:, 0:len(LEVELS) * P])
            dve.wait_ge(act_setup, 1)
            dve.tensor_tensor(fgw_lo[:, :, :], fgw[:, :, :], fgw_hi[:, :, :].bitcast(F32), ALU.subtract).then_inc(dve_setup, 1)
            g = cols[:, G_TURN + 8 * T_WOUT + 4:G_TURN + 8 * T_WOUT + 8]
            link(dve.tensor_scalar(g, g, 1.0 - LAM_INIT, None, ALU.mult))
            ffn(0, N_FFN1)
            postnorm(0)
            prenorm(1, T_WIN)
            lo(N_WIN)
            turn(T_WIN)
            lo(N_WIN + 1)
            lo(N_WIN + 2)
            dve.wait_ge(gate_product, 1)
            for t in range(TT):
                ins = dve.tensor_tensor(lf[:, 0, t, :], tp[:, 0, 8 * t:8 * t + 8], rows[:, R_FB:R_FB + 8], ALU.add)
            link(ins)
            dve.scalar_tensor_tensor(out=lf[:, 1, :, :], in0=lf[:, 0, :, :], scalar=-1.0, in1=lf[:, 0, :, :],
                                     op0=ALU.mult, op1=ALU.max).then_inc(gate_abs, 1)
            g0, g1 = cols[:, G_GAM:G_GAM + 8], cols[:, G_GAM + 8:G_GAM + 16]
            link(dve.tensor_tensor(lb[:, 0, :], g0, g1, ALU.max))
            dve.tensor_tensor(lb[:, 1, :], g0, lb[:, 0, :], ALU.subtract)
            dve.tensor_tensor(lb[:, 2, :], g1, lb[:, 0, :], ALU.subtract).then_inc(lb_in, 1)
            for n in range(2):
                q1, k1 = (rows[:, R_LAM + (2 * n + a) * 64:R_LAM + (2 * n + a + 1) * 64] for a in range(2))
                ins = dve.tensor_tensor_reduce(tmp[:, 0, n * 64:(n + 1) * 64], q1, k1, 1.0, 0.0, ALU.mult, ALU.add,
                                               lam[:, n:n + 1])
            ins.then_inc(lam_in, 1)
            dve.wait_ge(lb_exp, 1)
            link(dve.tensor_tensor(lb[:, 5, :], lb[:, 3, :], lb[:, 4, :], ALU.add))
            link(dve.reciprocal(lb[:, 0, :], lb[:, 5, :]))
            link(dve.tensor_tensor(lb[:, 6, :], lb[:, 3, :], lb[:, 0, :], ALU.mult))
            dve.tensor_scalar(lb[:, 7, :], lb[:, 6, :], -1.0, 1.0, ALU.mult, ALU.add)
            dve.wait_ge(lam_exp, 1)
            link(dve.tensor_tensor(lam[:, 4:5], lam[:, 2:3], lam[:, 3:4], ALU.subtract))
            dve.tensor_scalar(lam[:, 5:6], lam[:, 4:5], LAM_INIT, None, ALU.add)
            dve.wait_ge(gate_log, 2)
            dve.scalar_tensor_tensor(out=lf[:, 4, :, :], in0=lf[:, 0, :, :], scalar=0.0, in1=lf[:, 3, :, :],
                                     op0=ALU.min, op1=ALU.subtract).then_inc(log_f_ready, 1)
            dve.memset(qd_sb, 0.0).then_inc(padded, 1)
            dve.wait_ge(row_out, 16)
            for h in range(12):
                after(N_WIN, 0, h)
                if h == 9:
                    dve.wait_ge(decay_sum, 1)
                    dve.wait_ge(evac_a, 2)
                    c = tp[:, 1, 0:16].rearrange("p (t h) -> p t h", t=TT)
                    q2, k2 = (proj[:, :, a:a + 8 * AUG].rearrange("p t (h n) -> p t h n", h=8) for a in (FQ, FK))
                    dve.tensor_scalar(q2[:, :, :, 64], c, 8.0, None, ALU.mult)
                    dve.tensor_scalar(k2[:, :, :, 65], c, -1.0, None, ALU.mult)
                    dve.memset(q2[:, :, :, 65], 8.0)
                    dve.memset(k2[:, :, :, 64], 1.0).then_inc(aug_ready, 1)
            attention_between(0, N_WIN, 0, 12)
            attention(4, 8)
            dve.wait_ge(head_squares, 1)
            dve.tensor_reduce(sums[:, 2:10], xs[:, :, 0:BLK].rearrange("p t (h n) -> p t h n", h=4), AX, ALU.add)\
               .then_inc(head_sums, 1)
            lo(N_WOUT)
            dve.wait_ge(rstd_ready, norm_n("diff"))
            for t in range(TT):
                d = heads(proj[:, t, MIX + BLK:MIX + 2 * BLK], 4)
                dve.tensor_tensor(d, d, per(rstd[:, 2 + 4 * t:6 + 4 * t], P), ALU.mult).then_inc(src_ready, 1)
            turn(T_WOUT)
            two_blocks(N_WOUT)
            postnorm(1)
            prenorm(2, T_FFN2)
            lo(N_FFN2)
            turn(T_FFN2)
            ffn(1, N_FFN2)
            postnorm(2)
            prenorm(3, T_WIN2)
            lo(N_WIN2)
            turn(T_WIN2)
            lo(N_WIN2 + 1)
            lo(N_WIN2 + 2)
            with dve.Fori(0, 2) as i:
                for b in range(3):
                    lo(N_WIN2 + 3 + 2 * b, 2 * i)
                    evac(6 + b, N_WIN2 + 2 + 2 * b + 6 * i, proj[:, 1, bass.ds(b * BLK + i * (3 * BLK), BLK)])
                    lo(N_WIN2 + 4 + 2 * b, 2 * i)
            h = HG_FIRST
            for _ in range(HG_LEAD):
                after(N_WIN2, 6, h)
                h += 1
            for t in range(TT):
                dve.wait_ge(hg_turned, t + 1)
                f = heads(xs[:, t, :], 8)
                link(dve.tensor_tensor(f, heads(acc[:, 0, :, :].rearrange("p b n -> p (b n)"), 8), per(lb[:, 7, :], P),
                                       ALU.mult))
                dve.tensor_tensor(f, f, per(lb[:, 6, :], P), ALU.add).then_inc(hg_f, 1)
                dve.tensor_tensor(heads(proj[:, t, HF:HF + D], 8), heads(acc[:, 1, :, :].rearrange("p b n -> p (b n)"), 8),
                                  per(lb[:, 7, :], P), ALU.mult).then_inc(hg_k, 1)
                after(N_WIN2, 6, h)
                dve.wait_ge(hg_f, t + 1)
                dve.nop().then_inc(hg_tot, 1)
                after(N_WIN2, 6, h + 1)
                h += 2

            def decay_q(n, t):
                dve.wait_ge(hg_prod, TT * (n - 1) + t + 1)
                q = proj[:, t, HQ:HQ + D]
                if n == 1:
                    dve.wait_ge(hg_q0, TT)
                    dve.tensor_tensor(q, q, xs[:, t, :], ALU.mult).then_inc(hg_q, 1)
                    return
                m = 2 ** (n - 2)
                right = q.rearrange("p (b two m) -> p b two m", two=2, m=m)[:, :, 1, :]
                tot = tot_of(n - 2, t).rearrange("p (b two) -> p b two", two=2)
                dve.wait_ge(hg_q, TT * (n - 2) + t + 1)
                dve.tensor_tensor(right, right, tot[:, :, 0:1].to_broadcast([P, D // (2 * m), m]), ALU.mult)\
                   .then_inc(hg_q, 1)
                if n <= len(LEVELS):
                    nxt = tot_of(n - 1, t).rearrange("p (b o) -> p b o", o=1)
                    dve.tensor_tensor(nxt, tot[:, :, 0:1], tot[:, :, 1:2], ALU.mult).then_inc(hg_tot, 1)
                    dve.wait_ge(hg_tot, TT * (n - 1) + t + 1)

            def diag(n, t):
                dve.wait_ge(hg_prod, TT * n + t + 1)
                src = heads(acc[:, t, :, :].rearrange("p b n -> p (b n)"), 8)
                dst = attnT[:, :, 2 * t, :]
                if n == 0:
                    ins = dve.tensor_tensor(dst, src, idn.rearrange("p (o n) -> p o n", o=1).to_broadcast([P, 8, P]), ALU.mult)
                else:
                    ins = dve.copy_predicated(dst, level[:, n - 1:n, :].to_broadcast([P, 8, P]), src)
                ins.then_inc(hg_copied, 1)

            for n in range(len(LEVELS) + 1):
                for t in range(TT):
                    if n < len(LEVELS) or t:
                        decay_q(n + 1, t)
                    diag(n, t)
                    after(N_WIN2, 6, h)
                    h += 1
            after(N_WIN2, 6, h)
            for t in range(TT):
                dve.wait_ge(head_squares, 2 + t)
                dve.tensor_reduce(sums[:, 10 + 8 * t:18 + 8 * t], heads(xs[:, t, :], 8), AX, ALU.add).then_inc(head_sums, 1)
                after(N_WIN2, 6, h + 1 + t)
            for t in range(TT):
                dve.wait_ge(rstd_ready, norm_n("hg", t))
                dve.tensor_tensor(heads(proj[:, t, HQ:HQ + D], 8), heads(acc[:, t, :, :].rearrange("p b n -> p (b n)"), 8),
                                  per(rstd[:, 10 + 8 * t:18 + 8 * t], P), ALU.mult).then_inc(hg_out, 1)
            for h in range(h + 3, MOBA_FIRST):
                after(N_WIN2, 6, h)
            for n, col in enumerate((AQ, AK)):
                for t in range(TT):
                    dve.wait_ge(head_squares, 4 + 2 * n + t)
                    at = 26 + 8 * (2 * n + t)
                    dve.tensor_reduce(sums[:, at:at + 8], heads(xs[:, t, :], 8), AX, ALU.add).then_inc(head_sums, 1)
            dve.wait_ge(rstd_ready, norm_n("moba"))
            for t in range(TT):
                v = heads(proj[:, t, AQ:AQ + D], 8)
                ins = dve.tensor_tensor(v, v, per(rstd[:, 26 + 8 * t:34 + 8 * t], P), ALU.mult)
            dve.wait_ge(bias_in, 16 * TT)
            ins.then_inc(moba_normed, 1)

            def gate_of(p):
                t = p - 8
                if t < TT:
                    dve.wait_ge(hg_gate, t + 1)
                    s = proj[:, t, HG:HG + D]
                    link(dve.tensor_tensor(s, s, proj[:, t, HF:HF + D], ALU.mult))
                    dve.wait_ge(hg_out, TT)
                    o = proj[:, t, HQ:HQ + D]
                    dve.tensor_tensor(o, o, s, ALU.mult).then_inc(src_ready, 1)

            attention_between(8, N_WIN2, 6, MOBA_FIRST, gate_of)
            for h in range(MOBA_FIRST + 12, 72):
                after(N_WIN2, 6, h)
            lo(N_WHG)
            turn(T_WHG)
            two_blocks(N_WHG)
            dve.wait_ge(o_out, 12)
            dve.nop().then_inc(src_ready, TT)
            dve.wait_ge(merge_gates, TT)
            for b in range(2):
                dve.wait_ge(piece_used, N_WHG + 4)
                s = slice(b * BLK, (b + 1) * BLK)
                dve.tensor_tensor(proj[:, :, HG:HG + D][:, :, s], bank_pair(b), proj[:, :, G0:G0 + D][:, :, s], ALU.mult)\
                   .then_inc(merged, 1)
            lo(N_WAT)
            turn(T_WAT)
            two_blocks(N_WAT)
            for b in range(2):
                dve.wait_ge(piece_used, N_WAT + 4)
                s = slice(b * BLK, (b + 1) * BLK)
                link(dve.tensor_tensor(proj[:, :, G1:G1 + D][:, :, s], bank_pair(b), proj[:, :, G1:G1 + D][:, :, s], ALU.mult))
            for t in range(TT):
                dve.tensor_tensor(proj[:, t, HG:HG + D], proj[:, t, HG:HG + D], proj[:, t, G1:G1 + D], ALU.add)\
                   .then_inc(src_ready, 1)
            lo(N_WOUT2)
            turn(T_WOUT2)
            two_blocks(N_WOUT2)
            residual(3)
            prenorm(4, T_FFN3)
            lo(N_FFN3)
            turn(T_FFN3)
            ffn(2, N_FFN3)
            residual(4)


def kernel(**inputs):
    import concourse.bacc as bacc
    from concourse.bass_utils import run_bass_kernel_spmd

    def of(name, *shape):
        return np.ascontiguousarray(np.asarray(inputs[name]).reshape(shape))

    const, lv, hot_np = constants()
    one = np.ones((P, 8), np.float32)

    def by_feature(name):
        return of(name, KT, P).T

    def of_head(name, times):
        return np.repeat(of(name, P, 1), times, axis=1)

    packed_cols = np.concatenate([
        by_feature("ffn1_pre_g"), by_feature("mix_pre_g"),
        one[:, 0:4], of_head("diff_subln_g", 4),
        by_feature("ffn2_pre_g"), by_feature("attn_norm_g_2"), of_head("hg_out_norm_g_2", 8), one, one,
        by_feature("ffn_norm_g_2"), of("q_norm_g_2", P, 1), of("k_norm_g_2", P, 1),
        of("hg_lb_gamma_2", 2, KT, P).transpose(2, 0, 1).reshape(P, 16)], axis=1)
    packed_rows = np.concatenate([
        of(n, 1, 64) for n in ("diff_lambda_q1", "diff_lambda_k1", "diff_lambda_q2", "diff_lambda_k2")
    ] + [of("fox_forget_b", 1, 8)], axis=1)

    arrays = {"x": of("x", S, D)}
    for f, names in enumerate((("ffn1_w_gate", "ffn1_w_up", "ffn1_w_down"),
                               ("ffn2_w_gate", "ffn2_w_up", "ffn2_w_down"),
                               ("w_ffn_gate_2", "w_ffn_up_2", "w_ffn_down_2"))):
        for what, name in zip(("gate", "up"), names):
            arrays[f"{what}{f}"] = of(name, D, D_FF)
        arrays[f"down{f}"] = of(names[2], D_FF, D)
    arrays["w_in"] = of("w_in", D, 3080)
    arrays["w_out"] = of("w_out", D, D)
    arrays["w_in_2"] = of("w_in_2", D, PROJ)
    for name in ("w_branch_hg_2", "w_branch_attn_2", "w_out_2"):
        arrays[name] = of(name, D, D)
    arrays["packed_cols"] = np.ascontiguousarray(packed_cols)
    arrays["packed_rows"] = np.ascontiguousarray(packed_rows)
    arrays["post_gains"] = np.concatenate([of(n, 1, D) for n in ("ffn1_post_g", "mix_post_g", "ffn2_post_g")], axis=0)
    arrays["rel_table"] = of("rel_bias_table_2", REL_BUCKETS, 8)
    arrays["const"] = const
    arrays["level_masks"] = lv.reshape(P, -1)
    arrays["one_hot"] = hot_np

    nc = bacc.Bacc("TRN2", target_bir_lowering=False, num_devices=1)
    d = {n: nc.dram_tensor("in_" + n, a.shape, mybir.dt.from_np(a.dtype), kind="ExternalInput").ap() for n, a in arrays.items()}
    out = nc.dram_tensor("out", (S, D), F32, kind="ExternalOutput").ap()
    skew = nc.dram_tensor("skew", (P * 8 * TOEP,), F32, kind="Internal").ap()
    build(nc, d["x"], [d[f"gate{f}"] for f in range(3)], [d[f"up{f}"] for f in range(3)],
          [d[f"down{f}"] for f in range(3)], d["w_in"], d["w_out"], d["w_in_2"], d["w_branch_hg_2"],
          d["w_branch_attn_2"], d["w_out_2"], d["packed_cols"], d["packed_rows"], d["post_gains"], d["rel_table"], d["const"],
          d["level_masks"], d["one_hot"], out, skew)
    r = run_bass_kernel_spmd(nc, [{"in_" + n: a for n, a in arrays.items()}], core_ids=[0])
    return r.results[0]["out"].reshape(1, S, D)
```

```python
from contextlib import ExitStack

import numpy as np

import concourse.bass as bass
from concourse import mybir

F32 = mybir.dt.float32
F32R = mybir.dt.float32r
BF16 = mybir.dt.bfloat16
U8 = mybir.dt.uint8
ALU = mybir.AluOpType
ACT = mybir.ActivationFunctionType
AX = mybir.AxisListType.X

P = 128
S = 256
TT = S // P
D = 1024
KT = D // P
D_FF = 2816
FC = 256
NC = D_FF // FC
BLK = 512
RING = 3
PIECE = 2048
EPS = 1e-6
LAM_INIT = 0.2
ROPE_THETA = 500000.0
REL_BUCKETS, REL_MAX_DIST = 32, 128
MASKED = -1e30
HG_SCALE = float(128) ** -0.5
FOX_SCALE = 0.125
MOBA_SCALE = float(128) ** -0.5
FOX_GATE = 1536
TOEP = 384

AUG = 64 + 2
FQ, FK, FV, DQ, DK, DV, MIX = 0, 8 * AUG, 16 * AUG, 16 * AUG + 512, 16 * AUG + 1024, 16 * AUG + 1536, 16 * AUG + 2048
HQ, HF, HI, HG, AQ, AK, AV, G0, G1 = (1024 * n for n in range(9))
PROJ = 9 * 1024

FFN_PIECES = 3 * NC
N_FFN1 = 0
N_WIN = N_FFN1 + FFN_PIECES
N_WOUT = N_WIN + 12
N_FFN2 = N_WOUT + 4
N_WIN2 = N_FFN2 + FFN_PIECES
N_WHG = N_WIN2 + 36
N_WAT = N_WHG + 4
N_WOUT2 = N_WAT + 4
N_FFN3 = N_WOUT2 + 4
N_END = N_FFN3 + FFN_PIECES

T_FFN1, T_WIN, T_WOUT, T_FFN2, T_WIN2, T_WHG, T_WAT, T_WOUT2, T_FFN3 = range(9)
TURN_AFTER = {T_WOUT: N_WOUT, T_WAT: N_WHG, T_WOUT2: N_WAT}
BY_TILE, BY_HALF = [(0, 0), (0, 1), (1, 0), (1, 1)], [(0, 0), (1, 0), (0, 1), (1, 1)]
FILLS = [BY_HALF if u in (T_WOUT, T_WOUT2) else BY_TILE for u in range(9)]

C_ID, C_TRI, C_ONES, C_MASK, C_COS, C_SIN = 0, 128, 256, 384, 512, 528
C_END = 544
HG_FIRST, HG_LEAD, MOBA_FIRST = 24, 4, 54
MOBA_Q_SQUARES = [42, 43]
BY_B, BY_J = [(0, 0), (0, 1), (1, 0), (1, 1)], [(0, 0), (1, 0), (0, 1), (1, 1)]
LEVELS = [1, 2, 4, 8, 16, 32, 64]
R_LAM, R_FB, R_END = 0, 256, 264
G_TURN, G_QG, G_KG, G_GAM, G_END = 0, 72, 73, 74, 90


def constants():
    c = np.zeros((P, C_END), np.float32)
    row, col = np.arange(P)[:, None], np.arange(P)[None, :]
    c[:, C_ID:C_ID + P] = row == col
    c[:, C_TRI:C_TRI + P] = row <= col
    c[:, C_ONES:C_ONES + P] = 1.0
    c[:, C_MASK:C_MASK + P] = np.where(col > row, MASKED, 0.0)
    inv = np.float32(ROPE_THETA) ** (-np.arange(0, 16, 2, dtype=np.float32) / np.float32(16))
    ang = np.arange(S, dtype=np.float32)[:, None] * inv[None, :].astype(np.float32)
    for t in range(TT):
        c[:, C_COS + 8 * t:C_COS + 8 * t + 8] = np.cos(ang[t * P:(t + 1) * P])
        c[:, C_SIN + 8 * t:C_SIN + 8 * t + 8] = np.sin(ang[t * P:(t + 1) * P])
    lv = np.zeros((P, len(LEVELS), P), np.float32)
    for n, m in enumerate(LEVELS):
        lv[:, n, :] = (row // (2 * m) == col // (2 * m)) & (row // m % 2 == 0) & (col // m % 2 == 1)
    dist = 255 - np.arange(S)
    exact = REL_BUCKETS // 2
    nf = np.maximum(dist, 1).astype(np.float32)
    large = exact + (np.log(nf / exact) / np.log(REL_MAX_DIST / exact) * (REL_BUCKETS - exact)).astype(np.int32)
    bucket = np.where(dist < exact, dist, np.minimum(large, REL_BUCKETS - 1))
    hot = (np.arange(REL_BUCKETS)[:, None] == bucket[None, :]).astype(np.float32)
    return c, lv, hot


def per(ap, m):
    n = ap.shape[1]
    return ap.rearrange("p (k o) -> p k o", o=1).to_broadcast([ap.shape[0], n, m])


def build(nc, x_d, wg_d, wu_d, wd_d, win_d, wout_d, win2_d, whg_d, wat_d, wout2_d,
          fixed_d, rows_d, post_d, rel_d, level_d, hot_d, out_d, row_d, skew_d):
    with ExitStack() as ctx:
        def sb(name, shape, dt=F32):
            return ctx.enter_context(nc.sbuf_tensor(name, shape, dt))

        def sem(name):
            return ctx.enter_context(nc.semaphore(name))

        x = sb("x", [P, TT, D])
        raw = sb("raw", [P, RING, PIECE])
        whi = sb("whi", [P, RING, PIECE], F32R)
        wlo = sb("wlo", [P, RING, PIECE], F32R)
        act_hi = sb("act_hi", [P, KT, S], F32R)
        act_lo = sb("act_lo", [P, KT, S], F32R)
        rows = sb("rows", [P, R_END])
        fixed = sb("fixed", [P, C_END + G_END])
        cst, cols = fixed[:, 0:C_END], fixed[:, C_END:C_END + G_END]
        level = sb("level", [P, len(LEVELS), P], U8)
        hot = sb("hot", [REL_BUCKETS, S])
        rel = sb("rel", [REL_BUCKETS, 8])
        id16 = sb("id16", [P, P], BF16)
        mask16 = sb("mask16", [P, P], BF16)
        xs = sb("xs", [P, TT, D])
        tmp = sb("tmp", [P, 2, BLK])
        junk = sb("junk", [P, D], BF16)
        post = sb("post", [P, D])
        with nc.sbuf_tensor("proj_rounded", [P, TT, PROJ], F32R) as proj_rounded:
            pass
        proj = sb("proj", [P, TT, PROJ])
        fgw = sb("fgw", [P, KT, 8])
        fgw_hi = sb("fgw_hi", [P, KT, 8], F32R)
        fgw_lo = sb("fgw_lo", [P, KT, 8], F32R)
        lf = sb("lf", [P, 5, TT, 8])
        lb = sb("lb", [P, 8, 8])
        lam = sb("lam", [P, 8])
        sums = sb("sums", [P, 60])
        ms = sb("ms", [P, 32])
        rstd = sb("rstd", [P, 60])
        mhalf = sb("mhalf", [P, 32])
        warm = sb("warm", [P, 3])
        mx = sb("mx", [P, 8])
        nmx = sb("nmx", [P, 8])
        den = sb("den", [P, 4])
        rden = sb("rden", [P, 12])
        with ExitStack() as ffn_part:
            sil, hid = (ffn_part.enter_context(nc.sbuf_tensor(n, [P, TT, FC], F32)) for n in ("sil", "hid"))
            hT_hi, hT_lo = (ffn_part.enter_context(nc.sbuf_tensor(n, [P, 2, S], F32R)) for n in ("hT_hi", "hT_lo"))
        with nc.sbuf_tensor("hg_attn", [P, 8, 3, P], F32) as attnT:
            pass
        q_sb = sb("att_q", [P, 2, S])
        k_sb = sb("att_k", [P, 2, S])
        e_sb = sb("att_e", [P, 2, 3 * P])
        pT_sb = sb("att_pT", [P, 2, 3 * P])
        dec_sb = sb("att_dec", [P, 2, 3 * P])
        qd_sb = dec_sb[:, :, :].rearrange("p a n -> p (a n)")[:, 0:2 * S].rearrange("p (a n) -> p a n", a=2)

        acc = ctx.enter_context(nc.psum_tensor("acc", [P, TT, 2, BLK], F32))
        gu = ctx.enter_context(nc.psum_tensor("gu", [P, TT, BLK], F32))
        tp = ctx.enter_context(nc.psum_tensor("tp", [P, 2, BLK], F32))

        def block_banks(g):
            b = g - 6
            if b < 6:
                return [gu, acc[:, 0, :, :], acc[:, 1, :, :], tp, acc[:, 0, :, :], tp][g] if b < 0 else \
                    [gu, acc[:, 0, :, :], acc[:, 1, :, :]][b % 3]
            return [gu, tp][b % 2] if b < 14 else [acc[:, 0, :, :], tp][b % 2]

        FORMER = {4: 1, 5: 3, 9: 6, 10: 7, 11: 8, 12: 9, 14: 12, 15: 13, 16: 14, 17: 15, 18: 16, 19: 17, 21: 19, 22: 20, 23: 21}

        def heads(ap, n):
            return ap.rearrange("p (h n) -> p h n", h=n)

        idn = cst[:, C_ID:C_ID + P]
        tri = cst[:, C_TRI:C_TRI + P]
        ones = cst[:, C_ONES:C_ONES + P]

        x_in = [sem(f"x_in{t}") for t in range(TT)]
        head_in, bias_parts_in, tail_in = sem("head_in"), sem("bias_parts_in"), sem("tail_in")
        raw_in = [sem(f"raw_in{s}") for s in range(RING)]
        hi_ready, lo_ready, piece_used = sem("hi_ready"), sem("lo_ready"), sem("piece_used")
        row_product, row_copied, row_padded = sem("row_product"), sem("row_copied"), sem("row_padded")
        row_out, rows_spread, bias_in, post_in = sem("row_out"), sem("rows_spread"), sem("bias_in"), sem("post_in")
        dve_setup, act_setup = sem("dve_setup"), sem("act_setup")
        src_ready, turn_full, turn_scaled = sem("src_ready"), sem("turn_full"), sem("turn_scaled")
        act_hi_ready, act_lo_ready = sem("act_hi_ready"), sem("act_lo_ready")
        row_sums, head_squares, head_sums = sem("row_sums"), sem("head_squares"), sem("head_sums")
        rstd_ready, pool_step, dve_step = sem("rstd_ready"), sem("pool_step"), sem("dve_step")
        sil_ready, h_ready, hT_full = sem("sil_ready"), sem("h_ready"), sem("hT_full")
        hT_hi_ready, hT_lo_ready = sem("hT_hi_ready"), sem("hT_lo_ready")
        acc_first, gu_first, x_ready = sem("acc_first"), sem("gu_first"), sem("x_ready")
        evac_a, evac_d = sem("evac_a"), sem("evac_d")
        gate_rows, gate_copied = sem("gate_rows"), sem("gate_copied")
        gate_product, gate_abs, gate_log = sem("gate_product"), sem("gate_abs"), sem("gate_log")
        log_f_ready, decay_sum, aug_ready, padded = (
            sem("log_f_ready"), sem("decay_sum"), sem("aug_ready"), sem("padded"))
        lb_in, lb_exp, lam_in, lam_exp = sem("lb_in"), sem("lb_exp"), sem("lam_in"), sem("lam_exp")
        roped, moba_normed = sem("roped"), sem("moba_normed")
        qkT_full, qT_ready, kT_ready = sem("qkT_full"), sem("qT_ready"), sem("kT_ready")
        scores_done, logits_ready = sem("scores_done"), sem("logits_ready")
        max_found, nmax_ready, exp_done = sem("max_found"), sem("nmax_ready"), sem("exp_done")
        rden_ready, lam_scaled, other_scaled = sem("rden_ready"), sem("lam_scaled"), sem("other_scaled")
        pT_full, pT_a, pT_d, pv_done, o_out = sem("pT_full"), sem("pT_a"), sem("pT_d"), sem("pv_done"), sem("o_out")
        hg_sig, hg_turned, hg_q_turned, hg_f, hg_q0 = (
            sem("hg_sig"), sem("hg_turned"), sem("hg_q_turned"), sem("hg_f"), sem("hg_q0"))
        hg_q, hg_k, hg_tot, hg_prod, hg_copied = (
            sem("hg_q"), sem("hg_k"), sem("hg_tot"), sem("hg_prod"), sem("hg_copied"))
        hg_cross, hg_o, hg_gate, hg_out = sem("hg_cross"), sem("hg_o"), sem("hg_gate"), sem("hg_out")
        merge_gates, merged = sem("merge_gates"), sem("merged")
        out_in = sem("out_in")

        block = ctx.enter_context(nc.Block())

        def landed(k, r):
            return 32 * (k // RING + 1) + 32 * r

        turned = acc[:, 1, :, :]

        def late(p):
            return (tp if p in (5, 7) else gu)[:, 0, :]

        def early(p):
            return (tp if p in (5, 7) else gu)[:, 1, 0:S]

        def o_bank(p):
            return acc[:, 0, p % 2, :] if 4 <= p < 8 else gu[:, 0, :]

        def laid(p, q0):
            behind = (3, 1, 2) if p < 4 else (4, 2, 2)
            q = q0 + 2 + sum(behind) * (p % 4)
            out = []
            for n in behind:
                out.append(list(range(q, q + n)))
                q += n
            if p % 4 == 3:
                out[2] = []
            return out

        def halves(quarters):
            return [q // 2 for q in quarters if q % 2]

        def logits(p):
            return dec_sb[:, :, :] if p % 2 else tmp[:, :, 0:3 * P]

        def win_place(b, t):
            if b < 2:
                return heads(proj[:, t, b * 8 * AUG:(b + 1) * 8 * AUG], 8)[:, :, 0:64]
            return proj[:, t, FV + (b - 2) * BLK:FV + (b - 1) * BLK]

        def fill_bank(u, i):
            if u == T_WOUT and i < 2:
                return acc[:, 0, i, :]
            return {T_WHG: acc[:, 1, :, :], T_WAT: gu, T_WOUT2: gu}.get(u, tp)[:, i % 2, :]

        def turned_place(u, t, h):
            if u in (T_WHG, T_WOUT2):
                return [heads(proj_rounded[:, t, col + h * BLK:col + (h + 1) * BLK], 4) for col in (HF, HG)]
            return [a[:, 4 * h:4 * h + 4, t * P:(t + 1) * P] for a in (act_hi, act_lo)]

        X_TURNS = [T_FFN1, T_WIN, T_FFN2, T_WIN2, T_FFN3]
        def last_hT(h, t):
            return h[:, 2 * t:2 * t + 2, P:2 * P]

        def turn_n(u):
            return 4 * u

        POST = 58
        norms = []
        for name in ("pre0", "post0", "pre1", "diff", "post1", "pre2", "post2", "pre3", "moba_q", "moba_k", "hg",
                     "pre4"):
            if name == "diff":
                norms.append((name, 0, 2, 8, 1 / 128))
            elif name in ("moba_q", "moba_k"):
                norms += [(name, t, (26 if name == "moba_q" else 42) + 8 * t, 8, 1 / 128) for t in range(TT)]
            else:
                norms += [(name, t, 10 + 8 * t, 8, 1 / 128) if name == "hg" else
                          (name, t, t + (POST if name[:4] == "post" else 0), 1, 1 / D) for t in range(TT)]

        def norm_n(name, t=0):
            return [(m, a) for m, a, *_ in norms].index((name, t)) + 1

        def row_n(name, t):
            return [(m, a) for m, a, *_ in norms if m[:2] == "pr" or m[:2] == "po"].index((name, t)) + 1

        def head_n(name, t=0):
            return [(m, a) for m, a, *_ in norms if m[:2] != "pr" and m[:2] != "po"].index((name, t)) + 1

        ACC_AFTER = [N_WIN, N_FFN2, N_WIN2, N_FFN3, N_END]

        def tot_of(n, t):
            if n == 0:
                return xs[:, t, :]
            if n == 1:
                return tmp[:, t, :]
            at = 512 - (1024 >> (n - 1))
            return post[:, t * 512 + at:t * 512 + at + (1024 >> n)]

        @block.sync
        def _(sp):
            def load(k, r, parts):
                if k >= RING:
                    sp.wait_ge(lo_ready, k - RING + 1 + 3 * r)
                for dst, src in parts:
                    sp.dma_start(dst, src).then_inc(raw_in[k % RING], 16)

            def gate_up(f, k, r, c, j):
                dst = raw[:, k % RING, :].rearrange("p (k n) -> p k n", k=4)
                load(k, r, [(dst[:, :, w * FC:(w + 1) * FC],
                             m.rearrange("(k p) n -> p k n", p=P)[:, 4 * j:4 * j + 4, bass.ds(c * FC, FC)])
                            for w, m in enumerate((wg_d[f], wu_d[f]))])

            def down(f, k, r, c):
                dst = raw[:, k % RING, :].rearrange("p (k n) -> p k n", k=2)
                load(k, r, [(dst[:, w, :], wd_d[f][bass.ds(c * FC + w * P, P), :]) for w in range(2)])

            def ffn(f, n0):
                for j in range(2):
                    if f == 0:
                        sp.dma_start(x[:, j, :], x_d[j * P:(j + 1) * P, :]).then_inc(x_in[j], 16)
                    gate_up(f, n0 + j, 0, 0, j)

                def step(k, c, r):
                    gate_up(f, k, r, c, 0)
                    gate_up(f, k + 1, r, c, 1)
                    down(f, k + 2, r, c - 1)

                step(n0 + 2, 1, 0)
                with sp.Fori(2, NC) as c:
                    step(n0 - 1 + 6, c, c - 2)
                down(f, n0 + 3 * NC - 1, 0, NC - 1)

            def wide(w, k, r, col, j):
                dst = raw[:, k % RING, :].rearrange("p (k n) -> p k n", k=4)
                src = w.rearrange("(k p) n -> p k n", p=P)
                load(k, r, [(dst[:, 2 * a:2 * a + 2, :], src[:, 4 * j + 2 * a:4 * j + 2 * a + 2, bass.ds(col, BLK)])
                            for a in range(2)])

            def two_blocks(w, n0, order):
                for n, (b, j) in enumerate(order):
                    wide(w, n0 + n, 0, b * BLK, j)

            def three_blocks(w, n0, i, group):
                for b in range(3):
                    for j in range(2):
                        wide(w, n0 + 2 * b + j, 2 * i, i * group + b * BLK, j)

            def post_gain(m):
                if m:
                    sp.wait_ge(x_ready, TT * m)
                else:
                    sp.wait_ge(dve_setup, 1)
                sp.dma_start(post[:, :], post_d[m:m + 1, :].to_broadcast([P, D])).then_inc(post_in, 16)

            ffn(0, N_FFN1)
            post_gain(0)
            with sp.Fori(0, 2) as i:
                three_blocks(win_d, N_WIN, i, 3 * BLK + 8)
            post_gain(1)
            two_blocks(wout_d, N_WOUT, BY_J)
            ffn(1, N_FFN2)
            post_gain(2)
            with sp.Fori(0, 6) as i:
                three_blocks(win2_d, N_WIN2, i, 3 * BLK)
            two_blocks(whg_d, N_WHG, BY_B)
            two_blocks(wat_d, N_WAT, BY_B)
            two_blocks(wout2_d, N_WOUT2, BY_J)
            ffn(2, N_FFN3)
            for t in range(TT):
                sp.wait_ge(x_ready, 4 * TT + t + 1)
                sp.dma_start(out_d[t * P:(t + 1) * P, :], x[:, t, :]).then_inc(out_in, 16)
            sp.wait_ge(out_in, 16 * TT)

        @block.tensor
        def _(pe):
            def three(out, hi, lo, w_hi, w_lo, start, stop):
                pe.matmul(out, hi, w_hi, start=start, stop=False)
                pe.matmul(out, hi, w_lo, start=False, stop=False)
                return pe.matmul(out, lo, w_hi, start=False, stop=stop)

            def half(k, r, banks, j, t, u=None, tiles=range(4)):
                if t == 0 and tiles[0] == 0:
                    pe.wait_ge(lo_ready, k + 1 + 3 * r)
                w_hi = whi[:, k % RING, :].rearrange("p (k n) -> p k n", k=4)
                w_lo = wlo[:, k % RING, :].rearrange("p (k n) -> p k n", k=4)
                for a in tiles:
                    f = 4 * j + a
                    hi, lo = (place[:, a, :] for place in turned_place(u, t, j))
                    mm = three(banks[:, t, :], hi, lo,
                               w_hi[:, a, :], w_lo[:, a, :], start=(f == 0), stop=(f == KT - 1))
                if t and tiles[-1] == 3:
                    mm.then_inc(piece_used, 1)
                return mm

            def wide(k, r, banks, j):
                half(k, r, banks, j, 0)
                half(k, r, banks, j, 1)

            def block_half(n0, g0, h, tiles=range(4)):
                g = g0 + h // 4
                if h % 4 == 0 and tiles[0] == 0 and g in FORMER:
                    pe.wait_ge(evac_a, FORMER[g] + 1)
                    pe.wait_ge(evac_d, FORMER[g] + 1)
                half(n0 + h // 2, 0, block_banks(g), h // 2 % 2, h % 2, tiles=tiles)

            def quarters(n0, g0, qs):
                for q in qs:
                    block_half(n0, g0, q // 2, range(2 * (q % 2), 2 * (q % 2) + 2))

            def fill(u, i, src):
                t, h = FILLS[u][i]
                f = turn_n(u) + i
                if f >= 2:
                    pe.wait_ge(turn_scaled, f - 1)
                for a in range(4):
                    mm = pe.transpose(fill_bank(u, i)[:, a * P:(a + 1) * P], src(t, 4 * h + a), idn)
                mm.then_inc(turn_full, 1)

            def fills(u, src, *which):
                for i in which:
                    fill(u, i, src)

            def filled(u, n):
                pe.wait_ge(act_lo_ready, turn_n(u) + n)

            def turn_x(u, t):
                if u == T_FFN1:
                    pe.wait_ge(x_in[t], 16)
                else:
                    pe.wait_ge(x_ready, TT * X_TURNS.index(u) - TT + t + 1)
                fills(u, lambda t, k: x[:, t, k * P:(k + 1) * P], 2 * t, 2 * t + 1)

            def start_block(u, n0, banks, meanwhile=lambda: None):
                turn_x(u, 0)
                meanwhile()
                filled(u, 1)
                half(n0, 0, banks, 0, 0)
                turn_x(u, 1)
                filled(u, 2)
                mm = half(n0 + 1, 0, banks, 1, 0)
                if u in (T_FFN1, T_FFN2, T_FFN3):
                    mm.then_inc(gu_first, 1)
                filled(u, 3)
                half(n0, 0, banks, 0, 1)
                filled(u, 4)
                half(n0 + 1, 0, banks, 1, 1)

            def from_proj(col):
                return lambda t, k: proj[:, t, col + k * P:col + (k + 1) * P]

            def ffn(f, n0):
                h0, h1 = 2 * f * NC, f * (NC + 1)

                def hidden_to(bank, c, tiles):
                    for a in range(2):
                        for t in tiles:
                            mm = pe.transpose(tp[:, bank, a * S + t * P:a * S + (t + 1) * P],
                                              hid[:, t, a * P:(a + 1) * P], idn)
                    mm.then_inc(hT_full, 1)

                def turn_hidden(c):
                    pe.wait_ge(h_ready, h0 + 2 + 2 * c)
                    hidden_to(0, c, range(TT))

                def down(k, r, hT, first, last, t):
                    if t == 0:
                        pe.wait_ge(lo_ready, k + 1 + 3 * r)
                    w_hi = whi[:, k % RING, :].rearrange("p (k n) -> p k n", k=2)
                    w_lo = wlo[:, k % RING, :].rearrange("p (k n) -> p k n", k=2)
                    for a in range(2):
                        for b in range(2):
                            mm = three(acc[:, t, b, :], *hT(a, t), w_hi[:, a, b * BLK:(b + 1) * BLK],
                                       w_lo[:, a, b * BLK:(b + 1) * BLK], start=first and a == 0,
                                       stop=last and a == 1)
                    if t:
                        mm.then_inc(piece_used, 1)
                    return mm

                def of_step(a, t):
                    return tuple(h[:, a, t * P:(t + 1) * P] for h in (hT_hi, hT_lo))

                def of_last(a, t):
                    return tuple(last_hT(h, t)[:, a, :] for h in (act_hi, act_lo))

                def gu_free(c, t):
                    pe.wait_ge(h_ready, h0 + 2 * c - 1 + t)

                def step(k, r, c, first):
                    for t in range(TT):
                        gu_free(c, t)
                        half(k, r, gu, 0, t)
                    turn_hidden(c - 1)
                    wide(k + 1, r, gu, 1)
                    pe.wait_ge(hT_lo_ready, h1 + c)
                    for t in range(TT):
                        down(k + 2, r, of_step, first, False, t)

                step(n0 + 2, 0, 1, True)
                with pe.Fori(2, NC - 1) as c:
                    step(n0 - 1 + 6, c - 2, c, False)
                k = n0 + 3 * NC - 4
                gu_free(NC - 1, 0)
                half(k, 0, gu, 0, 0)
                turn_hidden(NC - 2)
                half(k + 1, 0, gu, 1, 0).then_inc(gu_first, 1)
                gu_free(NC - 1, 1)
                half(k, 0, gu, 0, 1)
                half(k + 1, 0, gu, 1, 1)
                pe.wait_ge(hT_lo_ready, h1 + NC - 1)
                pe.wait_ge(h_ready, h0 + 2 * NC - 1)
                hidden_to(0, NC - 1, [0])
                down(k + 2, 0, of_step, False, False, 0)
                pe.wait_ge(h_ready, h0 + 2 * NC)
                hidden_to(1, NC - 1, [1])
                pe.wait_ge(hT_lo_ready, h1 + NC)
                down(k + 3, 0, of_last, False, True, 0).then_inc(acc_first, 1)
                down(k + 2, 0, of_step, False, False, 1)
                pe.wait_ge(hT_lo_ready, h1 + NC + 1)
                down(k + 3, 0, of_last, False, True, 1)

            def turn_qk(p):
                kind, i = divmod(p, 4)
                for n in range(2):
                    for h in range(1 if kind == 1 else 2):
                        for t in range(TT):
                            if kind == 0:
                                src = proj[:, t, ((FQ, FK)[n] + (2 * i + h) * AUG):((FQ, FK)[n] + (2 * i + h + 1) * AUG)]
                            else:
                                col = (DQ, DK)[n] + i * P if kind == 1 else (AQ, AK)[n] + i * S + h * P
                                src = proj[:, t, col:col + P]
                            mm = pe.transpose(turned[0:src.shape[1], n, h * S + t * P:h * S + (t + 1) * P], src, idn)
                mm.then_inc(qkT_full, 1)

            def scores(p):
                kind = p // 4
                pe.wait_ge(qT_ready, p + 1)
                pe.wait_ge(kT_ready, p + 1)
                if p in (1, 2, 3, 4, 9, 10, 11):
                    pe.wait_ge(o_out, p)
                rows_used = AUG if kind == 0 else P
                for h in range(2):
                    q = (qd_sb if kind == 1 else q_sb)[0:rows_used, h, :]
                    k = k_sb[0:rows_used, 0 if kind == 1 else h, :]
                    lt, el = late(p)[:, h * S:(h + 1) * S], early(p)[:, h * P:(h + 1) * P]
                    mm = pe.matmul(lt, q[:, P:S], k, start=True, stop=kind == 2)
                    if kind < 2:
                        mm = pe.matmul(lt[:, P:S], id16[:, :], mask16[:, :], start=False, stop=True)
                    mm = pe.matmul(el, q[:, 0:P], k[:, 0:P], start=True, stop=kind == 2)
                    if kind < 2:
                        mm = pe.matmul(el, id16[:, :], mask16[:, :], start=False, stop=True)
                mm.then_inc(scores_done, 1)

            def turn_weights(p):
                pe.wait_ge(exp_done, p + 1)
                for h in range(2):
                    for n in range(3):
                        mm = pe.transpose(turned[:, h, n * P:(n + 1) * P], e_sb[:, h, n * P:(n + 1) * P], idn)
                mm.then_inc(pT_full, 1)

            def values(p):
                kind, i = divmod(p, 4)
                if p >= 2:
                    pe.wait_ge(o_out, p - 1)
                if p == 4:
                    pe.wait_ge(turn_scaled, turn_n(T_WOUT) + 2)
                for h in range(2):
                    wid = 64 if kind == 0 else P
                    col = (FV + i * P + 64 * h, DV + i * P, AV + i * S + h * P)[kind]
                    v = [proj[:, t, col:col + wid] for t in range(TT)]
                    o = [o_bank(p)[:, (2 * h + t) * P:(2 * h + t) * P + wid] for t in range(TT)]
                    pe.matmul(o[1], pT_sb[:, h, 0:P], v[0], start=True, stop=False)
                    pe.matmul(o[1], pT_sb[:, h, P:2 * P], v[1], start=False, stop=True)
                    mm = pe.matmul(o[0], pT_sb[:, h, 2 * P:3 * P], v[0], start=True, stop=True)
                mm.then_inc(pv_done, 1)

            def weights_read(p):
                pe.wait_ge(pT_a, p + 1)
                pe.wait_ge(pT_d, p + 1)

            def attention(p0, p1, meanwhile):
                turn_qk(p0)
                scores(p0)
                turn_qk(p0 + 1)
                meanwhile()
                for p in range(p0, p1):
                    if p + 1 < p1:
                        scores(p + 1)
                    turn_weights(p)
                    weights_read(p)
                    if p + 2 < p1:
                        turn_qk(p + 2)
                    values(p)

            def q_at(t, h):
                return proj[:, t, HQ + h * P:HQ + (h + 1) * P]

            def k_at(t, h):
                return proj[:, t, HF + h * P:HF + (h + 1) * P]

            def hg_turn_sig(t):
                pe.wait_ge(hg_sig, t + 1)
                if t:
                    pe.wait_ge(hg_q0, t)
                    pe.wait_ge(hg_k, t)
                for n, src in enumerate((xs[:, t, :], proj[:, t, HF:HF + D])):
                    for h in range(8):
                        mm = pe.transpose(acc[:, n, h // 4, h % 4 * P:(h % 4 + 1) * P], src[:, h * P:(h + 1) * P], idn)
                mm.then_inc(hg_turned, 1)

            def hg_turn_q(t):
                pe.wait_ge(hg_f, t + 1)
                for h in range(8):
                    mm = pe.transpose(acc[:, 0, h // 4, h % 4 * P:(h % 4 + 1) * P], q_at(t, h), idn)
                mm.then_inc(hg_q_turned, 1)

            def hg_level(n, t):
                if n == 0:
                    pe.wait_ge(hg_q0, TT)
                    pe.wait_ge(hg_k, TT)
                else:
                    pe.wait_ge(hg_q, TT * (n - 1) + t + 1)
                    if n > 1:
                        pe.wait_ge(hg_k, TT * (n - 1) + t + 1)
                    pe.wait_ge(hg_copied, TT * (n - 1) + t + 1)
                for h in range(8):
                    mm = pe.matmul(acc[:, t, h // 4, h % 4 * P:(h % 4 + 1) * P], k_at(t, h), q_at(t, h),
                                   start=True, stop=True)
                mm.then_inc(hg_prod, 1)

            def hg_across():
                n = len(LEVELS)
                pe.wait_ge(hg_q, TT * n + 1)
                pe.wait_ge(hg_k, TT * n + 1)
                pe.wait_ge(hg_copied, TT * n + 1)
                for h in range(8):
                    mm = pe.matmul(acc[:, 0, h // 4, h % 4 * P:(h % 4 + 1) * P], k_at(0, h), q_at(1, h),
                                   start=True, stop=True)
                mm.then_inc(hg_prod, 1)

            def hg_values(t):
                pe.wait_ge(hg_copied, TT * len(LEVELS) + t + 1)
                pe.wait_ge(hg_cross, 1)
                for h in range(8):
                    v = [proj[:, a, HI + h * P:HI + (h + 1) * P] for a in range(TT)]
                    o = acc[:, t, h // 4, h % 4 * P:(h % 4 + 1) * P]
                    if t:
                        pe.matmul(o, attnT[:, h, 1, :], v[0], start=True, stop=False)
                    mm = pe.matmul(o, attnT[:, h, 2 if t else 0, :], v[t], start=not t, stop=True)
                mm.then_inc(hg_o, 1)

            def attention_between(p0, n0, g0, h0):
                turn_qk(p0)
                block_half(n0, g0, h0)
                for p in range(p0, p0 + 4):
                    here = laid(p, 2 * h0)
                    scores(p)
                    quarters(n0, g0, here[0])
                    turn_weights(p)
                    quarters(n0, g0, here[1])
                    weights_read(p)
                    if p < p0 + 3:
                        turn_qk(p + 1)
                    values(p)
                    quarters(n0, g0, here[2])

            pe.wait_ge(head_in, 16)

            def bias_rows():
                pe.wait_ge(bias_parts_in, 16 * 2)
                pe.matmul(acc[0:8, 0, 0, 0:S], rel[:, :], hot[:, :], start=True, stop=True).then_inc(row_product, 1)

            start_block(T_FFN1, N_FFN1, gu, bias_rows)
            ffn(0, N_FFN1)
            start_block(T_WIN, N_WIN, block_banks(0))
            pe.wait_ge(dve_setup, 1)
            for f in range(KT):
                hi, lo = act_hi[:, f, :], act_lo[:, f, :]
                pe.matmul(tp[0:8, 0, 0:S], fgw_hi[:, f, :], hi, start=f == 0, stop=False)
                pe.matmul(tp[0:8, 0, 0:S], fgw_lo[:, f, :], hi, start=False, stop=False)
                mm = pe.matmul(tp[0:8, 0, 0:S], fgw_hi[:, f, :], lo, start=False, stop=f == KT - 1)
            mm.then_inc(gate_rows, 1)
            block_half(N_WIN, 0, 4)
            pe.wait_ge(gate_copied, 1)
            for t in range(TT):
                mm = pe.transpose(tp[:, 0, 8 * t:8 * t + 8], tmp[0:8, 1, t * P:(t + 1) * P], idn[0:8, 0:8])
            mm.then_inc(gate_product, 1)
            for a in range(1, 4):
                block_half(N_WIN, 0, 4 + a)
            pe.wait_ge(log_f_ready, 1)
            f = [lf[:, 4, t, :] for t in range(TT)]
            pe.matmul(tp[:, 1, 0:8], tri, f[0], start=True, stop=True)
            pe.matmul(tp[:, 1, 8:16], ones, f[0], start=True, stop=False)
            pe.matmul(tp[:, 1, 8:16], tri, f[1], start=False, stop=True).then_inc(decay_sum, 1)
            for a in range(4):
                block_half(N_WIN, 0, 8 + a)
            pe.wait_ge(aug_ready, 1)
            pe.wait_ge(evac_a, 3)
            pe.wait_ge(evac_d, 3)
            attention_between(0, N_WIN, 0, 12)
            pe.wait_ge(evac_a, 6)
            pe.wait_ge(evac_d, 6)
            pe.wait_ge(roped, 1)

            def turn_fox():
                pe.wait_ge(o_out, 4)
                fills(T_WOUT, from_proj(MIX), 0, 1)

            attention(4, 8, turn_fox)
            filled(T_WOUT, 2)
            for b in range(2):
                for t in range(TT):
                    if b == 1 and t == 0:
                        pe.wait_ge(o_out, 8)
                    if b == 1 and t == 1:
                        pe.wait_ge(src_ready, TT)
                        fills(T_WOUT, from_proj(MIX), 2, 3)
                    half(N_WOUT + b, 0, acc[:, :, b, :], 0, t)
            filled(T_WOUT, 4)
            for t in range(TT):
                for b in range(2):
                    mm = half(N_WOUT + 2 + b, 0, acc[:, :, b, :], 1, t)
                if t == 0:
                    mm.then_inc(acc_first, 1)
            start_block(T_FFN2, N_FFN2, gu)
            ffn(1, N_FFN2)
            start_block(T_WIN2, N_WIN2, block_banks(6))
            for h in range(4, HG_FIRST):
                block_half(N_WIN2, 6, h)
            h = HG_FIRST
            for _ in range(HG_LEAD):
                block_half(N_WIN2, 6, h)
                h += 1
            pe.wait_ge(evac_a, 12)
            pe.wait_ge(evac_d, 12)
            for t in range(TT):
                hg_turn_sig(t)
                block_half(N_WIN2, 6, h)
                hg_turn_q(t)
                block_half(N_WIN2, 6, h + 1)
                h += 2
            for n in range(len(LEVELS) + 1):
                for t in range(TT):
                    hg_level(n, t)
                    block_half(N_WIN2, 6, h)
                    h += 1
            hg_across()
            block_half(N_WIN2, 6, h)
            hg_values(0)
            block_half(N_WIN2, 6, h + 1)
            hg_values(1)
            for h in range(h + 2, MOBA_FIRST):
                block_half(N_WIN2, 6, h)
            pe.wait_ge(hg_out, TT)
            pe.wait_ge(moba_normed, 2)
            attention_between(8, N_WIN2, 6, MOBA_FIRST)
            for t in range(TT):
                pe.wait_ge(src_ready, TT + t + 1)
                fills(T_WHG, from_proj(HQ), 2 * t, 2 * t + 1)
                block_half(N_WIN2, 6, 70 + t)
            pe.wait_ge(evac_a, 23)
            pe.wait_ge(evac_d, 23)
            filled(T_WHG, 2)
            for t in range(TT):
                if t:
                    filled(T_WHG, 4)
                for j in range(2):
                    half(N_WHG + j, 0, acc[:, :, 0, :], j, t, T_WHG)
            for j in range(2):
                for t in range(TT):
                    half(N_WHG + 2 + j, 0, acc[:, :, 1, :], j, t, T_WHG)
                    if (j, t) == (0, 1):
                        pe.wait_ge(o_out, 12)
                        fills(T_WAT, from_proj(AQ), 0, 1)
                    elif (j, t) == (1, 0):
                        fills(T_WAT, from_proj(AQ), 2, 3)
            filled(T_WAT, 4)
            for j in range(2):
                for t in range(TT):
                    half(N_WAT + j, 0, gu, j, t)
            pe.wait_ge(evac_a, 24)
            pe.wait_ge(evac_d, 24)
            for j in range(2):
                for t in range(TT):
                    if j and not t:
                        pe.wait_ge(src_ready, 2 * TT + 1)
                        fills(T_WOUT2, from_proj(HI), 0, 1)
                    half(N_WAT + 2 + j, 0, tp, j, t)
            pe.wait_ge(merged, 2 * TT)
            filled(T_WOUT2, 2)
            for b in range(2):
                for t in range(TT):
                    half(N_WOUT2 + b, 0, acc[:, :, b, :], 0, t, T_WOUT2)
                    if b == 0 and t == 1:
                        pe.wait_ge(src_ready, 2 * TT + 2)
                        fills(T_WOUT2, from_proj(HI), 2, 3)
            filled(T_WOUT2, 4)
            for t in range(TT):
                for b in range(2):
                    mm = half(N_WOUT2 + 2 + b, 0, acc[:, :, b, :], 1, t, T_WOUT2)
                if t == 0:
                    mm.then_inc(acc_first, 1)
            start_block(T_FFN3, N_FFN3, gu)
            ffn(2, N_FFN3)

        @block.scalar
        def _(act):
            def hi(k, r=0):
                act.wait_ge(raw_in[k % RING], landed(k, r))
                if k >= RING:
                    act.wait_ge(piece_used, k - RING + 1 + 3 * r)
                act.activation(whi[:, k % RING, :], raw[:, k % RING, :], ACT.Copy).then_inc(hi_ready, 1)

            def fills(u, *which):
                if u in TURN_AFTER:
                    act.wait_ge(piece_used, TURN_AFTER[u])
                for i in which:
                    f = turn_n(u) + i
                    act.wait_ge(turn_scaled, f + 1)
                    act.activation(turned_place(u, *FILLS[u][i])[0], heads(tmp[:, f % 2, :], 4), ACT.Copy)\
                       .then_inc(act_hi_ready, 1)

            def x_sums(m, t):
                if m:
                    act.wait_ge(x_ready, TT * (m - 1) + t + 1)
                else:
                    act.wait_ge(x_in[t], 16)
                if m or t:
                    act.wait_ge(row_sums, row_n(f"pre{m}", t) - 1)
                act.activation(junk[:, :], x[:, t, :], ACT.Square, accum_out=sums[:, t:t + 1]).then_inc(row_sums, 1)

            def acc_ready(j, t):
                if t == 0:
                    act.wait_ge(acc_first, j + 1)
                else:
                    act.wait_ge(piece_used, ACC_AFTER[j])

            def acc_sums(m, t):
                acc_ready(m, t)
                act.wait_ge(row_sums, row_n(f"post{m}", t) - 1)
                act.activation(junk[:, :], acc[:, t, :, :].rearrange("p b n -> p (b n)"), ACT.Square,
                               accum_out=sums[:, POST + t:POST + t + 1]).then_inc(row_sums, 1)

            def norms_between(m, u, n1):
                if m in (0, 1, 2):
                    acc_sums(m, 0)
                hi(n1 + 1)
                if m in (0, 1, 2):
                    acc_sums(m, 1)
                fills(u, 0, 1)
                x_sums(m + 1, 0)
                hi(n1 + 2)
                fills(u, 2, 3)
                x_sums(m + 1, 1)

            def ffn(f, n0):
                h0, h1 = 2 * f * NC, f * (NC + 1)

                def silu(c, t):
                    if f or not isinstance(c, int) or c:
                        act.wait_ge(h_ready, h0 + 2 * c - 1 + t)
                    act.activation(sil[:, t, :], gu[:, t, 0:FC], ACT.Silu, scale=rstd[:, t:t + 1]).then_inc(sil_ready, 1)

                def edge_silu(k, c, t):
                    if t == 0:
                        act.wait_ge(gu_first, 2 * f + (2 if c else 1))
                    else:
                        act.wait_ge(piece_used, k + 1)
                    silu(c, t)

                def both(k, r, c):
                    act.wait_ge(piece_used, k + 1 + 3 * r)
                    for t in range(TT):
                        silu(c, t)

                def hidden(k, r, c):
                    act.wait_ge(hT_full, h1 + 1 + c)
                    if k:
                        act.wait_ge(piece_used, k + 1 + 3 * r)
                    act.activation(hT_hi[:, :, :], tp[:, 0, :].rearrange("p (a n) -> p a n", a=2), ACT.Copy)\
                       .then_inc(hT_hi_ready, 1)

                act.wait_ge(rstd_ready, norm_n(f"pre{2 * f}", 0))
                edge_silu(n0 + 1, 0, 0)
                hi(n0 + 3)
                act.wait_ge(rstd_ready, norm_n(f"pre{2 * f}", 1))
                edge_silu(n0 + 1, 0, 1)
                hi(n0 + 4)
                hidden(0, 0, 0)
                hi(n0 + 5)
                both(n0 + 3, 0, 1)
                hi(n0 + 6)
                hi(n0 + 7)
                with act.Fori(2, NC - 1) as c:
                    hidden(n0 + 4, c - 2, c - 1)
                    hi(n0 + 8, c - 2)
                    both(n0 + 6, c - 2, c)
                    hi(n0 + 9, c - 2)
                    hi(n0 + 10, c - 2)
                last = n0 + 3 * NC - 1
                hidden(last - 4, 0, NC - 2)
                edge_silu(last - 2, NC - 1, 0)
                hi(last)
                edge_silu(last - 2, NC - 1, 1)
                for t in range(TT):
                    act.wait_ge(hT_full, h1 + NC + t)
                    act.activation(last_hT(act_hi, t), heads(tp[:, t, :], 2)[:, :, t * P:(t + 1) * P], ACT.Copy)\
                       .then_inc(hT_hi_ready, 1)

            def evac(g, used, dst):
                act.wait_ge(piece_used, used)
                src = block_banks(g)[:, 0, :]
                act.activation(dst, heads(src, 8) if len(dst.shape) == 3 else src, ACT.Copy, scale=rstd[:, 0:1])\
                   .then_inc(evac_a, 1)

            def block_out(n0, g0, h):
                j = h // 2
                if h % 2 and j % 2:
                    b = j // 2
                    evac(g0 + b, n0 + j + 1, win_place(b, 0) if g0 == 0 else proj[:, 0, b * BLK:(b + 1) * BLK])

            def next_hi(n0, g0, h):
                if h % 2:
                    hi(n0 + h // 2 + RING)

            def after(n0, g0, h):
                block_out(n0, g0, h)
                next_hi(n0, g0, h)

            def q_out(p):
                act.wait_ge(qkT_full, p + 1)
                if p // 4 == 1:
                    act.activation(qd_sb[0:64, 0, :], turned[0:64, 0, 0:S], ACT.Copy, scale=FOX_SCALE)
                    act.activation(qd_sb[64:P, 1, :], turned[64:P, 0, 0:S], ACT.Copy, scale=FOX_SCALE).then_inc(qT_ready, 1)
                else:
                    r = AUG if p < 4 else P
                    act.activation(q_sb[0:r, :, :], heads(turned[0:r, 0, :], 2), ACT.Copy,
                                   scale=FOX_SCALE if p < 4 else cols[:, G_QG:G_QG + 1]).then_inc(qT_ready, 1)

            def exps(p):
                act.wait_ge(nmax_ready, p + 1)
                if p:
                    act.wait_ge(pT_full, p)
                    act.wait_ge(rden_ready, p)
                src = logits(p)
                for h in range(2):
                    lt = late(p)[:, h * S:(h + 1) * S] if p < 8 else src[:, h, 0:S]
                    el = early(p)[:, h * P:(h + 1) * P] if p < 8 else src[:, h, S:3 * P]
                    n = 4 * (p % 2)
                    act.activation(e_sb[:, h, 0:S], lt, ACT.Exp, bias=nmx[:, n + h:n + h + 1], accum_out=den[:, h:h + 1])
                    last = act.activation(e_sb[:, h, S:3 * P], el, ACT.Exp, bias=nmx[:, n + 2 + h:n + 3 + h],
                                          accum_out=den[:, 2 + h:3 + h])
                last.then_inc(exp_done, 1)

            def weights_out(p):
                act.wait_ge(pT_full, p + 1)
                if p:
                    act.wait_ge(pv_done, p)
                act.activation(pT_sb[:, 0, :], turned[:, 0, 0:3 * P], ACT.Copy).then_inc(pT_a, 1)

            def attention(p0, p1, meanwhile):
                q_out(p0)
                q_out(p0 + 1)
                exps(p0)
                meanwhile()
                for p in range(p0, p1):
                    weights_out(p)
                    if p + 2 < p1:
                        q_out(p + 2)
                    if p + 1 < p1:
                        exps(p + 1)

            def attention_between(p0, n0, g0, h0):
                block_out(n0, g0, h0 - 1)
                q_out(p0)
                next_hi(n0, g0, h0 - 1)
                for p in range(p0, p0 + 4):
                    here = [halves(q) for q in laid(p, 2 * h0)]
                    exps(p)
                    for h in here[0][:-1]:
                        after(n0, g0, h)
                    block_out(n0, g0, here[0][-1])
                    weights_out(p)
                    next_hi(n0, g0, here[0][-1])
                    for h in here[1]:
                        block_out(n0, g0, h)
                        if p < p0 + 3:
                            next_hi(n0, g0, h)
                    if p < p0 + 3:
                        q_out(p + 1)
                    for h in here[2]:
                        after(n0, g0, h)
                return here[1]

            def load_table(n, function):
                act.activation(warm[:, n:n + 1], mhalf[:, 0:1], function)

            act.dma_start(fixed[:, :], fixed_d).then_inc(head_in, 16)
            act.wait_ge(pool_step, 1)
            load_table(0, ACT.Silu)
            x_sums(0, 0)
            fills(T_FFN1, 0, 1)
            hi(0)
            hi(1)
            x_sums(0, 1)
            fills(T_FFN1, 2, 3)
            hi(2)
            act.wait_ge(row_product, 1)
            act.activation(proj[0:8, 0, 0:S], acc[0:8, 0, 0, 0:S], ACT.Copy).then_inc(row_copied, 1)
            act.wait_ge(row_copied, 1)
            act.wait_ge(row_padded, 1)
            act.dma_start(row_d, proj[0:8, 0, 0:TOEP]).then_inc(row_out, 16)
            act.wait_ge(tail_in, 16 * 3)
            act.activation(fgw_hi[:, :, :], fgw[:, :, :], ACT.Copy).then_inc(act_setup, 1)
            ffn(0, N_FFN1)
            act.wait_ge(row_out, 16)
            act.dma_start(skew_d.rearrange("(p h n) -> p h n", p=P, h=8),
                          row_d.rearrange("(o h) n -> o h n", o=1).to_broadcast([P, 8, TOEP])).then_inc(rows_spread, 16)
            hi(N_WIN)
            norms_between(0, T_WIN, N_WIN)
            act.wait_ge(rstd_ready, norm_n("pre1", 0))
            for h in range(4):
                after(N_WIN, 0, h)
            act.wait_ge(lb_in, 1)
            act.activation(lb[:, 3:5, :], lb[:, 1:3, :], ACT.Exp).then_inc(lb_exp, 1)
            act.wait_ge(lam_in, 1)
            act.activation(lam[:, 2:4], lam[:, 0:2], ACT.Exp).then_inc(lam_exp, 1)
            act.wait_ge(gate_abs, 1)
            act.activation(lf[:, 2, :, :], lf[:, 1, :, :], ACT.Exp, scale=-1.0).then_inc(gate_log, 1)
            act.wait_ge(gate_log, 1)
            act.activation(lf[:, 3, :, :], lf[:, 2, :, :], ACT.Ln, bias=1.0).then_inc(gate_log, 1)
            load_table(1, ACT.Exp)
            for h in range(4, 11):
                after(N_WIN, 0, h)
            left = attention_between(0, N_WIN, 0, 12)

            def meanwhile():
                fills(T_WOUT, 0, 1)
                for h in left:
                    next_hi(N_WIN, 0, h)

            act.wait_ge(padded, 1)
            attention(4, 8, meanwhile)
            act.wait_ge(o_out, 8)
            act.activation(xs[:, :, 0:BLK], proj[:, :, MIX + BLK:MIX + 2 * BLK], ACT.Square).then_inc(head_squares, 1)
            fills(T_WOUT, 2, 3)
            hi(N_WOUT + 3)
            hi(N_FFN2)
            norms_between(1, T_FFN2, N_FFN2)
            ffn(1, N_FFN2)
            hi(N_WIN2)
            norms_between(2, T_WIN2, N_WIN2)
            act.wait_ge(rstd_ready, norm_n("pre3", 0))
            with act.Fori(0, 2) as i:
                for b in range(3):
                    hi(N_WIN2 + 3 + 2 * b, 2 * i)
                    evac(6 + b, N_WIN2 + 2 + 2 * b + 6 * i, proj[:, 0, bass.ds(b * BLK + i * (3 * BLK), BLK)])
                    hi(N_WIN2 + 4 + 2 * b, 2 * i)
            h = HG_FIRST
            act.wait_ge(evac_d, 12)
            act.wait_ge(evac_a, 12)
            for t in range(TT):
                act.activation(xs[:, t, :], proj[:, t, HF:HF + D], ACT.Sigmoid)
                act.activation(proj[:, t, HF:HF + D], proj[:, t, HF:HF + D], ACT.Sigmoid, scale=-1.0)
                act.activation(proj[:, t, HQ:HQ + D], proj[:, t, HQ:HQ + D], ACT.Copy, scale=HG_SCALE).then_inc(hg_sig, 1)
                for _ in range(HG_LEAD // 2):
                    after(N_WIN2, 6, h)
                    h += 1
            for t in range(TT):
                after(N_WIN2, 6, h)
                act.wait_ge(hg_q_turned, t + 1)
                act.activation(proj[:, t, HQ:HQ + D], acc[:, 0, :, :].rearrange("p b n -> p (b n)"), ACT.Copy)\
                   .then_inc(hg_q0, 1)
                after(N_WIN2, 6, h + 1)
                h += 2
            n = TT * (len(LEVELS) + 1)
            for _ in range(n):
                after(N_WIN2, 6, h)
                if h in MOBA_Q_SQUARES:
                    t = MOBA_Q_SQUARES.index(h)
                    act.wait_ge(hg_k, 2 * TT)
                    act.wait_ge(hg_tot, 2 * TT)
                    act.wait_ge(evac_a, 16)
                    act.wait_ge(evac_d, 16)
                    act.activation(xs[:, t, :], proj[:, t, AQ:AQ + D], ACT.Square).then_inc(head_squares, 1)
                h += 1
            act.wait_ge(evac_a, 18)
            act.wait_ge(evac_d, 18)
            for t in range(TT):
                act.wait_ge(head_sums, head_n("moba_q", t))
                act.activation(xs[:, t, :], proj[:, t, AK:AK + D], ACT.Square).then_inc(head_squares, 1)
            act.wait_ge(hg_prod, n + 1)
            act.activation(attnT[:, :, 1, :], heads(acc[:, 0, :, :].rearrange("p b n -> p (b n)"), 8), ACT.Copy)\
               .then_inc(hg_cross, 1)
            after(N_WIN2, 6, h)
            for t in range(TT):
                act.wait_ge(hg_o, t + 1)
                act.wait_ge(head_sums, head_n("moba_k", t))
                act.activation(xs[:, t, :], acc[:, t, :, :].rearrange("p b n -> p (b n)"), ACT.Square)\
                   .then_inc(head_squares, 1)
                after(N_WIN2, 6, h + 1 + t)
            for t in range(TT):
                after(N_WIN2, 6, h + 3 + t)
                act.activation(proj[:, t, HF:HF + D], proj[:, t, HG:HG + D], ACT.Sigmoid).then_inc(hg_gate, 1)
            load_table(2, ACT.Exp)
            for h in range(h + 5, MOBA_FIRST - 1):
                after(N_WIN2, 6, h)
            left = attention_between(8, N_WIN2, 6, MOBA_FIRST)
            for h in left:
                next_hi(N_WIN2, 6, h)
            fills(T_WHG, 0, 1)
            fills(T_WHG, 2, 3)
            after(N_WIN2, 6, 71)
            act.wait_ge(evac_d, 24)
            act.wait_ge(evac_a, 24)
            for t in range(TT):
                act.activation(proj[:, t, G0:G0 + 2 * D], proj[:, t, G0:G0 + 2 * D], ACT.Sigmoid).then_inc(merge_gates, 1)
            hi(N_WHG + 3)
            hi(N_WAT)
            fills(T_WAT, 0, 1, 2, 3)
            for k in range(4):
                hi(N_WAT + 1 + k)
            fills(T_WOUT2, 0, 1)
            hi(N_WOUT2 + 1)
            hi(N_WOUT2 + 2)
            fills(T_WOUT2, 2, 3)
            hi(N_WOUT2 + 3)
            hi(N_FFN3)
            norms_between(3, T_FFN3, N_FFN3)
            ffn(2, N_FFN3)

        @block.gpsimd
        def _(pool):
            steps = [0]

            def link(ins):
                steps[0] += 1
                ins.then_inc(pool_step, 1)
                pool.wait_ge(pool_step, steps[0])

            def norm(name, tile=None):
                for m, t, col, n, inv in norms:
                    if m != name or tile not in (None, t):
                        continue
                    if name[:2] in ("pr", "po"):
                        pool.wait_ge(row_sums, row_n(name, t))
                    else:
                        pool.wait_ge(head_sums, head_n(name, t))
                    link(pool.tensor_scalar(ms[:, 0:n], sums[:, col:col + n], inv, EPS, ALU.mult, ALU.add))
                    pool.tensor_tensor(rstd[:, col:col + n], ms[:, 0:n], mhalf[:, 0:n], ALU.pow).then_inc(rstd_ready, 1)
                    pool.wait_ge(rstd_ready, norm_n(name, t))

            def rest_of(k, b):
                pool.wait_ge(hi_ready, k + 1)
                s = slice(b * PIECE // 2, (b + 1) * PIECE // 2)
                ins = pool.tensor_tensor(wlo[:, k % RING, s], raw[:, k % RING, s], whi[:, k % RING, s].bitcast(F32),
                                         ALU.subtract)
                if b:
                    ins.then_inc(lo_ready, 1)
                else:
                    link(ins)

            def norms_between(m, n1):
                if m < 3:
                    norm(f"post{m}", 0)
                pool.wait_ge(lo_ready, n1 + 1)
                rest_of(n1 + 1, 0)
                if m < 3:
                    norm(f"post{m}", 1)
                rest_of(n1 + 1, 1)
                norm(f"pre{m + 1}")

            link(pool.memset(mhalf[:, :], -0.5))
            for dst, src in ((hot[:, :], hot_d), (rel[:, :], rel_d)):
                pool.dma_start(dst, src).then_inc(bias_parts_in, 16)
            with nc.allow_non_contiguous_dma(reason="eight columns"):
                pool.dma_start(fgw[:, :, :], win_d.rearrange("(k p) n -> p k n", p=P)[:, :, FOX_GATE:FOX_GATE + 8])\
                    .then_inc(tail_in, 16)
            pool.dma_start(rows[:, :], rows_d.to_broadcast([P, R_END])).then_inc(tail_in, 16)
            pool.dma_start(post[:, 0:len(LEVELS) * P], level_d).then_inc(tail_in, 16)
            norm("pre0")
            norms_between(0, N_WIN)
            pool.wait_ge(evac_a, 5)
            pool.wait_ge(evac_d, 5)
            for t in range(TT):
                qk = proj[:, t, DQ:DQ + D].rearrange("p (g n) -> p g n", g=16)
                x1, x2 = qk[:, :, 0:8], qk[:, :, 8:16]
                c, s = (cst[:, C + 8 * t:C + 8 * t + 8].rearrange("p (o n) -> p o n", o=1).to_broadcast([P, 16, 8])
                        for C in (C_COS, C_SIN))
                part = [tmp[:, 1, n * P:(n + 1) * P].rearrange("p (g n) -> p g n", g=16) for n in range(4)]
                pool.tensor_tensor(part[0], x1, c, ALU.mult)
                pool.tensor_tensor(part[1], x2, s, ALU.mult)
                pool.tensor_tensor(part[2], x2, c, ALU.mult)
                link(pool.tensor_tensor(part[3], x1, s, ALU.mult))
                pool.tensor_tensor(x1, part[0], part[1], ALU.subtract)
                link(pool.tensor_tensor(x2, part[2], part[3], ALU.add))
            pool.nop().then_inc(roped, 1)
            pool.wait_ge(lo_ready, N_WOUT + 2)
            for b in range(2):
                rest_of(N_WOUT + 2, b)
            norm("diff")
            norms_between(1, N_FFN2)
            norms_between(2, N_WIN2)
            for n in range(2, len(LEVELS) + 2):
                if n == len(LEVELS):
                    norm("moba_q")
                m = 2 ** (n - 2)
                for t in range(TT if n <= len(LEVELS) else 1):
                    pool.wait_ge(hg_tot, TT * (n - 2) + t + 1)
                    pool.wait_ge(hg_prod, TT * (n - 1) + t + 1)
                    k = proj[:, t, HF:HF + D].rearrange("p (b two m) -> p b two m", two=2, m=m)[:, :, 0, :]
                    tot = tot_of(n - 2, t).rearrange("p (b two) -> p b two", two=2)[:, :, 1:2]
                    pool.tensor_tensor(k, k, tot.to_broadcast([P, D // (2 * m), m]), ALU.mult).then_inc(hg_k, 1)
            norm("moba_k")
            for t in range(TT):
                v = heads(proj[:, t, AK:AK + D], 8)
                ins = pool.tensor_tensor(v, v, per(rstd[:, 42 + 8 * t:50 + 8 * t], P), ALU.mult)
            ins.then_inc(moba_normed, 1)
            pool.wait_ge(hg_o, TT)
            pool.wait_ge(rows_spread, 16)
            for t in range(TT):
                pool.dma_start(heads(proj[:, t, HI:HI + D], 8),
                             bass.AP(tensor=skew_d.tensor, offset=P - 1 + t * P,
                                     ap=[[8 * TOEP - 1, P], [TOEP, 8], [1, P]])).then_inc(bias_in, 16)
            norm("hg")
            norms_between(3, N_FFN3)

        @block.vector
        def _(dve):
            steps = [0]

            def link(ins):
                steps[0] += 1
                ins.then_inc(dve_step, 1)
                dve.wait_ge(dve_step, steps[0])

            def lo(k, r=0):
                dve.wait_ge(hi_ready, k + 1 + 3 * r)
                dve.tensor_tensor(wlo[:, k % RING, :], raw[:, k % RING, :], whi[:, k % RING, :].bitcast(F32),
                                  ALU.subtract).then_inc(lo_ready, 1)

            def fills(u, *which):
                for first in which[::2]:
                    for i in (first, first + 1):
                        f = turn_n(u) + i
                        dve.wait_ge(turn_full, f + 1)
                        if f >= 2:
                            dve.wait_ge(act_lo_ready, f - 1)
                        at = G_TURN + 8 * u + 4 * FILLS[u][i][1]
                        dve.tensor_tensor(heads(tmp[:, f % 2, :], 4), heads(fill_bank(u, i), 4),
                                          per(cols[:, at:at + 4], P), ALU.mult).then_inc(turn_scaled, 1)
                    for i in (first, first + 1):
                        f = turn_n(u) + i
                        dve.wait_ge(act_hi_ready, f + 1)
                        hi, rest = turned_place(u, *FILLS[u][i])
                        dve.tensor_tensor(rest, heads(tmp[:, f % 2, :], 4), hi.bitcast(F32), ALU.subtract)\
                           .then_inc(act_lo_ready, 1)

            def postnorm(m, t):
                dve.wait_ge(rstd_ready, norm_n(f"post{m}", t))
                if t:
                    dve.wait_ge(piece_used, ACC_AFTER[m])
                else:
                    dve.wait_ge(post_in, 16 * (m + 1))
                r = rstd[:, POST + t:POST + t + 1]
                if m != 1:
                    link(dve.tensor_scalar(r, r, 0.5, None, ALU.mult))
                link(dve.scalar_tensor_tensor(out=xs[:, t, :], in0=acc[:, t, :, :].rearrange("p b n -> p (b n)"), scalar=r,
                                              in1=post[:, :], op0=ALU.mult, op1=ALU.mult))
                dve.tensor_tensor(x[:, t, :], x[:, t, :], xs[:, t, :], ALU.add).then_inc(x_ready, 1)

            def residual(j, t):
                if t == 0:
                    dve.wait_ge(acc_first, j + 1)
                else:
                    dve.wait_ge(piece_used, ACC_AFTER[j])
                dve.tensor_tensor(x[:, t, :], x[:, t, :], acc[:, t, :, :].rearrange("p b n -> p (b n)"), ALU.add)\
                   .then_inc(x_ready, 1)

            def norms_between(m, u, n1):
                step = residual if m == 3 else postnorm
                step(m, 0)
                fills(u, 0, 1)
                step(m, 1)
                fills(u, 2, 3)
                dve.wait_ge(lo_ready, n1 + 2)
                lo(n1 + 2)

            def ffn(f, n0):
                h0, h1 = 2 * f * NC, f * (NC + 1)

                def product(c, t):
                    dve.wait_ge(sil_ready, h0 + 2 * c + t + 1)
                    if f or not isinstance(c, int) or c:
                        dve.wait_ge(hT_full, h1 + c)
                    dve.scalar_tensor_tensor(out=hid[:, t, :], in0=gu[:, t, FC:2 * FC], scalar=rstd[:, t:t + 1],
                                             in1=sil[:, t, :], op0=ALU.mult, op1=ALU.mult).then_inc(h_ready, 1)

                def both(c):
                    for t in range(TT):
                        product(c, t)

                def hidden(c):
                    dve.wait_ge(hT_hi_ready, h1 + 1 + c)
                    dve.tensor_tensor(hT_lo[:, :, :], tp[:, 0, :].rearrange("p (a n) -> p a n", a=2),
                                      hT_hi[:, :, :].bitcast(F32), ALU.subtract).then_inc(hT_lo_ready, 1)

                product(0, 0)
                lo(n0 + 3)
                product(0, 1)
                lo(n0 + 4)
                with dve.Fori(1, NC - 1) as c:
                    hidden(c - 1)
                    lo(n0 + 5, c - 1)
                    both(c)
                    lo(n0 + 6, c - 1)
                    lo(n0 + 7, c - 1)
                hidden(NC - 2)
                product(NC - 1, 0)
                lo(n0 + 3 * NC - 1)
                product(NC - 1, 1)
                for t in range(TT):
                    dve.wait_ge(hT_hi_ready, h1 + NC + t)
                    dve.tensor_tensor(last_hT(act_lo, t), heads(tp[:, t, :], 2)[:, :, t * P:(t + 1) * P],
                                      last_hT(act_hi, t).bitcast(F32), ALU.subtract).then_inc(hT_lo_ready, 1)

            def evac(g, used, dst):
                dve.wait_ge(piece_used, used)
                src = block_banks(g)[:, 1, :]
                dve.tensor_scalar(dst, heads(src, 8) if len(dst.shape) == 3 else src, rstd[:, 1:2], None, ALU.mult)\
                   .then_inc(evac_d, 1)

            def block_out(n0, g0, h):
                j = h // 2
                if h % 2 and j % 2:
                    b = j // 2
                    evac(g0 + b, n0 + j + 1, win_place(b, 1) if g0 == 0 else proj[:, 1, b * BLK:(b + 1) * BLK])

            def next_lo(n0, g0, h):
                j = h // 2
                if h % 2:
                    lo(n0 + j + RING)

            def after(n0, g0, h):
                block_out(n0, g0, h)
                next_lo(n0, g0, h)

            def k_out(p):
                dve.wait_ge(qkT_full, p + 1)
                if p // 4 == 1:
                    dve.tensor_copy(k_sb[:, 0, :], turned[:, 1, 0:S]).then_inc(kT_ready, 1)
                elif p < 4:
                    dve.tensor_copy(k_sb[0:AUG, :, :], heads(turned[0:AUG, 1, :], 2)).then_inc(kT_ready, 1)
                else:
                    dve.tensor_scalar(k_sb[:, :, :], heads(turned[:, 1, :], 2), cols[:, G_KG:G_KG + 1], None, ALU.mult)\
                       .then_inc(kT_ready, 1)

            def maxima(p):
                dve.wait_ge(scores_done, p + 1)
                lt, el = heads(late(p), 2), heads(early(p), 2)
                if p >= 8:
                    if p >= 10:
                        dve.wait_ge(exp_done, p - 1)
                    i, dst = p - 8, logits(p)
                    b = [heads(proj[:, t, HI + i * S:HI + (i + 1) * S], 2) for t in range(TT)]
                    for t in range(TT):
                        dve.scalar_tensor_tensor(out=dst[:, :, t * P:(t + 1) * P], in0=lt[:, :, t * P:(t + 1) * P],
                                                 scalar=MOBA_SCALE, in1=b[t], op0=ALU.mult, op1=ALU.add)
                    dve.scalar_tensor_tensor(out=dst[:, :, S:3 * P], in0=el, scalar=MOBA_SCALE, in1=b[1],
                                             op0=ALU.mult, op1=ALU.add).then_inc(logits_ready, 1)
                    dve.wait_ge(logits_ready, i + 1)
                    lt, el = dst[:, :, 0:S], dst[:, :, S:3 * P]
                n = 4 * (p % 2)
                dve.tensor_reduce(mx[:, n:n + 2], lt, AX, ALU.max)
                dve.tensor_reduce(mx[:, n + 2:n + 4], el, AX, ALU.max).then_inc(max_found, 1)
                dve.wait_ge(max_found, p + 1)
                if p >= 2:
                    dve.wait_ge(exp_done, p - 1)
                dve.tensor_scalar(nmx[:, n:n + 4], mx[:, n:n + 4], -1.0, None, ALU.mult).then_inc(nmax_ready, 1)

            def weights_out(p):
                dve.wait_ge(exp_done, p + 1)
                n = 6 * (p % 2)
                dve.reciprocal(rden[:, n:n + 4], den[:, :]).then_inc(rden_ready, 1)
                dve.wait_ge(rden_ready, p + 1)
                if p // 4 == 1:
                    dve.tensor_scalar(rden[:, n + 4:n + 6], rden[:, n + 1:n + 4:2], lam[:, 5:6], None, ALU.mult)\
                       .then_inc(lam_scaled, 1)
                dve.wait_ge(pT_full, p + 1)
                if p:
                    dve.wait_ge(pv_done, p)
                dve.tensor_copy(pT_sb[:, 1, :], turned[:, 1, 0:3 * P]).then_inc(pT_d, 1)

            def output(p):
                kind, i = divmod(p, 4)
                dve.wait_ge(pv_done, p + 1)
                o = [[o_bank(p)[:, (2 * h + t) * P:(2 * h + t + 1) * P] for t in range(TT)] for h in range(2)]
                n = 6 * (p % 2)
                if kind == 1:
                    dve.wait_ge(lam_scaled, i + 1)
                    for t in range(TT):
                        r = n + 4 + (0 if t else 1)
                        ins = dve.tensor_scalar(tmp[:, 0, t * P:(t + 1) * P], o[1][t], rden[:, r:r + 1], None, ALU.mult)
                    ins.then_inc(other_scaled, 1)
                    dve.wait_ge(other_scaled, i + 1)
                for t in range(TT):
                    for h in range(1 if kind == 1 else 2):
                        r = rden[:, n + (0 if t else 2) + h:n + (0 if t else 2) + h + 1]
                        col = (MIX + i * P + 64 * h, MIX + BLK + i * P, AQ + i * S + h * P)[kind]
                        if kind == 1:
                            ins = dve.scalar_tensor_tensor(out=proj[:, t, col:col + P], in0=o[0][t], scalar=r,
                                                           in1=tmp[:, 0, t * P:(t + 1) * P], op0=ALU.mult, op1=ALU.subtract)
                        else:
                            wid = 64 if kind == 0 else P
                            ins = dve.tensor_scalar(proj[:, t, col:col + wid], o[h][t][:, 0:wid], r, None, ALU.mult)
                ins.then_inc(o_out, 1)

            def attention(p0, p1, meanwhile):
                k_out(p0)
                maxima(p0)
                k_out(p0 + 1)
                meanwhile()
                for p in range(p0, p1):
                    weights_out(p)
                    if p + 2 < p1:
                        k_out(p + 2)
                    if p + 1 < p1:
                        maxima(p + 1)
                    output(p)

            def attention_between(p0, n0, g0, h0, also=lambda p: None):
                block_out(n0, g0, h0 - 1)
                k_out(p0)
                put_off = [h0 - 1]
                for p in range(p0, p0 + 4):
                    here = [[h for h in halves(q) if h % 2] for q in laid(p, 2 * h0)]
                    maxima(p)
                    for h in put_off:
                        next_lo(n0, g0, h)
                    if p > p0:
                        also(p - 1)
                    for h in here[0]:
                        block_out(n0, g0, h)
                    put_off = here[0] + here[1]
                    weights_out(p)
                    for h in here[1]:
                        block_out(n0, g0, h)
                    if p < p0 + 3:
                        k_out(p + 1)
                    output(p)
                    if p < p0 + 3 and put_off:
                        next_lo(n0, g0, put_off.pop(0))
                    for h in here[2]:
                        block_out(n0, g0, h)
                        put_off.append(h)
                also(p0 + 3)
                return put_off

            dve.memset(proj[0:8, 0, S:TOEP], MASKED).then_inc(row_padded, 1)
            dve.wait_ge(head_in, 16)
            dve.tensor_copy(id16[:, :], idn)
            dve.tensor_copy(mask16[:, :], cst[:, C_MASK:C_MASK + P])
            fills(T_FFN1, 0, 1)
            lo(0)
            lo(1)
            fills(T_FFN1, 2, 3)
            lo(2)
            dve.wait_ge(tail_in, 16 * 3)
            dve.tensor_copy(level[:, :, :].rearrange("p l n -> p (l n)"), post[:, 0:len(LEVELS) * P])
            dve.wait_ge(act_setup, 1)
            dve.tensor_tensor(fgw_lo[:, :, :], fgw[:, :, :], fgw_hi[:, :, :].bitcast(F32), ALU.subtract).then_inc(dve_setup, 1)
            g = cols[:, G_TURN + 8 * T_WOUT + 4:G_TURN + 8 * T_WOUT + 8]
            link(dve.tensor_scalar(g, g, 1.0 - LAM_INIT, None, ALU.mult))
            ffn(0, N_FFN1)
            lo(N_WIN)
            norms_between(0, T_WIN, N_WIN)
            dve.wait_ge(rstd_ready, norm_n("pre1", 1))
            dve.wait_ge(row_out, 16)
            for h in range(4):
                after(N_WIN, 0, h)
            dve.wait_ge(gate_rows, 1)
            dve.tensor_copy(tmp[0:8, 1, 0:S], tp[0:8, 0, 0:S]).then_inc(gate_copied, 1)
            g0, g1 = cols[:, G_GAM:G_GAM + 8], cols[:, G_GAM + 8:G_GAM + 16]
            link(dve.tensor_tensor(lb[:, 0, :], g0, g1, ALU.max))
            dve.tensor_tensor(lb[:, 1, :], g0, lb[:, 0, :], ALU.subtract)
            dve.tensor_tensor(lb[:, 2, :], g1, lb[:, 0, :], ALU.subtract).then_inc(lb_in, 1)
            for n in range(2):
                q1, k1 = (rows[:, R_LAM + (2 * n + a) * 64:R_LAM + (2 * n + a + 1) * 64] for a in range(2))
                ins = dve.tensor_tensor_reduce(tmp[:, 0, n * 64:(n + 1) * 64], q1, k1, 1.0, 0.0, ALU.mult, ALU.add,
                                               lam[:, n:n + 1])
            ins.then_inc(lam_in, 1)
            dve.wait_ge(gate_product, 1)
            for t in range(TT):
                ins = dve.scalar_tensor_tensor(out=lf[:, 0, t, :], in0=tp[:, 0, 8 * t:8 * t + 8], scalar=rstd[:, t:t + 1],
                                               in1=rows[:, R_FB:R_FB + 8], op0=ALU.mult, op1=ALU.add)
            link(ins)
            dve.scalar_tensor_tensor(out=lf[:, 1, :, :], in0=lf[:, 0, :, :], scalar=-1.0, in1=lf[:, 0, :, :],
                                     op0=ALU.mult, op1=ALU.max).then_inc(gate_abs, 1)
            dve.wait_ge(lb_exp, 1)
            link(dve.tensor_tensor(lb[:, 5, :], lb[:, 3, :], lb[:, 4, :], ALU.add))
            link(dve.reciprocal(lb[:, 0, :], lb[:, 5, :]))
            link(dve.tensor_tensor(lb[:, 6, :], lb[:, 3, :], lb[:, 0, :], ALU.mult))
            dve.tensor_scalar(lb[:, 7, :], lb[:, 6, :], -1.0, 1.0, ALU.mult, ALU.add)
            dve.wait_ge(lam_exp, 1)
            link(dve.tensor_tensor(lam[:, 4:5], lam[:, 2:3], lam[:, 3:4], ALU.subtract))
            dve.tensor_scalar(lam[:, 5:6], lam[:, 4:5], LAM_INIT, None, ALU.add)
            dve.wait_ge(gate_log, 2)
            dve.scalar_tensor_tensor(out=lf[:, 4, :, :], in0=lf[:, 0, :, :], scalar=0.0, in1=lf[:, 3, :, :],
                                     op0=ALU.min, op1=ALU.subtract).then_inc(log_f_ready, 1)
            dve.memset(qd_sb, 0.0).then_inc(padded, 1)
            for h in range(4, 11):
                after(N_WIN, 0, h)
                if h == 9:
                    dve.wait_ge(decay_sum, 1)
                    dve.wait_ge(evac_a, 2)
                    c = tp[:, 1, 0:16].rearrange("p (t h) -> p t h", t=TT)
                    q2, k2 = (proj[:, :, a:a + 8 * AUG].rearrange("p t (h n) -> p t h n", h=8) for a in (FQ, FK))
                    dve.tensor_scalar(q2[:, :, :, 64], c, 8.0, None, ALU.mult)
                    dve.tensor_scalar(k2[:, :, :, 65], c, -1.0, None, ALU.mult)
                    dve.memset(q2[:, :, :, 65], 8.0)
                    dve.memset(k2[:, :, :, 64], 1.0).then_inc(aug_ready, 1)
            attention_between(0, N_WIN, 0, 12)
            dve.wait_ge(roped, 1)
            attention(4, 8, lambda: fills(T_WOUT, 0, 1))
            dve.wait_ge(head_squares, 1)
            dve.tensor_reduce(sums[:, 2:10], xs[:, :, 0:BLK].rearrange("p t (h n) -> p t h n", h=4), AX, ALU.add)\
               .then_inc(head_sums, 1)
            dve.wait_ge(rstd_ready, norm_n("diff"))
            for t in range(TT):
                d = heads(proj[:, t, MIX + BLK:MIX + 2 * BLK], 4)
                dve.tensor_tensor(d, d, per(rstd[:, 2 + 4 * t:6 + 4 * t], P), ALU.mult).then_inc(src_ready, 1)
            fills(T_WOUT, 2, 3)
            dve.wait_ge(lo_ready, N_WOUT + 3)
            lo(N_WOUT + 3)
            lo(N_FFN2)
            norms_between(1, T_FFN2, N_FFN2)
            ffn(1, N_FFN2)
            lo(N_WIN2)
            norms_between(2, T_WIN2, N_WIN2)
            dve.wait_ge(rstd_ready, norm_n("pre3", 1))
            with dve.Fori(0, 2) as i:
                for b in range(3):
                    lo(N_WIN2 + 3 + 2 * b, 2 * i)
                    evac(6 + b, N_WIN2 + 2 + 2 * b + 6 * i, proj[:, 1, bass.ds(b * BLK + i * (3 * BLK), BLK)])
                    lo(N_WIN2 + 4 + 2 * b, 2 * i)
            h = HG_FIRST
            for _ in range(HG_LEAD - 1):
                after(N_WIN2, 6, h)
                h += 1
            for t in range(TT):
                block_out(N_WIN2, 6, h)
                dve.wait_ge(hg_turned, t + 1)
                f = heads(xs[:, t, :], 8)
                link(dve.tensor_tensor(f, heads(acc[:, 0, :, :].rearrange("p b n -> p (b n)"), 8), per(lb[:, 7, :], P),
                                       ALU.mult))
                dve.tensor_tensor(f, f, per(lb[:, 6, :], P), ALU.add).then_inc(hg_f, 1)
                dve.tensor_tensor(heads(proj[:, t, HF:HF + D], 8), heads(acc[:, 1, :, :].rearrange("p b n -> p (b n)"), 8),
                                  per(lb[:, 7, :], P), ALU.mult).then_inc(hg_k, 1)
                next_lo(N_WIN2, 6, h)
                after(N_WIN2, 6, h + 1)
                dve.wait_ge(hg_f, t + 1)
                dve.nop().then_inc(hg_tot, 1)
                h += 2
            after(N_WIN2, 6, h)
            h += 1

            def decay_q(n, t):
                dve.wait_ge(hg_prod, TT * (n - 1) + t + 1)
                q = proj[:, t, HQ:HQ + D]
                if n == 1:
                    dve.wait_ge(hg_q0, TT)
                    dve.tensor_tensor(q, q, xs[:, t, :], ALU.mult).then_inc(hg_q, 1)
                    return
                m = 2 ** (n - 2)
                right = q.rearrange("p (b two m) -> p b two m", two=2, m=m)[:, :, 1, :]
                tot = tot_of(n - 2, t).rearrange("p (b two) -> p b two", two=2)
                dve.wait_ge(hg_q, TT * (n - 2) + t + 1)
                dve.tensor_tensor(right, right, tot[:, :, 0:1].to_broadcast([P, D // (2 * m), m]), ALU.mult)\
                   .then_inc(hg_q, 1)
                if n <= len(LEVELS):
                    nxt = tot_of(n - 1, t).rearrange("p (b o) -> p b o", o=1)
                    dve.tensor_tensor(nxt, tot[:, :, 0:1], tot[:, :, 1:2], ALU.mult).then_inc(hg_tot, 1)
                    dve.wait_ge(hg_tot, TT * (n - 1) + t + 1)

            def diag(n, t):
                dve.wait_ge(hg_prod, TT * n + t + 1)
                src = heads(acc[:, t, :, :].rearrange("p b n -> p (b n)"), 8)
                dst = attnT[:, :, 2 * t, :]
                if n == 0:
                    ins = dve.tensor_tensor(dst, src, idn.rearrange("p (o n) -> p o n", o=1).to_broadcast([P, 8, P]), ALU.mult)
                else:
                    ins = dve.copy_predicated(dst, level[:, n - 1:n, :].to_broadcast([P, 8, P]), src)
                ins.then_inc(hg_copied, 1)

            def square_sums(name, t):
                dve.wait_ge(head_squares, head_n(name, t))
                at = {"moba_q": 26, "moba_k": 42, "hg": 10}[name] + 8 * t
                dve.tensor_reduce(sums[:, at:at + 8], heads(xs[:, t, :], 8), AX, ALU.add).then_inc(head_sums, 1)

            for n in range(len(LEVELS) + 1):
                for t in range(TT):
                    if n < len(LEVELS) or t:
                        decay_q(n + 1, t)
                    diag(n, t)
                    after(N_WIN2, 6, h)
                    if h in MOBA_Q_SQUARES:
                        square_sums("moba_q", MOBA_Q_SQUARES.index(h))
                    h += 1
            for t in range(TT):
                square_sums("moba_k", t)
            after(N_WIN2, 6, h)
            for t in range(TT):
                dve.wait_ge(rstd_ready, norm_n("moba_q", t))
                v = heads(proj[:, t, AQ:AQ + D], 8)
                ins = dve.tensor_tensor(v, v, per(rstd[:, 26 + 8 * t:34 + 8 * t], P), ALU.mult)
                if t:
                    ins.then_inc(moba_normed, 1)
                square_sums("hg", t)
                after(N_WIN2, 6, h + 1 + t)
            for t in range(TT):
                dve.wait_ge(rstd_ready, norm_n("hg", t))
                dve.tensor_tensor(heads(proj[:, t, HQ:HQ + D], 8), heads(acc[:, t, :, :].rearrange("p b n -> p (b n)"), 8),
                                  per(rstd[:, 10 + 8 * t:18 + 8 * t], P), ALU.mult).then_inc(hg_out, 1)
            for h in range(h + 3, MOBA_FIRST - 1):
                after(N_WIN2, 6, h)
            dve.wait_ge(bias_in, 16 * TT)

            def gate_of(p):
                t = p - 8
                if t < TT:
                    dve.wait_ge(hg_gate, t + 1)
                    s = proj[:, t, HG:HG + D]
                    link(dve.tensor_tensor(s, s, proj[:, t, HF:HF + D], ALU.mult))
                    dve.wait_ge(hg_out, TT)
                    o = proj[:, t, HQ:HQ + D]
                    dve.tensor_tensor(o, o, s, ALU.mult).then_inc(src_ready, 1)

            left = attention_between(8, N_WIN2, 6, MOBA_FIRST, gate_of)
            fills(T_WHG, 0, 1)
            for h in left:
                next_lo(N_WIN2, 6, h)
            fills(T_WHG, 2, 3)
            after(N_WIN2, 6, 71)
            lo(N_WHG + 3)

            def merge_hg(b):
                dve.wait_ge(piece_used, N_WHG + 2 + 2 * b)
                dve.wait_ge(merge_gates, TT)
                for t in range(TT):
                    total, gate = (proj[:, t, col + b * BLK:col + (b + 1) * BLK] for col in (HI, G0))
                    dve.tensor_tensor(total, acc[:, t, b, :], gate, ALU.mult).then_inc(merged, 1)

            def merge_at(b):
                dve.wait_ge(piece_used, N_WAT + 2 + 2 * b)
                s = slice(b * BLK, (b + 1) * BLK)
                gate, total = proj[:, :, G1:G1 + D][:, :, s], proj[:, :, HI:HI + D][:, :, s]
                link(dve.tensor_tensor(gate, (gu, tp)[b][:, :, :], gate, ALU.mult))
                dve.wait_ge(merged, TT * (b + 1))
                dve.tensor_tensor(total, total, gate, ALU.add).then_inc(src_ready, 1)

            merge_hg(0)
            lo(N_WAT)
            fills(T_WAT, 0, 1, 2, 3)
            lo(N_WAT + 1)
            lo(N_WAT + 2)
            merge_hg(1)
            lo(N_WAT + 3)
            merge_at(0)
            fills(T_WOUT2, 0, 1)
            lo(N_WOUT2)
            lo(N_WOUT2 + 1)
            merge_at(1)
            fills(T_WOUT2, 2, 3)
            lo(N_WOUT2 + 2)
            lo(N_WOUT2 + 3)
            lo(N_FFN3)
            norms_between(3, T_FFN3, N_FFN3)
            ffn(2, N_FFN3)
            residual(4, 0)
            residual(4, 1)


def kernel(**inputs):
    import concourse.bacc as bacc
    from concourse.bass_utils import run_bass_kernel_spmd

    def of(name, *shape):
        return np.ascontiguousarray(np.asarray(inputs[name]).reshape(shape))

    const, lv, hot_np = constants()
    one = np.ones((P, 8), np.float32)

    def by_feature(name):
        return of(name, KT, P).T

    def of_head(name, times):
        return np.repeat(of(name, P, 1), times, axis=1)

    packed_cols = np.concatenate([
        by_feature("ffn1_pre_g"), by_feature("mix_pre_g"),
        one[:, 0:4], of_head("diff_subln_g", 4),
        by_feature("ffn2_pre_g"), by_feature("attn_norm_g_2"), of_head("hg_out_norm_g_2", 8), one, one,
        by_feature("ffn_norm_g_2"), of("q_norm_g_2", P, 1), of("k_norm_g_2", P, 1),
        of("hg_lb_gamma_2", 2, KT, P).transpose(2, 0, 1).reshape(P, 16)], axis=1)
    packed_rows = np.concatenate([
        of(n, 1, 64) for n in ("diff_lambda_q1", "diff_lambda_k1", "diff_lambda_q2", "diff_lambda_k2")
    ] + [of("fox_forget_b", 1, 8)], axis=1)

    arrays = {"x": of("x", S, D)}
    for f, names in enumerate((("ffn1_w_gate", "ffn1_w_up", "ffn1_w_down"),
                               ("ffn2_w_gate", "ffn2_w_up", "ffn2_w_down"),
                               ("w_ffn_gate_2", "w_ffn_up_2", "w_ffn_down_2"))):
        for what, name in zip(("gate", "up"), names):
            arrays[f"{what}{f}"] = of(name, D, D_FF)
        arrays[f"down{f}"] = of(names[2], D_FF, D)
    arrays["w_in"] = of("w_in", D, 3080)
    arrays["w_out"] = of("w_out", D, D)
    arrays["w_in_2"] = of("w_in_2", D, PROJ)
    for name in ("w_branch_hg_2", "w_branch_attn_2", "w_out_2"):
        arrays[name] = of(name, D, D)
    arrays["fixed"] = np.concatenate([const, packed_cols], axis=1)
    arrays["packed_rows"] = np.ascontiguousarray(packed_rows)
    arrays["post_gains"] = np.concatenate([of(n, 1, D) for n in ("ffn1_post_g", "mix_post_g", "ffn2_post_g")], axis=0)
    arrays["rel_table"] = of("rel_bias_table_2", REL_BUCKETS, 8)
    arrays["level_masks"] = lv.reshape(P, -1)
    arrays["one_hot"] = hot_np

    nc = bacc.Bacc("TRN2", target_bir_lowering=False, num_devices=1)
    d = {n: nc.dram_tensor("in_" + n, a.shape, mybir.dt.from_np(a.dtype), kind="ExternalInput").ap() for n, a in arrays.items()}
    out = nc.dram_tensor("out", (S, D), F32, kind="ExternalOutput").ap()
    skew = nc.dram_tensor("skew", (P * 8 * TOEP,), F32, kind="Internal").ap()
    row = nc.dram_tensor("bias_rows", (8, TOEP), F32, kind="Internal").ap()
    build(nc, d["x"], [d[f"gate{f}"] for f in range(3)], [d[f"up{f}"] for f in range(3)],
          [d[f"down{f}"] for f in range(3)], d["w_in"], d["w_out"], d["w_in_2"], d["w_branch_hg_2"],
          d["w_branch_attn_2"], d["w_out_2"], d["fixed"], d["packed_rows"], d["post_gains"], d["rel_table"],
          d["level_masks"], d["one_hot"], out, row, skew)
    r = run_bass_kernel_spmd(nc, [{"in_" + n: a for n, a in arrays.items()}], core_ids=[0])
    return r.results[0]["out"].reshape(1, S, D)
```
